# Optimizing a Trainium2 kernel written in Bass

```python
import jax, jax.numpy as jnp
from jax import lax
import numpy as np
import math

D_MODEL = 1024
BATCH = 1
SEQ = 512
DEPTH = 1

MEM_LEN = 256
HEAD_DIM = 64
CHUNK = 128
A_GROUPS = 4
A_WIDTH = D_MODEL // 2
A_GROUP_W = A_WIDTH // A_GROUPS
SWA_HEADS = 4
SWA_KV_HEADS = 2
SWA_WIDTH = SWA_HEADS * HEAD_DIM
SWA_KV_WIDTH = SWA_KV_HEADS * HEAD_DIM
WINDOW = 128
MEM_HEADS = 4
MEM_WIDTH = MEM_HEADS * HEAD_DIM
MIX_WIDTH = A_WIDTH + SWA_WIDTH + MEM_WIDTH
IN_WIDTH = 2 * A_WIDTH + SWA_WIDTH + 2 * SWA_KV_WIDTH + MEM_WIDTH + MIX_WIDTH
N_BUCKETS = 32
MAX_DISTANCE = 128
EPS = 1e-6
NEG = -1e30


def rms_norm(x, g):
    xf = x.astype(jnp.float32)
    y = xf * lax.rsqrt(jnp.mean(xf * xf, axis=-1, keepdims=True) + EPS)
    return (y * g.astype(jnp.float32)).astype(x.dtype)

def t5_causal_buckets(dist):
    n = np.maximum(dist, 0)
    max_exact = N_BUCKETS // 2
    large = max_exact + (np.log(np.maximum(n, 1) / max_exact) / np.log(MAX_DISTANCE / max_exact)
                         * (N_BUCKETS - max_exact)).astype(np.int32)
    large = np.minimum(large, N_BUCKETS - 1)
    return np.where(n < max_exact, n, large).astype(np.int32)

def chunked_spatial_gating(u, v, v_g, v_b, w_s, b_s):
    b, s, _ = u.shape
    nc = s // CHUNK
    vg = v.reshape(b, s, A_GROUPS, A_GROUP_W).astype(jnp.float32)
    mu = jnp.mean(vg, axis=-1, keepdims=True)
    var = jnp.mean(jnp.square(vg - mu), axis=-1, keepdims=True)
    vg = (vg - mu) * lax.rsqrt(var + EPS)
    vg = vg * v_g.reshape(A_GROUPS, A_GROUP_W).astype(jnp.float32) + v_b.reshape(A_GROUPS, A_GROUP_W).astype(jnp.float32)
    vc = vg.astype(v.dtype).reshape(b, nc, CHUNK, A_GROUPS, A_GROUP_W)
    causal = jnp.tril(jnp.ones((CHUNK, CHUNK), dtype=w_s.dtype))
    w = w_s * causal[None]
    sv = jnp.einsum('gts,bnsgc->bntgc', w, vc) + b_s.T[None, None, :, :, None]
    return u * sv.reshape(b, s, A_WIDTH)

def sliding_window_attention(q, k, v, sinks, rel_bias):
    b, s, hq, dh = q.shape
    nb = s // CHUNK
    g = hq // SWA_KV_HEADS
    qb = q.reshape(b, nb, CHUNK, SWA_KV_HEADS, g, dh)

    def band(t):
        tb = t.reshape(b, nb, CHUNK, SWA_KV_HEADS, dh)
        prev = jnp.pad(tb, ((0, 0), (1, 0), (0, 0), (0, 0), (0, 0)))[:, :-1]
        return jnp.concatenate([prev, tb], axis=2)

    kb, vb = band(k), band(v)
    logits = jnp.einsum('bnqhgd,bnjhd->bnhgqj', qb, kb).astype(jnp.float32) * (dh ** -0.5)

    qi = np.arange(CHUNK)[:, None]
    kj = np.arange(2 * CHUNK)[None, :]
    dist = qi + CHUNK - kj
    blk = np.arange(nb)[:, None, None]
    valid = (dist >= 0) & (dist < WINDOW) & (blk * CHUNK + kj - CHUNK >= 0)
    buckets = t5_causal_buckets(dist)
    bias = rel_bias.astype(jnp.float32)[buckets]
    bias = jnp.transpose(bias, (2, 0, 1)).reshape(SWA_KV_HEADS, g, CHUNK, 2 * CHUNK)

    logits = jnp.where(valid[None, :, None, None], logits + bias[None, None], NEG)
    sink = sinks.astype(jnp.float32).reshape(1, 1, SWA_KV_HEADS, g, 1, 1)
    m = jnp.maximum(jnp.max(logits, axis=-1, keepdims=True), sink)
    p = jnp.exp(logits - m)
    probs = p / (jnp.sum(p, axis=-1, keepdims=True) + jnp.exp(sink - m))
    out = jnp.einsum('bnhgqj,bnjhd->bnqhgd', probs.astype(v.dtype), vb)
    return out.reshape(b, s, hq * dh)

def memory_cross_attention(q, mem_k, mem_v):
    b, s, h, dh = q.shape
    logits = jnp.einsum('bshd,bmhd->bhsm', q, mem_k).astype(jnp.float32) * (dh ** -0.5)
    probs = jax.nn.softmax(logits, axis=-1)
    out = jnp.einsum('bhsm,bmhd->bshd', probs.astype(mem_v.dtype), mem_v)
    return out.reshape(b, s, h * dh)

def first_inputs(seed: int = 0) -> dict:
    key = jax.random.key(seed)
    ks = jax.random.split(key, 16)
    f32 = jnp.float32
    x = jax.random.normal(ks[0], (BATCH, SEQ, D_MODEL), f32)
    mem = jax.random.normal(ks[1], (BATCH, MEM_LEN, D_MODEL), f32)
    pre_norm_g = 1.0 + 0.05 * jax.random.normal(ks[2], (DEPTH, D_MODEL), f32)
    post_norm_g = 1.0 + 0.05 * jax.random.normal(ks[3], (DEPTH, D_MODEL), f32)
    mem_norm_g = 1.0 + 0.05 * jax.random.normal(ks[4], (DEPTH, D_MODEL), f32)
    w_in = jax.random.normal(ks[5], (DEPTH, D_MODEL, IN_WIDTH), f32) * D_MODEL ** -0.5
    w_mem_kv = jax.random.normal(ks[6], (DEPTH, D_MODEL, 2 * MEM_WIDTH), f32) * D_MODEL ** -0.5
    v_norm_g = 1.0 + 0.05 * jax.random.normal(ks[7], (DEPTH, A_WIDTH), f32)
    v_norm_b = 0.02 * jax.random.normal(ks[8], (DEPTH, A_WIDTH), f32)
    w_spatial = jax.random.normal(ks[9], (DEPTH, A_GROUPS, CHUNK, CHUNK), f32) * CHUNK ** -0.5
    b_spatial = 1.0 + 0.1 * jax.random.normal(ks[10], (DEPTH, A_GROUPS, CHUNK), f32)
    attn_sinks = 0.5 * jax.random.normal(ks[11], (DEPTH, SWA_HEADS), f32)
    rel_bias = 0.5 * jax.random.normal(ks[12], (N_BUCKETS, SWA_HEADS), f32)
    w_out = jax.random.normal(ks[13], (DEPTH, MIX_WIDTH, D_MODEL), f32) * MIX_WIDTH ** -0.5
    return {"x": x, "mem": mem, "pre_norm_g": pre_norm_g, "post_norm_g": post_norm_g,
            "mem_norm_g": mem_norm_g, "w_in": w_in, "w_mem_kv": w_mem_kv,
            "v_norm_g": v_norm_g, "v_norm_b": v_norm_b, "w_spatial": w_spatial,
            "b_spatial": b_spatial, "attn_sinks": attn_sinks, "rel_bias": rel_bias,
            "w_out": w_out}

def first_block(x, mem, pre_norm_g, post_norm_g, mem_norm_g, w_in, w_mem_kv, v_norm_g, v_norm_b,
              w_spatial, b_spatial, attn_sinks, rel_bias, w_out):
    b, s, _ = x.shape
    m_len = mem.shape[1]
    split_at = np.cumsum([A_WIDTH, A_WIDTH, SWA_WIDTH, SWA_KV_WIDTH, SWA_KV_WIDTH, MEM_WIDTH]).tolist()
    for layer in range(DEPTH):
        h = rms_norm(x, pre_norm_g[layer])
        proj = h @ w_in[layer]
        a_u, a_v, sq, sk, sv, mq, z = jnp.split(proj, split_at, axis=-1)

        y_a = chunked_spatial_gating(jax.nn.gelu(a_u), jax.nn.gelu(a_v), v_norm_g[layer],
                                     v_norm_b[layer], w_spatial[layer], b_spatial[layer])

        y_b = sliding_window_attention(sq.reshape(b, s, SWA_HEADS, HEAD_DIM),
                                       sk.reshape(b, s, SWA_KV_HEADS, HEAD_DIM),
                                       sv.reshape(b, s, SWA_KV_HEADS, HEAD_DIM),
                                       attn_sinks[layer], rel_bias)

        mkv = rms_norm(mem, mem_norm_g[layer]) @ w_mem_kv[layer]
        mk, mv = jnp.split(mkv, 2, axis=-1)
        y_c = memory_cross_attention(mq.reshape(b, s, MEM_HEADS, HEAD_DIM),
                                     mk.reshape(b, m_len, MEM_HEADS, HEAD_DIM),
                                     mv.reshape(b, m_len, MEM_HEADS, HEAD_DIM))

        y = jnp.concatenate([y_a, y_b, y_c], axis=-1) * jax.nn.silu(z)
        x = x + rms_norm(y @ w_out[layer], post_norm_g[layer])
    return x


CHUNK_2 = 64
Q_BLOCK = 128
N_HEADS = 16
N_KV_HEADS = 4
ROPE_DIM = HEAD_DIM // 4
ROPE_THETA = 500000.0
IDX_HEADS = 8
IDX_DIM = 64
TOPK_MAX = 256
SSD_D_INNER = 2 * D_MODEL
SSD_HEAD_DIM = 64
SSD_HEADS = SSD_D_INNER // SSD_HEAD_DIM
SSD_GROUPS = 4
SSD_STATE = 128
SSD_CONV = 4
SSD_XBC = SSD_D_INNER + 2 * SSD_GROUPS * SSD_STATE
N_EXPERT_GROUPS = 4
EXPERTS_PER_GROUP = 8
EXPERT_TOPK = 2
EXPERT_HIDDEN = 256
Q_W = N_HEADS * HEAD_DIM
KV_W = N_KV_HEADS * HEAD_DIM
IQ_W = IDX_HEADS * IDX_DIM
SPLITS = (Q_W, KV_W, KV_W, IQ_W, IDX_DIM, IDX_HEADS, SSD_D_INNER, SSD_XBC, SSD_HEADS, D_MODEL, D_MODEL)
IN_PROJ_W = sum(SPLITS)


def rmsnorm(x, g):
    xf = x.astype(jnp.float32)
    y = xf * lax.rsqrt(jnp.mean(xf * xf, axis=-1, keepdims=True) + EPS)
    return (y * g.astype(jnp.float32)).astype(x.dtype)

def rope_partial(x, pos):
    half = ROPE_DIM // 2
    inv = ROPE_THETA ** (-jnp.arange(half, dtype=jnp.float32) * 2.0 / ROPE_DIM)
    ang = pos.astype(jnp.float32)[:, None] * inv[None, :]
    cos = jnp.cos(ang)[:, None, :]
    sin = jnp.sin(ang)[:, None, :]
    xr = x[..., :ROPE_DIM].astype(jnp.float32)
    x1, x2 = xr[..., :half], xr[..., half:]
    rot = jnp.concatenate([x1 * cos - x2 * sin, x2 * cos + x1 * sin], axis=-1)
    return jnp.concatenate([rot.astype(x.dtype), x[..., ROPE_DIM:]], axis=-1)

def dsa_attention(q, k, v, iq, ik, iw):
    Bsz, T = q.shape[0], q.shape[1]
    topk = min(TOPK_MAX, T // 4)
    nblk = T // Q_BLOCK
    grp = N_HEADS // N_KV_HEADS
    key_chunk = jnp.arange(T) // CHUNK_2
    ikf = ik.astype(jnp.float32)

    def to_blocks(a):
        return a.reshape(Bsz, nblk, Q_BLOCK, *a.shape[2:]).swapaxes(0, 1)

    def one_block(args):
        qb, iqb, iwb, start = args
        q_chunk = (start + jnp.arange(Q_BLOCK)) // CHUNK_2
        admissible = key_chunk[None, :] <= q_chunk[:, None]
        rel = jax.nn.relu(jnp.einsum('bqhd,bsd->bqhs', iqb.astype(jnp.float32), ikf) * IDX_DIM ** -0.5)
        score = jnp.einsum('bqhs,bqh->bqs', rel, iwb.astype(jnp.float32) * IDX_HEADS ** -0.5)
        score = jnp.where(admissible[None], score, -jnp.inf)
        top_s, sel = lax.top_k(score, topk)
        valid = jnp.isfinite(top_s)
        k_sel = jax.vmap(lambda kk, ii: kk[ii])(k, sel)
        v_sel = jax.vmap(lambda vv, ii: vv[ii])(v, sel)
        qg = qb.reshape(Bsz, Q_BLOCK, N_KV_HEADS, grp, HEAD_DIM).astype(jnp.float32)
        logits = jnp.einsum('bqhgd,bqkhd->bqhgk', qg, k_sel.astype(jnp.float32)) * HEAD_DIM ** -0.5
        logits = jnp.where(valid[:, :, None, None, :], logits, -jnp.inf)
        p = jax.nn.softmax(logits, axis=-1)
        o = jnp.einsum('bqhgk,bqkhd->bqhgd', p, v_sel.astype(jnp.float32))
        return o.reshape(Bsz, Q_BLOCK, N_HEADS * HEAD_DIM).astype(q.dtype)

    starts = jnp.arange(nblk, dtype=jnp.int32) * Q_BLOCK
    out = lax.map(one_block, (to_blocks(q), to_blocks(iq), to_blocks(iw), starts))
    return out.swapaxes(0, 1).reshape(Bsz, T, N_HEADS * HEAD_DIM)

def causal_depthwise_conv(x, w, b):
    y = lax.conv_general_dilated(x, w[:, None, :], window_strides=(1,),
                                 padding=[(w.shape[0] - 1, 0)],
                                 dimension_numbers=('NWC', 'WIO', 'NWC'),
                                 feature_group_count=x.shape[-1])
    return y + b

def ssd_chunked(xh, dt, A, Bm, Cm):
    Bsz, T, H, P = xh.shape
    nc = T // CHUNK_2
    R = H // SSD_GROUPS
    x = (xh * dt[..., None]).reshape(Bsz, nc, CHUNK_2, SSD_GROUPS, R, P)
    a_cs = jnp.cumsum((dt * A).reshape(Bsz, nc, CHUNK_2, SSD_GROUPS, R), axis=2)
    Bc = Bm.reshape(Bsz, nc, CHUNK_2, SSD_GROUPS, SSD_STATE)
    Cc = Cm.reshape(Bsz, nc, CHUNK_2, SSD_GROUPS, SSD_STATE)
    seg = a_cs[:, :, :, None] - a_cs[:, :, None, :]
    causal = jnp.tril(jnp.ones((CHUNK_2, CHUNK_2), dtype=bool))[None, None, :, :, None, None]
    decay = jnp.exp(jnp.where(causal, seg, -jnp.inf))
    cb = jnp.einsum('bclgn,bcsgn->bclsg', Cc, Bc)
    y_diag = jnp.einsum('bclsg,bclsgr,bcsgrp->bclgrp', cb, decay, x)
    decay_to_end = jnp.exp(a_cs[:, :, -1:] - a_cs)
    states = jnp.einsum('bclgn,bclgr,bclgrp->bcgrpn', Bc, decay_to_end, x)
    chunk_decay = jnp.exp(a_cs[:, :, -1])

    def step(h, inp):
        dec, st = inp
        return dec[..., None, None] * h + st, h

    h0 = jnp.zeros((Bsz, SSD_GROUPS, R, P, SSD_STATE), jnp.float32)
    _, prev = lax.scan(step, h0, (chunk_decay.swapaxes(0, 1), states.swapaxes(0, 1)))
    prev = prev.swapaxes(0, 1)
    y_off = jnp.einsum('bclgn,bcgrpn,bclgr->bclgrp', Cc, prev, jnp.exp(a_cs))
    return (y_diag + y_off).reshape(Bsz, T, H, P)

def gated_group_rmsnorm(y, z, g):
    yf = y.astype(jnp.float32) * jax.nn.silu(z.astype(jnp.float32))
    yg = yf.reshape(*yf.shape[:-1], SSD_GROUPS, -1)
    yg = yg * lax.rsqrt(jnp.mean(yg * yg, axis=-1, keepdims=True) + EPS)
    return yg.reshape(yf.shape) * g.astype(jnp.float32)

def hier_moe(h, w_rg, b_rg, w_re, b_re, w_gate, w_up, w_down):
    Bsz, T, D = h.shape
    hf = h.reshape(-1, D)
    g_logits = (hf @ w_rg + b_rg).astype(jnp.float32)
    g_prob = jax.nn.softmax(g_logits, axis=-1)
    g_idx = jnp.argmax(g_logits, axis=-1)
    g_w = jnp.take_along_axis(g_prob, g_idx[:, None], axis=-1)
    e_logits = (hf @ w_re + b_re).astype(jnp.float32).reshape(-1, N_EXPERT_GROUPS, EXPERTS_PER_GROUP)
    e_in = jnp.take_along_axis(e_logits, g_idx[:, None, None], axis=1)[:, 0]
    top_v, top_i = lax.top_k(e_in, EXPERT_TOPK)
    top_p = jax.nn.softmax(top_v, axis=-1)
    within = jnp.sum(jax.nn.one_hot(top_i, EXPERTS_PER_GROUP, dtype=jnp.float32) * top_p[..., None], axis=1)
    combine = jax.nn.one_hot(g_idx, N_EXPERT_GROUPS, dtype=jnp.float32)[:, :, None] * (g_w * within)[:, None, :]
    combine = combine.astype(hf.dtype)
    out = jnp.zeros_like(hf)
    for g in range(N_EXPERT_GROUPS):
        a = jnp.einsum('nd,edf->nef', hf, w_gate[g])
        u = jnp.einsum('nd,edf->nef', hf, w_up[g])
        act = jax.nn.silu(a) * u * combine[:, g, :, None]
        out = out + jnp.einsum('nef,efd->nd', act, w_down[g])
    return out.reshape(Bsz, T, D)

def second_inputs(seed: int = 0) -> dict:
    key = jax.random.key(seed)
    ks = jax.random.split(key, 24)
    L = DEPTH
    f32 = jnp.float32

    def nrm(k, shape, scale):
        return jax.random.normal(k, shape, f32) * scale

    def gain(k, n):
        return 1.0 + 0.02 * jax.random.normal(k, (L, n), f32)

    dt0 = jnp.exp(jax.random.uniform(ks[8], (L, SSD_HEADS), f32, math.log(1e-3), math.log(1e-1)))
    return {
        "x": nrm(ks[0], (BATCH, SEQ, D_MODEL), 1.0),
        "attn_norm": gain(ks[1], D_MODEL),
        "w_in": nrm(ks[2], (L, D_MODEL, IN_PROJ_W), D_MODEL ** -0.5),
        "q_norm": gain(ks[3], HEAD_DIM),
        "k_norm": gain(ks[4], HEAD_DIM),
        "idx_k_norm": gain(ks[5], IDX_DIM),
        "conv_w": nrm(ks[6], (L, SSD_CONV, SSD_XBC), SSD_CONV ** -0.5),
        "conv_b": nrm(ks[7], (L, SSD_XBC), 0.02),
        "dt_bias": dt0 + jnp.log(-jnp.expm1(-dt0)),
        "a_log": jnp.log(jax.random.uniform(ks[9], (L, SSD_HEADS), f32, 1.0, 16.0)),
        "d_skip": 1.0 + 0.1 * jax.random.normal(ks[10], (L, SSD_HEADS), f32),
        "ssd_norm": gain(ks[11], SSD_D_INNER),
        "w_attn_branch": nrm(ks[12], (L, Q_W, D_MODEL), Q_W ** -0.5),
        "w_ssd_branch": nrm(ks[13], (L, SSD_D_INNER, D_MODEL), SSD_D_INNER ** -0.5),
        "w_out": nrm(ks[14], (L, D_MODEL, D_MODEL), D_MODEL ** -0.5),
        "ffn_norm": gain(ks[15], D_MODEL),
        "w_route_group": nrm(ks[16], (L, D_MODEL, N_EXPERT_GROUPS), D_MODEL ** -0.5),
        "b_route_group": nrm(ks[17], (L, N_EXPERT_GROUPS), 0.01),
        "w_route_expert": nrm(ks[18], (L, D_MODEL, N_EXPERT_GROUPS * EXPERTS_PER_GROUP), D_MODEL ** -0.5),
        "b_route_expert": nrm(ks[19], (L, N_EXPERT_GROUPS * EXPERTS_PER_GROUP), 0.01),
        "w_gate": nrm(ks[20], (L, N_EXPERT_GROUPS, EXPERTS_PER_GROUP, D_MODEL, EXPERT_HIDDEN), D_MODEL ** -0.5),
        "w_up": nrm(ks[21], (L, N_EXPERT_GROUPS, EXPERTS_PER_GROUP, D_MODEL, EXPERT_HIDDEN), D_MODEL ** -0.5),
        "w_down": nrm(ks[22], (L, N_EXPERT_GROUPS, EXPERTS_PER_GROUP, EXPERT_HIDDEN, D_MODEL), EXPERT_HIDDEN ** -0.5),
    }

def second_block(x, attn_norm, w_in, q_norm, k_norm, idx_k_norm, conv_w, conv_b, dt_bias, a_log, d_skip,
              ssd_norm, w_attn_branch, w_ssd_branch, w_out, ffn_norm, w_route_group, b_route_group,
              w_route_expert, b_route_expert, w_gate, w_up, w_down):
    Bsz, T, _ = x.shape
    pos = jnp.arange(T)
    offs = np.cumsum(SPLITS)[:-1].tolist()
    for l in range(DEPTH):
        h = rmsnorm(x, attn_norm[l])
        proj = h @ w_in[l]
        (q, k, v, iq, ik, iw, z, xbc, dt_raw, gate_a, gate_b) = jnp.split(proj, offs, axis=-1)
        q = rope_partial(rmsnorm(q.reshape(Bsz, T, N_HEADS, HEAD_DIM), q_norm[l]), pos)
        k = rope_partial(rmsnorm(k.reshape(Bsz, T, N_KV_HEADS, HEAD_DIM), k_norm[l]), pos)
        v = v.reshape(Bsz, T, N_KV_HEADS, HEAD_DIM)
        iq = rope_partial(iq.reshape(Bsz, T, IDX_HEADS, IDX_DIM), pos)
        ik = rope_partial(rmsnorm(ik, idx_k_norm[l])[:, :, None, :], pos)[:, :, 0, :]
        y_attn = dsa_attention(q, k, v, iq, ik, iw)
        xbc = jax.nn.silu(causal_depthwise_conv(xbc, conv_w[l], conv_b[l]))
        xs, bs, cs = jnp.split(xbc, [SSD_D_INNER, SSD_D_INNER + SSD_GROUPS * SSD_STATE], axis=-1)
        xh = xs.reshape(Bsz, T, SSD_HEADS, SSD_HEAD_DIM).astype(jnp.float32)
        dt = jax.nn.softplus(dt_raw.astype(jnp.float32) + dt_bias[l].astype(jnp.float32))
        A = -jnp.exp(a_log[l].astype(jnp.float32))
        y_ssd = ssd_chunked(xh, dt, A,
                            bs.reshape(Bsz, T, SSD_GROUPS, SSD_STATE).astype(jnp.float32),
                            cs.reshape(Bsz, T, SSD_GROUPS, SSD_STATE).astype(jnp.float32))
        y_ssd = y_ssd + d_skip[l].astype(jnp.float32)[:, None] * xh
        y_ssd = gated_group_rmsnorm(y_ssd.reshape(Bsz, T, SSD_D_INNER), z, ssd_norm[l]).astype(x.dtype)
        merged = jax.nn.sigmoid(gate_a) * (y_attn @ w_attn_branch[l]) + jax.nn.sigmoid(gate_b) * (y_ssd @ w_ssd_branch[l])
        x = x + merged @ w_out[l]
        x = x + hier_moe(rmsnorm(x, ffn_norm[l]), w_route_group[l], b_route_group[l], w_route_expert[l],
                         b_route_expert[l], w_gate[l], w_up[l], w_down[l])
    return x


def setup_inputs(seed=0):
    out = dict(first_inputs(seed))
    for name, value in second_inputs(seed + 1).items():
        if name != "x":
            out[name + "_2"] = value
    return out


def reference(
    x, mem, pre_norm_g, post_norm_g, mem_norm_g, w_in, w_mem_kv, v_norm_g, v_norm_b, w_spatial,
    b_spatial, attn_sinks, rel_bias, w_out, attn_norm_2, w_in_2, q_norm_2, k_norm_2,
    idx_k_norm_2, conv_w_2, conv_b_2, dt_bias_2, a_log_2, d_skip_2, ssd_norm_2, w_attn_branch_2,
    w_ssd_branch_2, w_out_2, ffn_norm_2, w_route_group_2, b_route_group_2, w_route_expert_2,
    b_route_expert_2, w_gate_2, w_up_2, w_down_2,
):
    x = first_block(
        x, mem, pre_norm_g, post_norm_g, mem_norm_g, w_in, w_mem_kv, v_norm_g, v_norm_b,
        w_spatial, b_spatial, attn_sinks, rel_bias, w_out,
    )
    return second_block(
        x, attn_norm_2, w_in_2, q_norm_2, k_norm_2, idx_k_norm_2, conv_w_2, conv_b_2, dt_bias_2,
        a_log_2, d_skip_2, ssd_norm_2, w_attn_branch_2, w_ssd_branch_2, w_out_2, ffn_norm_2,
        w_route_group_2, b_route_group_2, w_route_expert_2, b_route_expert_2, w_gate_2, w_up_2,
        w_down_2,
    )


_drawn_inputs = setup_inputs


def setup_inputs(seed=0):
    import zlib

    import numpy as np

    out = dict(_drawn_inputs(seed))
    spreads = {}
    factors = {'mem_norm_g': 4.134,
     'v_norm_b': 4.674,
     'attn_sinks': 4.891,
     'attn_norm_2': 2.69,
     'q_norm_2': 8.0,
     'k_norm_2': 7.108,
     'idx_k_norm_2': 5.445,
     'conv_b_2': 2.752,
     'ssd_norm_2': 3.827,
     'ffn_norm_2': 2.819,
     'b_route_group_2': 4.547,
     'b_route_expert_2': 5.974,
     'd_skip_2': 2.997}
    for name, (base, spread) in spreads.items():
        noise = np.random.default_rng([zlib.crc32(name.encode()), seed]).standard_normal(out[name].shape)
        drawn = base * np.exp(spread * noise) if base else spread * noise
        out[name] = __import__('jax').numpy.asarray(drawn.astype(out[name].dtype))
    for name, factor in factors.items():
        out[name] = (out[name] * factor).astype(out[name].dtype)
    return out
```

```python
from contextlib import ExitStack, contextmanager

import numpy as np

import concourse.bass as bass
from concourse import mybir

F32 = mybir.dt.float32
F32R = mybir.dt.float32r
ALU = mybir.AluOpType
ACT = mybir.ActivationFunctionType
AX = mybir.AxisListType

P = 128
S = 512
D = 1024
TT = S // P
KC = D // P
HALF = KC // 2
EPS = 1e-6
NEG = -1e30
MEM = 256
HD = 64

A_U, A_V, SQKV, MQ, Z1 = 0, 512, 1024, 1536, 1792
Q2, KV2, IQ2, IK2, Z2, XBC2, DT2, GA2, GB2 = 0, 1024, 1536, 2048, 2120, 4168, 7240, 7272, 8296
SMALL = 104
TOPK = 128
ARENA = 118
N_EXP = 32
HID = 256

ROWS_A = {"pre": 0, "mem": 8, "attn": 16, "ffn": 24, "ssd": 32, "conv_b": 48}
N_ROWS_A, N_ROWS_B = 72, 96


class Turns:

    def __init__(self, eng, full, free):
        self.eng, self.full, self.free = eng, full, free
        self.k, self.off, self.half = 0, 0, 0

    def take(self):
        s = self.k % 2
        if self.k >= 2:
            self.eng.wait_ge(self.free[s], self.half + self.k // 2)
        self.k += 1
        return s

    def see(self):
        s = self.k % 2
        self.k += 1
        self.eng.wait_ge(self.full, self.off + self.k)
        return s

    def skip(self, n=1):
        self.k += n

    @contextmanager
    def loop(self, count, per):
        first = self.k
        with self.eng.Fori(0, count) as i:
            self.off, self.half = i * per, i * (per // 2)
            yield i
        assert self.k == first + per and per % 2 == 0
        self.off = self.half = 0
        self.k = first + per * count


def consts():
    k = np.arange(P)
    c = {"c_ident": np.eye(P), "c_tri": (k[:, None] <= k[None, :]), "c_flip": np.eye(P)[::-1]}
    dist = 255 - np.arange(384)
    ok = (dist >= 0) & (dist < 128)
    n = np.maximum(dist, 0)
    large = 16 + (np.log(np.maximum(n, 1) / 16) / np.log(128 / 16) * 16).astype(np.int32)
    bucket = np.where(n < 16, n, np.minimum(large, 31))
    c["c_bucket"] = (bucket[None, :] == np.arange(32)[:, None]) & ok[None, :]
    c["c_outside"] = np.broadcast_to(np.where(ok, 0.0, NEG), (4, 384))
    inv = np.float32(500000.0) ** (-np.arange(8, dtype=np.float32) * np.float32(2.0) / np.float32(16))
    ang = (np.arange(S, dtype=np.float32)[:, None] * inv[None, :].astype(np.float32)).astype(np.float32)
    c["c_cos"] = np.cos(ang)
    c["c_sin"] = np.sin(ang)
    c["c_order"] = np.broadcast_to(np.arange(8, 0, -1), (P, 8))
    return {n: np.ascontiguousarray(a, dtype=np.float32) for n, a in c.items()}


def bc(ap, axis, n):
    a = ap.unsqueeze(axis)
    shape = list(a.shape)
    shape[axis] = n
    return a.broadcast_to(shape)



def matmul3(pe, out, x, w, first, last):
    pe.matmul(out, x[0], w[0], start=first, stop=False)
    pe.matmul(out, x[1], w[0], start=False, stop=False)
    return pe.matmul(out, x[0], w[1], start=False, stop=last)


def program(nc, d, out):
    w1, w2 = d["w_in"][0], d["w_in_2"][0]
    x1_dram = nc.dram_tensor("x1_scratch", [S, D], F32, kind="Internal").ap()
    bias_dram = nc.dram_tensor("bias_scratch", [4, 384], F32, kind="Internal").ap()
    e_gate, e_up, e_down = (d[n][0].rearrange("g e k n -> (g e) k n") for n in ("w_gate_2", "w_up_2", "w_down_2"))

    with ExitStack() as ctx:
        def sb(name, shape, dt=F32):
            return ctx.enter_context(nc.sbuf_tensor(name, shape, dt))

        def sem(name):
            return ctx.enter_context(nc.semaphore(name))

        hi = sb("hi", [P, KC, S], F32R)
        lo = sb("lo", [P, KC, S], F32R)
        stage = sb("stage", [P, 2, HALF, 512])
        w_hi = sb("w_hi", [P, 2, HALF, 512], F32R)
        w_lo = sb("w_lo", [P, 2, HALF, 512], F32R)
        ident, tri, flip, ones = (sb(n, [P, P]) for n in ("ident", "tri", "flip", "ones"))
        rows_a, rows_b = sb("rows_a", [N_ROWS_A, P]), sb("rows_b", [N_ROWS_B, P])
        cols = sb("cols", [P, N_ROWS_A + N_ROWS_B])
        cos, sin = sb("cos", [P, TT, 8]), sb("sin", [P, TT, 8])
        unit = sb("unit", [P, 1])
        order = sb("order", [P, 8])
        sinks = sb("sinks", [P, 4])
        q_g, k_g, ik_g = sb("q_g", [P, HD]), sb("k_g", [P, HD]), sb("ik_g", [P, HD])
        dt_b, a_log, d_skip = sb("dt_b", [P, 32]), sb("a_log", [P, 32]), sb("d_skip", [P, 32])
        b_rt = sb("b_rt", [P, 36])
        w_rt = sb("w_rt", [P, KC, 36])
        st = sb("st", [P, 10, 64])
        top = sb("top", [P, 2, 8])
        sm = sb("sm", [P, 6, 4, 4])
        ps = [ctx.enter_context(nc.psum_tensor(f"ps{i}", [P, 4, 512], F32)) for i in range(2)]

        base = -(-nc.sbuf_base // 64) * 64
        assert base + ARENA * 1024 <= nc.sbuf_top

        def at(name, kib, shape, dt=F32):
            size = int(np.prod(shape[1:])) * 4
            assert kib * 1024 + size <= ARENA * 1024, name
            return nc.alloc_sbuf_tensor_at(name, shape, dt, offset=base + int(kib * 1024))

        xres = at("xres", 0, [P, TT, D])
        xn = at("xn", 16, [P, TT, D])
        pr1, pT1 = at("pr1", 16, [P, 2, 4, 256]), at("pT1", 24, [P, 4, 256])
        vtmp = at("vtmp", 16, [P, TT, 512])
        yT = at("yT", 32, [P, KC, S])
        relb, bucket = at("relb", 32, [32, 4]), at("bucket", 33, [32, 384])
        outside, brow = at("outside", 35, [4, 384]), at("brow", 37, [4, 384])
        uT, vt = at("uT", 48, [P, 4, S]), at("vt", 56, [P, TT, 512])
        zT = at("zT", 64, [P, KC, S])
        memb = at("memb", 64, [P, 2, D])
        qT1, mqT = at("qT1", 80, [P, 2, S]), at("mqT", 84, [P, 2, S])
        kT1, sv1 = at("kT1", 88, [P, S]), at("sv1", 90, [P, TT, P])
        mkT, mv = at("mkT", 92, [P, 2, MEM]), at("mv", 94, [P, 2, MEM])
        v_g, v_b, b_s = at("v_g", 96, [P, 512]), at("v_b", 98, [P, 512]), at("b_s", 100, [P, 4, P])
        post_g = at("post_g", 102, [P, D])
        wsp, wspT = at("wsp", 106, [P, 4, P]), at("wspT", 108, [P, 4, P])
        bias, bias_r = at("bias", 106, [P, 4, 256]), at("bias_r", 110, [P, 4, 256])
        yt1 = at("yt1", 114, [P, 2, 256])
        junk1 = at("junk1", 116, [P, 512])
        sg = at("sg", 0, [P, KC, S])
        qt = at("qt", 16, [P, TT, 1024])
        yah = at("yah", 16, [P, KC, S], F32R)
        iqt, iqT = at("iqt", 32, [P, TT, 512]), at("iqT", 40, [P, 4, S])
        yal = at("yal", 32, [P, KC, S], F32R)
        kvt, kT2 = at("kvt", 48, [P, TT, 512]), at("kT2", 56, [P, 2, S])
        qT2, sel = at("qT2", 60, [P, 8, S]), at("sel", 76, [P, TT, S])
        yt2, rot = at("yt2", 84, [P, 2, 256]), at("rot", 86, [P, 2, TT, 128])
        ikt = at("ikt", 90, [P, TT, P])
        pT2, pr2 = at("pT2", 92, [P, 4, 512]), at("pr2", 100, [P, 2, 4, 512])
        dtt = at("dtt", 0, [P, 8, TT, 32])
        sqr, rel = at("sqr", 92, [P, 2, 1024]), at("rel", 100, [P, 4, 512])
        score, ikT = at("score", 108, [P, 3, 512]), at("ikT", 114, [P, S])
        smt = at("smt", 116, [P, TT, SMALL])
        mT = at("mT", 100, [P, KC, S])
        xd, xe = at("xd", 0, [P, 32, HD]), at("xe", 8, [P, 32, HD])
        yoff = at("yoff", 0, [P, 32, HD])
        xtok = at("xtok", 16, [P, TT, 2048])
        bT, cT, btok = at("bT", 48, [P, 4, S]), at("cT", 56, [P, 4, S]), at("btok", 64, [P, TT, 512])
        cpad, xsT = at("cpad", 72, [P, 4, 3 + S]), at("xsT", 80.125, [P, 4, S])
        decay = at("decay", 72, [P, 32, P])
        state = at("state", 88.25, [P, 2048])
        cb = at("cb", 96.25, [P, 4, P])
        dts = at("dts", 98.25, [P, 3, TT, 32])
        sgb, sz = at("sgb", 48, [P, KC, S]), at("sz", 64, [P, TT, 512])
        junk3 = at("junk3", 72, [P, 1024])
        ssm = st
        comb = at("comb", 32, [P, TT, N_EXP])
        cw = at("cw", 33, [P, 2, TT])
        rt = at("rt", 34, [P, 16, TT, 36])
        sa, act = at("sa", 44, [P, 2, S]), at("act", 48, [P, 2, S])
        act_hi = [at(f"act_hi{i}", 52 + 8 * i, [P, 2, S], F32R) for i in range(2)]
        act_lo = [at(f"act_lo{i}", 56 + 8 * i, [P, 2, S], F32R) for i in range(2)]
        comb_e = at("comb_e", 70, [P, N_EXP, TT])

        def gain(name, k):
            return cols[:, ROWS_A[name] + k:ROWS_A[name] + k + 1]

        x_in, mem_in, par_in = sem("x_in"), sem("mem_in"), sem("par_in")
        w_in_sem = [sem("w_even_in"), sem("w_odd_in")]
        w_split = sem("w_split")
        w_used = sem("w_used")
        turn_full = sem("turn_full")
        turn_free = [sem("turn_free0"), sem("turn_free1")]
        cols_ready, setup_done = sem("cols_ready"), sem("setup_done")
        ss_ready, rms_ready, rows_ready = sem("ss_ready"), sem("rms_ready"), sem("rows_ready")
        hi_ready, lo_ready = sem("hi_ready"), sem("lo_ready")
        brow_ready, bias_out, bias_in = sem("brow_ready"), sem("bias_out"), sem("bias_in")
        wspT_ready, u_ready, v_ready, v_normed = sem("wspT_ready"), sem("u_ready"), sem("v_ready"), sem("v_normed")
        qkv1_ready, mkv_ready, z1_ready = sem("qkv1_ready"), sem("mkv_ready"), sem("z1_ready")
        max_ready, exp_ready, sink_ready = sem("max_ready"), sem("exp_ready"), sem("sink_ready")
        pT_ready, yt_ready, yT_ready = sem("pT_ready"), sem("yt_ready"), sem("yT_ready")
        wo_ready, x1_ready, x1_saved, x1_back = sem("wo_ready"), sem("x1_ready"), sem("x1_saved"), sem("x1_back")
        iq_ready, small_ready, kv_ready, q_ready = sem("iq_ready"), sem("small_ready"), sem("kv_ready"), sem("q_ready")
        iq_rows, k_rows, q_rows = sem("iq_rows"), sem("k_rows"), sem("q_rows")
        iqT_ready, kT_ready, qT_ready, rel_ready = sem("iqT_ready"), sem("kT_ready"), sem("qT_ready"), sem("rel_ready")
        sq_ready, rel_used, sel_ready, sga_ready = sem("sq_ready"), sem("rel_used"), sem("sel_ready"), sem("sga_ready")
        conv_in, conv_out, xs_ready, xtok_ready = sem("conv_in"), sem("conv_out"), sem("xs_ready"), sem("xtok_ready")
        dt_step, dt_act = sem("dt_step"), sem("dt_act")
        acs_ready, e_ready, m_ready = sem("acs_ready"), sem("e_ready"), sem("m_ready")
        xd_ready, xe_ready, st_ready = sem("xd_ready"), sem("xe_ready"), sem("st_ready")
        sgb_ready, sz_ready, gated, y_rows = sem("sgb_ready"), sem("sz_ready"), sem("gated"), sem("y_rows")
        rt_step, rt_act = sem("rt_step"), sem("rt_act")
        sa_ready, act_ready, acth_ready, actl_ready = sem("sa_ready"), sem("act_ready"), sem("acth_ready"), sem("actl_ready")
        x2_ready, out_done = sem("x2_ready"), sem("out_done")
        mT_ready = sem("mT_ready")
        yal_ready = sem("yal_ready")

        JOBS = 36
        TILES = 2 * JOBS + 3 * N_EXP
        PARAMS = 0

        block = ctx.enter_context(nc.Block())

        params = [
            (ident[:], d["c_ident"]), (tri[:], d["c_tri"]), (flip[:], d["c_flip"]), (bucket[:], d["c_bucket"]), (outside[:], d["c_outside"]),
            (cos[:], d["c_cos"].rearrange("(t p) f -> p t f", p=P)), (sin[:], d["c_sin"].rearrange("(t p) f -> p t f", p=P)),
            (order[:], d["c_order"]), (relb[:], d["rel_bias"]),
            (rows_b[:], d["conv_w_2"][0].rearrange("k (c p) -> (k c) p", p=P)),
            (wsp[:], d["w_spatial"][0].rearrange("g t s -> t g s")),
            (w_rt[:, :, 0:4], d["w_route_group_2"][0].rearrange("(k p) n -> p k n", p=P)),
            (w_rt[:, :, 4:36], d["w_route_expert_2"][0].rearrange("(k p) n -> p k n", p=P)),
        ]
        for name, key in (("pre", "pre_norm_g"), ("mem", "mem_norm_g"), ("attn", "attn_norm_2"), ("ffn", "ffn_norm_2"),
                          ("ssd", "ssd_norm_2"), ("conv_b", "conv_b_2")):
            v = d[key][0].rearrange("(c p) -> c p", p=P)
            params.append((rows_a[ROWS_A[name]:ROWS_A[name] + v.shape[0], :], v))
        for dst, v in ((v_g[:], d["v_norm_g"][0]), (v_b[:], d["v_norm_b"][0]), (post_g[:], d["post_norm_g"][0]),
                       (b_s[:], d["b_spatial"][0].rearrange("g t -> (g t)")),
                       (sinks[:], d["attn_sinks"][0]), (q_g[:], d["q_norm_2"][0]), (k_g[:], d["k_norm_2"][0]),
                       (ik_g[:], d["idx_k_norm_2"][0]), (dt_b[:], d["dt_bias_2"][0]), (a_log[:], d["a_log_2"][0]),
                       (d_skip[:], d["d_skip_2"][0]), (b_rt[:, 0:4], d["b_route_group_2"][0]),
                       (b_rt[:, 4:36], d["b_route_expert_2"][0])):
            src = v.partition_broadcast(P)
            if len(dst.shape) == 3:
                dst = dst.rearrange("p g t -> p (g t)")
            params.append((dst, src))
        PARAMS = 16 * len(params)

        @block.sync
        def _(sp):
            tiles = [0]

            def tile(parts):
                n = tiles[0]
                if n >= 2:
                    sp.wait_ge(w_split, n - 1)
                for dst, src in parts(stage[:, n % 2]):
                    sp.dma_start(dst, src).then_inc(w_in_sem[n % 2], 16)
                tiles[0] += 1

            def halves(w, r0, c0, ncols=512):
                for h in range(2):
                    src = w[r0 + 512 * h:r0 + 512 * (h + 1), c0:c0 + ncols].rearrange("(k p) n -> p k n", p=P)
                    tile(lambda t, src=src: [(t[:, a:a + 2, 0:ncols], src[:, a:a + 2, :]) for a in (0, 2)])

            sp.dma_start(memb[:], d["mem"][0].rearrange("(t p) n -> p t n", p=P)).then_inc(mem_in, 16)
            halves(d["w_mem_kv"][0], 0, 0)
            sp.dma_start(xres[:], d["x"][0].rearrange("(t p) n -> p t n", p=P)).then_inc(x_in, 16)
            for c0, n in ((SQKV, 512), (A_V, 512), (A_U, 512), (MQ, 256), (Z1, 512), (Z1 + 512, 512)):
                halves(w1, 0, c0, n)
            sp.wait_ge(brow_ready, 1)
            sp.dma_start(bias_dram, brow[:]).then_inc(bias_out, 16)
            sp.wait_ge(bias_out, 16)
            for h in range(4):
                shifted = bass.AP(bias_dram.tensor, h * 384, [[1, P], [1, 256]])
                sp.dma_start(bias_r[:, h, :], shifted).then_inc(bias_in, 16)
            for c in range(2):
                halves(d["w_out"][0], 0, 512 * c)
            halves(w2, 0, IQ2)
            for h in range(2):
                rows = slice(512 * h, 512 * (h + 1))
                a = w2[rows, IK2:IK2 + 72].rearrange("(k p) n -> p k n", p=P)
                b = w2[rows, DT2:DT2 + 32].rearrange("(k p) n -> p k n", p=P)
                tile(lambda t, a=a, b=b: [(t[:, :, 0:72], a), (t[:, :, 72:SMALL], b)])
            for c0 in (KV2, Q2, Q2 + 512, GA2, GA2 + 512):
                halves(w2, 0, c0)
                if c0 == KV2:
                    sp.wait_ge(x1_ready, 1)
                    sp.dma_start(x1_dram.rearrange("(t p) n -> p t n", p=P), xres[:]).then_inc(x1_saved, 16)
            for c in range(2):
                halves(d["w_attn_branch_2"][0], 0, 512 * c)
            for c0 in (XBC2 + 2048, XBC2 + 2560, XBC2, XBC2 + 512, XBC2 + 1024, XBC2 + 1536, GB2, GB2 + 512):
                halves(w2, 0, c0)
            for g in range(4):
                halves(w2, 0, Z2 + 512 * g)
            sp.wait_ge(x1_saved, 16)
            sp.wait_ge(gated, 1)
            sp.dma_start(xres[:], x1_dram.rearrange("(t p) n -> p t n", p=P)).then_inc(x1_back, 16)
            for r in range(2):
                for c in range(2):
                    halves(d["w_ssd_branch_2"][0], 1024 * r, 512 * c)
            for c in range(2):
                halves(d["w_out_2"][0], 0, 512 * c)
            assert tiles[0] == 2 * JOBS
            with sp.Fori(0, N_EXP // 2) as i:
                for j in range(2):
                    e = 2 * i + j
                    for h in range(3):
                        n = 3 * j + h
                        sp.wait_ge(w_split, 6 * i + (2 * JOBS + n - 1))
                        if h < 2:
                            for c, w in ((0, e_gate), (1, e_up)):
                                src = w[bass.ds(e, 1), 512 * h:512 * (h + 1), :].rearrange("e (k p) n -> p (e k) n", p=P)
                                sp.dma_start(stage[:, n % 2, :, 256 * c:256 * (c + 1)], src).then_inc(w_in_sem[n % 2], 16)
                        else:
                            rows = stage[:, n % 2].rearrange("p (f a) n -> p f (a n)", f=2)
                            src = e_down[bass.ds(e, 1), :, :].rearrange("e (f p) n -> p (e f) n", p=P)
                            for f in range(2):
                                sp.dma_start(rows[:, f:f + 1, :], src[:, f:f + 1, :]).then_inc(w_in_sem[n % 2], 16)
            sp.wait_ge(x2_ready, 2)
            sp.dma_start(out[0].rearrange("(t p) n -> p t n", p=P), xres[:]).then_inc(out_done, 16)
            sp.wait_ge(out_done, 16)

        @block.gpsimd
        def _(pool):
            def split(b):
                nc.gpsimd.tensor_tensor(w_hi[:, b], stage[:, b], unit[:].unsqueeze(1).broadcast_to([P, HALF, 512]), ALU.mult)
                pool.drain()
                nc.gpsimd.tensor_tensor(w_lo[:, b], stage[:, b], w_hi[:, b].bitcast(F32), ALU.subtract).then_inc(w_split, 1)

            nc.gpsimd.memset(unit[:], 1.0)
            pool.drain()
            for b in range(2):
                pool.wait_ge(w_in_sem[b], 32)
                split(b)
            with pool.Fori(1, TILES // 2) as i:
                for b in range(2):
                    pool.wait_ge(w_in_sem[b], 32 * i + 32)
                    pool.wait_ge(w_used, 2 * i + (b - 1))
                    split(b)

        @block.tensor
        def _(pe):
            turns = Turns(pe, turn_full, turn_free)
            tile = [0, 0]

            def parts(t, *ix):
                return t[0][ix], t[1][ix]

            x_parts, w_parts, ya_parts = (hi, lo), (w_hi, w_lo), (yah, yal)
            everything = slice(None)

            def weights():
                b = tile[0] % 2
                pe.wait_ge(w_split, tile[1] + tile[0] + 1)
                tile[0] += 1
                return b

            def features(x=x_parts, chunks=4, n=S, more=None):
                s = turns.take()
                for half in range(2):
                    b = weights()
                    for m in range(chunks):
                        for k in range(HALF):
                            w = parts(w_parts, everything, b, k)
                            w = tuple(a[:, P * m:P * (m + 1)] for a in w)
                            last = matmul3(pe, ps[s][:, m, 0:n], w, parts(x, everything, HALF * half + k, slice(0, n)),
                                           half == 0 and k == 0, half == 1 and k == HALF - 1)
                    if more:
                        last = more(s, b, half)
                    last.then_inc(w_used, 1)
                pe.drain().then_inc(turn_full, 1)

            def tokens(x=x_parts, n=512, tiles=TT):
                s = turns.take()
                for half in range(2):
                    b = weights()
                    for t in range(tiles):
                        for k in range(HALF):
                            last = matmul3(pe, ps[s][:, t, 0:n],
                                           parts(x, everything, HALF * half + k, slice(P * t, P * (t + 1))),
                                           parts(w_parts, everything, b, k, slice(0, n)),
                                           half == 0 and k == 0, half == 1 and k == HALF - 1)
                    last.then_inc(w_used, 1)
                pe.drain().then_inc(turn_full, 1)

            def turn_rows(rows, tiles=TT, chunks=KC):
                for c0 in range(0, chunks, 4):
                    s = turns.take()
                    for c in range(4):
                        for t in range(tiles):
                            last = pe.transpose(ps[s][:, c, P * t:P * (t + 1)], rows(t, c0 + c), ident[:])
                    last.then_inc(turn_full, 1)

            pe.wait_ge(par_in, PARAMS)
            s = turns.take()
            pe.transpose(ps[s][:, 0, 0:N_ROWS_A], rows_a[:], ident[0:N_ROWS_A, 0:N_ROWS_A])
            pe.transpose(ps[s][:, 0, N_ROWS_A:N_ROWS_A + N_ROWS_B], rows_b[:], ident[0:N_ROWS_B, 0:N_ROWS_B])
            pe.matmul(ps[s][0:4, 1, 0:384], relb[:], bucket[:], start=True, stop=True)
            for g in range(4):
                last = pe.transpose(ps[s][:, 2, P * g:P * (g + 1)], wsp[:, g, :], ident[:])
            last.then_inc(turn_full, 1)

            pe.wait_ge(rows_ready, 1)
            turn_rows(lambda t, c: xn[:, t, P * c:P * (c + 1)], tiles=2)
            pe.wait_ge(lo_ready, 2)

            def mem_values(s, b, half):
                for t in range(2):
                    for k in range(HALF):
                        last = matmul3(pe, ps[s][:, 2 + t, 0:MEM],
                                       parts(x_parts, everything, HALF * half + k, slice(P * t, P * (t + 1))),
                                       parts(w_parts, everything, b, k, slice(256, 512)),
                                       half == 0 and k == 0, half == 1 and k == HALF - 1)
                return last

            features(chunks=2, n=MEM, more=mem_values)

            pe.wait_ge(rows_ready, 2)
            turn_rows(lambda t, c: xn[:, t, P * c:P * (c + 1)])
            pe.wait_ge(lo_ready, 4)

            def swa_values(s, b, half):
                for t in range(TT):
                    for k in range(HALF):
                        last = matmul3(pe, ps[s][:, 3, P * t:P * (t + 1)],
                                       parts(x_parts, everything, HALF * half + k, slice(P * t, P * (t + 1))),
                                       parts(w_parts, everything, b, k, slice(384, 512)),
                                       half == 0 and k == 0 and t == 0, half == 1 and k == HALF - 1 and t == TT - 1)
                return last

            features(chunks=3, more=swa_values)
            tokens()
            features()
            features(chunks=2)
            features()
            features()

            pe.wait_ge(v_normed, 1)
            pe.wait_ge(wspT_ready, 1)
            s = turns.take()
            for g in range(4):
                for n in range(TT):
                    last = pe.matmul(ps[s][:, g, P * n:P * (n + 1)], vt[:, n, P * g:P * (g + 1)], wspT[:, g, :],
                                     start=True, stop=True)
            last.then_inc(turn_full, 1)

            pe.wait_ge(bias_in, 64)
            s = turns.take()
            for h in range(4):
                last = pe.matmul(ps[s][:, h, 0:256], flip[:], bias_r[:, h, :], start=True, stop=True)
            last.then_inc(turn_full, 1)

            def attention(batches, scores, values, nkb, pr, pT, yt, base):
                for i in range(batches + 3):
                    if i < batches:
                        s = turns.take()
                        scores(i, s).then_inc(turn_full, 1)
                    b = i - 2
                    if 0 <= b < batches:
                        s = turns.take()
                        pe.wait_ge(pT_ready, base + b + 1)
                        for h in range(4):
                            for kb in range(nkb(b)):
                                last = pe.matmul(ps[s][:, 0, HD * h:HD * (h + 1)], pT(b)[:, h, P * kb:P * (kb + 1)],
                                                 values(b, h, kb), start=(kb == 0), stop=(kb == nkb(b) - 1))
                        last.then_inc(turn_full, 1)
                    b = i - 1
                    if 0 <= b < batches:
                        s = turns.take()
                        pe.wait_ge(exp_ready, base + b + 1)
                        for h in range(4):
                            for kb in range(nkb(b)):
                                last = pe.transpose(ps[s][:, h, P * kb:P * (kb + 1)],
                                                    pr(b)[:, h, P * kb:P * (kb + 1)], ident[:])
                        last.then_inc(turn_full, 1)
                    b = i - 3
                    if 0 <= b < batches:
                        s = turns.take()
                        pe.wait_ge(yt_ready, base + b + 1)
                        for c in range(2):
                            last = pe.transpose(ps[s][:, 0, P * c:P * (c + 1)], yt[:, b % 2, P * c:P * (c + 1)], ident[:])
                        last.then_inc(turn_full, 1)

            def scores1(b, s):
                n = b % 4
                for h in range(4):
                    if b < 4:
                        lanes = slice(HD * (h // 2), HD * (h // 2 + 1))
                        q, k = qT1[lanes, h % 2, P * n:P * (n + 1)], kT1[lanes, P * max(n - 1, 0):P * (n + 1)]
                    else:
                        lanes = slice(HD * (h % 2), HD * (h % 2 + 1))
                        q, k = mqT[lanes, h // 2, P * n:P * (n + 1)], mkT[lanes, h // 2, :]
                    last = pe.matmul(ps[s][:, h, 0:k.shape[1]], q, k, start=True, stop=True)
                return last

            def values1(b, h, kb):
                if b < 4:
                    return sv1[:, max(b - 1, 0) + kb, HD * (h // 2):HD * (h // 2 + 1)]
                return mv[:, kb, HD * h:HD * (h + 1)]

            pe.wait_ge(qkv1_ready, 2)
            pe.wait_ge(mkv_ready, 1)
            attention(8, scores1, values1, lambda b: 1 if b == 0 else 2, lambda b: pr1[:, b % 2], lambda b: pT1, yt1, 0)

            pe.wait_ge(lo_ready, 6)
            tokens()
            tokens()

            pe.wait_ge(rows_ready, 3)
            turn_rows(lambda t, c: qt[:, t, P * c:P * (c + 1)])
            pe.wait_ge(lo_ready, 8)
            tokens()
            tokens(n=SMALL)
            tokens()
            pe.wait_ge(iq_rows, 1)
            turn_rows(lambda t, c: iqt[:, t, P * c:P * (c + 1)], chunks=4)
            pe.wait_ge(iq_rows, 2)
            s = turns.take()
            for t in range(TT):
                last = pe.transpose(ps[s][:, 0, P * t:P * (t + 1)], ikt[:, t, :], ident[:])
            last.then_inc(turn_full, 1)
            tokens()
            pe.wait_ge(iqT_ready, 2)
            for n in range(1, TT):
                for h4 in range(2):
                    s = turns.take()
                    for h in range(4):
                        i = 4 * h4 + h
                        lanes = slice(HD * (i % 2), HD * (i % 2 + 1))
                        last = pe.matmul(ps[s][:, h, 0:P * (n + 1)], iqT[lanes, i // 2, P * n:P * (n + 1)],
                                         ikT[lanes, 0:P * (n + 1)], start=True, stop=True)
                    last.then_inc(turn_full, 1)
            tokens()
            features()
            features()
            pe.wait_ge(k_rows, 1)
            s = turns.take()
            for c in range(2):
                for t in range(TT):
                    last = pe.transpose(ps[s][:, c, P * t:P * (t + 1)], kvt[:, t, P * c:P * (c + 1)], ident[:])
            last.then_inc(turn_full, 1)
            pe.wait_ge(q_rows, 1)
            turn_rows(lambda t, c: qt[:, t, P * c:P * (c + 1)])

            def scores2(b, s):
                n, g = b // 4, b % 4
                lanes = slice(HD * (g % 2), HD * (g % 2 + 1))
                for i in range(4):
                    last = pe.matmul(ps[s][:, i, 0:P * (n + 1)], qT2[lanes, 4 * (g // 2) + i, P * n:P * (n + 1)],
                                     kT2[lanes, g // 2, 0:P * (n + 1)], start=True, stop=True)
                return last

            pe.wait_ge(kT_ready, 1)
            pe.wait_ge(qT_ready, 2)
            attention(16, scores2, lambda b, h, kb: kvt[:, kb, 256 + HD * (b % 4):256 + HD * (b % 4 + 1)],
                      lambda b: b // 4 + 1, lambda b: pr2[:, b % 2], lambda b: pT2, yt2, 8)
            pe.wait_ge(yal_ready, 16)
            features(ya_parts)
            features(ya_parts)

            def turn_back(n):
                pe.wait_ge(xs_ready, n)
                s = turns.take()
                src = bT if n == 1 else xsT
                for t in range(TT):
                    for c in range(4):
                        last = pe.transpose(ps[s][:, t, P * c:P * (c + 1)], src[:, c, P * t:P * (t + 1)], ident[:])
                last.then_inc(turn_full, 1)

            features()
            features()
            turn_back(1)
            for j in range(4):
                features()
                turn_back(3 + j)

            pe.wait_ge(dt_step, 3)
            for c in range(TT):
                tok = slice(P * c, P * (c + 1))
                s = turns.take()
                pe.matmul(ps[s][:, 0, 0:32], tri[:], dts[:, 1, c, :], start=True, stop=True)
                pe.matmul(ps[s][:, 0, 32:64], ones[:], dts[:, 1, c, :], start=True, stop=True)
                for g in range(4):
                    last = pe.matmul(ps[s][:, 1, P * g:P * (g + 1)], bT[:, g, tok], cT[:, g, tok], start=True, stop=True)
                last.then_inc(turn_full, 1)
                for half in range(2):
                    s = turns.take()
                    for h in range(16):
                        col = dts[:, 1, c, 16 * half + h:16 * half + h + 1].broadcast_to([P, P])
                        last = pe.matmul(ps[s][:, h // 4, P * (h % 4):P * (h % 4 + 1)], col, tri[:], start=True, stop=True)
                    last.then_inc(turn_full, 1)
                pe.wait_ge(m_ready, 4 * (c + 1))
                pe.wait_ge(xd_ready, c + 1)
                s = turns.take()
                for h in range(32):
                    last = pe.matmul(ps[s][:, h // 8, HD * (h % 8):HD * (h % 8 + 1)], decay[:, h, :], xd[:, h, :],
                                     start=True, stop=True)
                last.then_inc(turn_full, 1)
                if c > 0:
                    pe.wait_ge(st_ready, c)
                    s = turns.take()
                    for g in range(4):
                        last = pe.matmul(ps[s][:, g, :], cT[:, g, tok], state[:, 512 * g:512 * (g + 1)], start=True, stop=True)
                    last.then_inc(turn_full, 1)
                if c < TT - 1:
                    pe.wait_ge(xe_ready, c + 1)
                    s = turns.take()
                    for g in range(4):
                        last = pe.matmul(ps[s][:, g, :], btok[:, c, P * g:P * (g + 1)], xe[:, 8 * g:8 * (g + 1), :],
                                         start=True, stop=True)
                    last.then_inc(turn_full, 1)

            features()
            features()
            for g in range(4):
                tokens()
            for r in range(2):
                pe.wait_ge(y_rows, r + 1)
                turn_rows(lambda t, c, r=r: xtok[:, t, 1024 * r + P * c:1024 * r + P * (c + 1)])
                pe.wait_ge(lo_ready, 10 + 2 * r)
                features()
                features()
            pe.wait_ge(lo_ready, 14)
            tokens()
            tokens()

            pe.wait_ge(rows_ready, 4)
            turn_rows(lambda t, c: xn[:, t, P * c:P * (c + 1)])
            pe.wait_ge(lo_ready, 16)
            s = turns.take()
            for t in range(TT):
                for k in range(KC):
                    for i, part in enumerate((hi, lo)):
                        last = pe.matmul(ps[s][:, t, 0:36], part[:, k, P * t:P * (t + 1)].bitcast(F32), w_rt[:, k, :],
                                         start=(k == 0 and i == 0), stop=(k == KC - 1 and i == 1))
            last.then_inc(turn_full, 1)
            with turns.loop(N_EXP // 2, 6) as i:
                first = tile[0]
                tile[1] = 6 * i
                for j in range(2):
                    features()
                    pe.wait_ge(actl_ready, 2 * i + (j + 1))
                    b = weights()
                    down = [w[:, b].rearrange("p (f a) n -> p f (a n)", f=2) for w in w_parts]
                    for c in range(2):
                        s = turns.take()
                        for t in range(TT):
                            for f in range(2):
                                last = matmul3(pe, ps[s][:, t, :], (act_hi[j][:, f, P * t:P * (t + 1)], act_lo[j][:, f, P * t:P * (t + 1)]),
                                               [w[:, f, 512 * c:512 * (c + 1)] for w in down], f == 0, f == 1)
                        if c == 1:
                            last.then_inc(w_used, 1)
                            pe.drain().then_inc(turn_full, 1)
                        else:
                            last.then_inc(turn_full, 1)
                assert tile[0] == first + 6

        @block.scalar
        def _(act_eng):
            A = act_eng
            turns = Turns(A, turn_full, turn_free)
            for dst, src in params:
                A.dma_start(dst, src).then_inc(par_in, 16)

            def norm(rows, n, junk, k):
                for t in range(n):
                    A.activation(junk, rows(t), ACT.Square, accum_out=st[:, 0, k + t:k + t + 1])
                    A.drain()
                A.drain()
                A.activation(st[:, 1, k:k + n], st[:, 0, k:k + n], ACT.Sqrt, scale=1.0 / D, bias=st[:, 9, 0:1]).then_inc(rms_ready, 1)

            def high_parts(name, first=0, n=S, chunks=KC):
                for c0 in range(0, chunks, 4):
                    s = turns.see()
                    for c in range(4):
                        A.activation(hi[:, c0 + c, 0:n], ps[s][:, c, 0:n], ACT.Copy, scale=gain(name, first + c0 + c))\
                            .then_inc(hi_ready, 1)

            def softmax(b, base, width, src, dst, sinks_too):
                k = b % 4
                A.wait_ge(max_ready, base + b + 1)
                for h in range(4):
                    last = A.activation(dst[:, h, 0:width], src[:, h, 0:width], ACT.Exp, bias=sm[:, 2, k, h:h + 1],
                                        accum_out=sm[:, 1, k, h:h + 1])
                if sinks_too:
                    last = A.activation(sm[:, 4, k, :], sm[:, 3, k, :], ACT.Exp)
                last.then_inc(exp_ready, 1)

            A.wait_ge(setup_done, 1)
            A.wait_ge(mem_in, 16)
            norm(lambda t: memb[:, t, :], 2, yT[:, 6:8, :].rearrange("p c n -> p (c n)"), 0)
            A.wait_ge(cols_ready, 1)
            turns.skip()
            high_parts("mem", n=MEM)
            A.wait_ge(x_in, 16)
            norm(lambda t: xres[:, t, :], TT, yT[:, 6:8, :].rearrange("p c n -> p (c n)"), 4)
            s = turns.see()
            A.activation(mkT[:], ps[s][:, 0:2, 0:MEM], ACT.Copy)
            A.activation(mv[:], ps[s][:, 2:4, 0:MEM], ACT.Copy).then_inc(mkv_ready, 1)
            A.drain().then_inc(turn_free[s], 1)
            high_parts("pre")
            s = turns.see()
            for h in range(4):
                A.activation(qT1[HD * (h // 2):HD * (h // 2 + 1), h % 2, :], ps[s][HD * (h % 2):HD * (h % 2 + 1), h // 2, :],
                             ACT.Copy, scale=HD ** -0.5)
            A.activation(kT1[:], ps[s][:, 2, :], ACT.Copy)
            A.activation(sv1[:], ps[s][:, 3, :].rearrange("p (t n) -> p t n", t=TT), ACT.Copy).then_inc(qkv1_ready, 1)
            A.drain().then_inc(turn_free[s], 1)
            s = turns.see()
            A.activation(vt[:], ps[s][:], ACT.Gelu_apprx_tanh).then_inc(v_ready, 1)
            A.drain().then_inc(turn_free[s], 1)
            A.wait_ge(v_ready, 2)
            A.activation(st[:, 4, 0:16], st[:, 3, 0:16], ACT.Sqrt, scale=1.0 / P, bias=st[:, 9, 0:1]).then_inc(rms_ready, 1)
            s = turns.see()
            A.activation(uT[:], ps[s][:], ACT.Gelu_apprx_tanh).then_inc(u_ready, 1)
            A.drain().then_inc(turn_free[s], 1)
            s = turns.see()
            A.activation(mqT[:], ps[s][:, 0:2, :], ACT.Copy, scale=HD ** -0.5).then_inc(qkv1_ready, 1)
            A.drain().then_inc(turn_free[s], 1)
            for c in range(2):
                s = turns.see()
                A.activation(zT[:, 4 * c:4 * c + 4, :], ps[s][:], ACT.Silu).then_inc(z1_ready, 1)
                A.drain().then_inc(turn_free[s], 1)
            turns.skip(2)

            for i in range(8 + 3):
                if i < 8:
                    width = P if i == 0 else 256
                    if i < 4:
                        turns.skip()
                        softmax(i, 0, width, pr1[:, i % 2], pr1[:, i % 2], True)
                    else:
                        s = turns.see()
                        softmax(i, 0, width, ps[s], pr1[:, i % 2], False)
                        A.drain().then_inc(turn_free[s], 1)
                if 0 <= i - 2 < 8:
                    turns.skip()
                if 0 <= i - 1 < 8:
                    width = P if i == 1 else 256
                    s = turns.see()
                    A.activation(pT1[:, :, 0:width], ps[s][:, :, 0:width], ACT.Copy).then_inc(pT_ready, 1)
                    A.drain().then_inc(turn_free[s], 1)
                b = i - 3
                if b >= 0:
                    s = turns.see()
                    c0, n = (4, b) if b < 4 else (6, b - 4)
                    A.activation(yT[:, c0:c0 + 2, P * n:P * (n + 1)],
                                 ps[s][:, 0, 0:256].rearrange("p (c t) -> p c t", c=2), ACT.Copy).then_inc(yT_ready, 1)
                    A.drain().then_inc(turn_free[s], 1)
            for c0 in (0, 4):
                A.wait_ge(z1_ready, 3 + c0 // 4)
                A.activation(hi[:, c0:c0 + 4, :], yT[:, c0:c0 + 4, :], ACT.Copy).then_inc(hi_ready, 4)
            for c in range(2):
                s = turns.see()
                A.activation(xn[:, :, 512 * c:512 * (c + 1)], ps[s][:], ACT.Copy).then_inc(wo_ready, 1)
                A.drain().then_inc(turn_free[s], 1)
            norm(lambda t: xn[:, t, :], TT, yT[:, 0:2, :].rearrange("p c n -> p (c n)"), 8)

            A.wait_ge(x1_ready, 1)
            norm(lambda t: xres[:, t, :], TT, iqt[:, 0:2, :].rearrange("p c n -> p (c n)"), 12)
            high_parts("attn")
            s = turns.see()
            A.activation(iqt[:], ps[s][:], ACT.Copy).then_inc(iq_ready, 1)
            A.drain().then_inc(turn_free[s], 1)
            s = turns.see()
            A.activation(smt[:], ps[s][:, :, 0:SMALL], ACT.Copy).then_inc(small_ready, 1)
            A.drain().then_inc(turn_free[s], 1)
            A.wait_ge(sq_ready, 1)
            A.activation(st[:, 4, 16:20], st[:, 3, 16:20], ACT.Sqrt, scale=1.0 / HD, bias=st[:, 9, 0:1]).then_inc(rms_ready, 1)
            s = turns.see()
            A.activation(kvt[:], ps[s][:], ACT.Copy).then_inc(kv_ready, 1)
            A.drain().then_inc(turn_free[s], 1)
            s = turns.see()
            A.activation(iqT[:], ps[s][:], ACT.Copy, scale=HD ** -0.5).then_inc(iqT_ready, 1)
            A.drain().then_inc(turn_free[s], 1)
            s = turns.see()
            A.activation(ikT[:], ps[s][:, 0, :], ACT.Copy).then_inc(iqT_ready, 1)
            A.drain().then_inc(turn_free[s], 1)
            A.wait_ge(sq_ready, 2)
            A.activation(st[:, 4, 20:36], st[:, 3, 20:36], ACT.Sqrt, scale=1.0 / HD, bias=st[:, 9, 0:1]).then_inc(rms_ready, 1)
            s = turns.see()
            A.activation(qt[:, :, 0:512], ps[s][:], ACT.Copy).then_inc(q_ready, 1)
            A.drain().then_inc(turn_free[s], 1)
            for i in range(6):
                s = turns.see()
                n = 1 + i // 2
                if i > 0:
                    A.wait_ge(rel_used, i)
                A.activation(rel[:, :, 0:P * (n + 1)], ps[s][:, :, 0:P * (n + 1)], ACT.Relu).then_inc(rel_ready, 1)
                A.drain().then_inc(turn_free[s], 1)
            s = turns.see()
            A.activation(qt[:, :, 512:1024], ps[s][:], ACT.Copy).then_inc(q_ready, 1)
            A.drain().then_inc(turn_free[s], 1)
            A.wait_ge(x1_saved, 16)
            for c in range(2):
                s = turns.see()
                A.activation(sg[:, 4 * c:4 * c + 4, :], ps[s][:], ACT.Tanh, scale=0.5).then_inc(sga_ready, 1)
                A.drain().then_inc(turn_free[s], 1)
            A.wait_ge(sq_ready, 3)
            A.activation(st[:, 7, 0:64], st[:, 6, 0:64], ACT.Sqrt, scale=1.0 / HD, bias=st[:, 9, 0:1]).then_inc(rms_ready, 1)
            s = turns.see()
            A.activation(kT2[:], ps[s][:, 0:2, :], ACT.Copy).then_inc(kT_ready, 1)
            A.drain().then_inc(turn_free[s], 1)
            for c in range(2):
                s = turns.see()
                for j in range(2):
                    for odd in range(2):
                        last = A.activation(qT2[HD * j:HD * (j + 1), 4 * c + odd:4 * c + odd + 3:2, :],
                                            ps[s][HD * odd:HD * (odd + 1), 2 * j:2 * j + 2, :], ACT.Copy, scale=HD ** -0.5)
                last.then_inc(qT_ready, 1)
                A.drain().then_inc(turn_free[s], 1)
            for i in range(16 + 3):
                if i < 16:
                    turns.skip()
                    softmax(i, 8, P * (i // 4 + 1), pr2[:, i % 2], pr2[:, i % 2], False)
                if 0 <= i - 2 < 16:
                    turns.skip()
                if 0 <= i - 1 < 16:
                    width = P * ((i - 1) // 4 + 1)
                    s = turns.see()
                    A.activation(pT2[:, :, 0:width], ps[s][:, :, 0:width], ACT.Copy).then_inc(pT_ready, 1)
                    A.drain().then_inc(turn_free[s], 1)
                b = i - 3
                if b >= 0:
                    s = turns.see()
                    n, g = b // 4, b % 4
                    A.activation(yah[:, 2 * g:2 * g + 2, P * n:P * (n + 1)],
                                 ps[s][:, 0, 0:256].rearrange("p (c t) -> p c t", c=2), ACT.Copy).then_inc(yT_ready, 1)
            turns.skip(2)

            A.wait_ge(dt_step, 1)
            A.activation(dtt[:, 1], dtt[:, 0], ACT.Abs)
            A.activation(dtt[:, 6, 0, :], a_log[:], ACT.Exp)
            A.drain()
            A.activation(dtt[:, 2], dtt[:, 1], ACT.Exp, scale=-1.0).then_inc(dt_act, 1)
            A.wait_ge(dt_step, 2)
            A.activation(dtt[:, 5], dtt[:, 3], ACT.Ln).then_inc(dt_act, 1)

            def into_conv(n):
                s = turns.see()
                if n > 1:
                    A.wait_ge(conv_out, n - 1)
                A.activation(cpad[:, :, 3:3 + S], ps[s][:], ACT.Copy).then_inc(conv_in, 1)
                A.drain().then_inc(turn_free[s], 1)

            def out_of_conv(n, dst):
                A.wait_ge(conv_out, n)
                A.activation(dst[:], dst[:], ACT.Silu).then_inc(xs_ready, 1)

            def rows_back(dst):
                s = turns.see()
                A.activation(dst, ps[s][:], ACT.Copy).then_inc(xtok_ready, 1)
                A.drain().then_inc(turn_free[s], 1)

            A.wait_ge(conv_in, 1)
            into_conv(1)
            out_of_conv(1, bT)
            into_conv(2)
            out_of_conv(2, cT)
            rows_back(btok[:])
            for j in range(4):
                into_conv(3 + j)
                out_of_conv(3 + j, xsT)
                rows_back(xtok[:, :, 512 * j:512 * (j + 1)])

            for c in range(TT):
                turns.skip()
                A.wait_ge(acs_ready, c + 1)
                A.activation(st[:, 5, 0:32], st[:, 2, 0:32], ACT.Exp)
                A.activation(st[:, 4, 0:32], st[:, 1, 0:32], ACT.Exp)
                A.activation(st[:, 6, 0:32], st[:, 3, 0:32], ACT.Exp).then_inc(e_ready, 1)
                for half in range(2):
                    s = turns.see()
                    for h in range(16):
                        hh = 16 * half + h
                        A.activation(decay[:, hh, :], ps[s][:, h // 4, P * (h % 4):P * (h % 4 + 1)], ACT.Relu,
                                     bias=st[:, 1, hh:hh + 1], scale=-1.0)
                    A.drain()
                    for g in (2 * half, 2 * half + 1):
                        e = decay[:, 8 * g:8 * g + 8, :]
                        A.activation(e, e, ACT.Exp, scale=-1.0).then_inc(e_ready, 1)
                    A.drain().then_inc(turn_free[s], 1)
                turns.skip(1 + (c > 0) + (c < TT - 1))

            for c in range(2):
                s = turns.see()
                A.activation(sgb[:, 4 * c:4 * c + 4, :], ps[s][:], ACT.Tanh, scale=0.5).then_inc(sgb_ready, 1)
                A.drain().then_inc(turn_free[s], 1)
            for g in range(4):
                s = turns.see()
                if g > 0:
                    A.wait_ge(gated, g)
                A.activation(sz[:], ps[s][:], ACT.Silu).then_inc(sz_ready, 1)
                A.drain().then_inc(turn_free[s], 1)
            A.wait_ge(gated, 4)
            for g in range(4):
                for t in range(TT):
                    A.activation(junk3[:, 0:512], xtok[:, t, 512 * g:512 * (g + 1)], ACT.Square,
                                 accum_out=st[:, 0, 32 + 4 * g + t:33 + 4 * g + t])
                    A.drain()
            A.drain()
            A.activation(st[:, 1, 32:48], st[:, 0, 32:48], ACT.Sqrt, scale=1.0 / 512, bias=st[:, 9, 0:1]).then_inc(rms_ready, 1)
            for r in range(2):
                high_parts("ssd", first=KC * r)
                turns.skip(2)
            for c0 in (0, 4):
                A.wait_ge(mT_ready, 1)
                A.activation(hi[:, c0:c0 + 4, :], mT[:, c0:c0 + 4, :], ACT.Copy, scale=0.5).then_inc(hi_ready, 4)
            turns.skip(2)

            A.wait_ge(x2_ready, 1)
            norm(lambda t: xres[:, t, :], TT, junk3[:], 16)
            high_parts("ffn")
            turns.skip()
            A.wait_ge(rt_step, 1)
            A.activation(rt[:, 1, :, 0:4], rt[:, 1, :, 0:4], ACT.Exp).then_inc(rt_act, 1)
            A.wait_ge(rt_step, 2)
            A.activation(rt[:, 8, :, 0:1], rt[:, 8, :, 0:1], ACT.Exp).then_inc(rt_act, 1)
            with turns.loop(N_EXP // 2, 6) as i:
                for j in range(2):
                    s = turns.see()
                    A.wait_ge(act_ready, 2 * i + (j + 1))
                    A.activation(sa[:], ps[s][:, 0:2, :], ACT.Silu).then_inc(sa_ready, 1)
                    A.wait_ge(act_ready, 2 * i + (j + 2))
                    A.activation(act_hi[j][:], act[:], ACT.Copy).then_inc(acth_ready, 1)
                    turns.skip(2)

        @block.vector
        def _(V):
            turns = Turns(V, turn_full, turn_free)
            his = [0]

            def unit_rows(dst, rows, n, count, k):
                V.wait_ge(rms_ready, count)
                V.reciprocal(st[:, 2, k:k + n], st[:, 1, k:k + n])
                V.drain()
                for t in range(n):
                    last = V.tensor_scalar(dst(t), rows(t), st[:, 2, k + t:k + t + 1], None, ALU.mult)
                return last

            def low_parts(name, first=0, n=S, chunks=KC):
                for c0 in range(0, chunks, 4):
                    s = turns.see()
                    for c in range(4):
                        his[0] += 1
                        V.wait_ge(hi_ready, his[0])
                        last = V.scalar_tensor_tensor(lo[:, c0 + c, 0:n], ps[s][:, c, 0:n], gain(name, first + c0 + c),
                                                      hi[:, c0 + c, 0:n].bitcast(F32), ALU.mult, ALU.subtract)
                    last.then_inc(lo_ready, 1)
                    V.drain().then_inc(turn_free[s], 1)

            def rope(x, heads):
                a, b = x[:, :, :, 0:8], x[:, :, :, 8:16]
                c, s = bc(cos[:], 2, heads), bc(sin[:], 2, heads)
                a_s, b_s_ = (rot[:, i, :, 0:8 * heads].rearrange("p t (h f) -> p t h f", h=heads) for i in range(2))
                V.tensor_tensor(a_s, a, s, ALU.mult)
                V.tensor_tensor(b_s_, b, s, ALU.mult)
                V.drain()
                V.tensor_tensor(a, a, c, ALU.mult)
                V.tensor_tensor(b, b, c, ALU.mult)
                V.drain()
                V.tensor_tensor(a, a, b_s_, ALU.subtract)
                return V.tensor_tensor(b, b, a_s, ALU.add)

            V.memset(st[:, 9, :], EPS).then_inc(setup_done, 1)
            V.memset(ones[:], 1.0)
            V.wait_ge(par_in, PARAMS)
            s = turns.see()
            V.tensor_copy(cols[:], ps[s][:, 0, 0:N_ROWS_A + N_ROWS_B]).then_inc(cols_ready, 1)
            V.tensor_tensor(brow[:], ps[s][0:4, 1, 0:384], outside[:], ALU.add).then_inc(brow_ready, 1)
            V.tensor_tensor(wspT[:], ps[s][:, 2, :].rearrange("p (g t) -> p g t", g=4), bc(tri[:], 1, 4), ALU.mult)\
                .then_inc(wspT_ready, 1)
            V.drain().then_inc(turn_free[s], 1)

            unit_rows(lambda t: xn[:, t, :], lambda t: memb[:, t, :], 2, 1, 0).then_inc(rows_ready, 1)
            V.drain()
            low_parts("mem", n=MEM)
            unit_rows(lambda t: xn[:, t, :], lambda t: xres[:, t, :], TT, 2, 4).then_inc(rows_ready, 1)
            turns.skip()
            low_parts("pre")
            turns.skip()

            turns.skip()
            V.wait_ge(v_ready, 1)
            v4 = vt[:].rearrange("p t (g c) -> p (t g) c", g=4)
            t4 = vtmp[:].rearrange("p t (g c) -> p (t g) c", g=4)
            V.tensor_reduce(st[:, 3, 0:16], v4, AX.X, ALU.add)
            V.drain()
            V.tensor_scalar(st[:, 5, 0:16], st[:, 3, 0:16], 1.0 / P, None, ALU.mult)
            V.drain()
            V.tensor_tensor(v4, v4, bc(st[:, 5, 0:16], 2, P), ALU.subtract)
            V.drain()
            V.tensor_tensor(t4, v4, v4, ALU.mult)
            V.drain()
            V.tensor_reduce(st[:, 3, 0:16], t4, AX.X, ALU.add).then_inc(v_ready, 1)
            V.wait_ge(rms_ready, 3)
            V.reciprocal(st[:, 5, 0:16], st[:, 4, 0:16])
            V.drain()
            V.tensor_tensor(v4, v4, bc(st[:, 5, 0:16], 2, P), ALU.mult)
            V.drain()
            V.tensor_tensor(vt[:], vt[:], bc(v_g[:], 1, TT), ALU.mult)
            V.drain()
            V.tensor_tensor(vt[:], vt[:], bc(v_b[:], 1, TT), ALU.add).then_inc(v_normed, 1)
            turns.skip(4)
            V.wait_ge(bias_in, 64)
            s = turns.see()
            for g in range(4):
                last = V.tensor_tensor(yT[:, g, :].rearrange("p (n t) -> p n t", n=TT),
                                       ps[s][:, g, :].rearrange("p (n t) -> p n t", n=TT), bc(b_s[:, g, :], 1, TT), ALU.add)
            V.drain().then_inc(turn_free[s], 1)
            V.wait_ge(u_ready, 1)
            V.tensor_tensor(yT[:, 0:4], yT[:, 0:4], uT[:], ALU.mult)
            V.drain()
            V.wait_ge(z1_ready, 1)
            V.tensor_tensor(yT[:, 0:4], yT[:, 0:4], zT[:, 0:4], ALU.mult)

            s = turns.see()
            V.tensor_copy(bias[:], ps[s][:, :, 0:256])
            V.drain().then_inc(turn_free[s], 1)

            def probabilities_used(b, base, yt, sinks_too):
                s = turns.see()
                k = b % 4
                V.wait_ge(exp_ready, base + b + 1)
                den = sm[:, 1, k, :]
                if sinks_too:
                    V.tensor_tensor(den, den, sm[:, 4, k, :], ALU.add)
                    V.drain()
                V.reciprocal(sm[:, 5, k, :], den)
                V.drain()
                V.tensor_tensor(yt[:, b % 2, :].rearrange("p (h d) -> p h d", h=4),
                                ps[s][:, 0, 0:256].rearrange("p (h d) -> p h d", h=4), bc(sm[:, 5, k, :], 2, HD), ALU.mult)\
                    .then_inc(yt_ready, 1)
                V.drain().then_inc(turn_free[s], 1)

            for i in range(8 + 3):
                if i < 8:
                    k, n = i % 4, i
                    s = turns.see()
                    if i < 4:
                        width = P if n == 0 else 256
                        for h in range(4):
                            V.tensor_tensor_reduce(pr1[:, i % 2, h, 0:width], ps[s][:, h, 0:width], bias[:, h, 256 - width:256],
                                                   1.0, -3e38, ALU.add, ALU.max, sm[:, 0, k, h:h + 1])
                        V.drain().then_inc(turn_free[s], 1)
                        V.tensor_tensor(sm[:, 0, k, :], sm[:, 0, k, :], sinks[:], ALU.max)
                        V.drain()
                        V.tensor_tensor(sm[:, 3, k, :], sinks[:], sm[:, 0, k, :], ALU.subtract)
                    else:
                        V.tensor_reduce(sm[:, 0, k, :], ps[s][:, :, 0:MEM], AX.X, ALU.max)
                        V.drain()
                    V.tensor_scalar(sm[:, 2, k, :], sm[:, 0, k, :], -1.0, None, ALU.mult).then_inc(max_ready, 1)
                if 0 <= i - 2 < 8:
                    probabilities_used(i - 2, 0, yt1, i - 2 < 4)
                if 0 <= i - 1 < 8:
                    turns.skip()
                if i >= 3:
                    turns.skip()
            V.drain().then_inc(z1_ready, 1)
            V.wait_ge(z1_ready, 3)
            V.wait_ge(yT_ready, 8)
            V.tensor_tensor(yT[:, 4:8], yT[:, 4:8], zT[:, 4:8], ALU.mult).then_inc(z1_ready, 1)
            for c0 in (0, 4):
                his[0] += 4
                V.wait_ge(z1_ready, 3 + c0 // 4)
                V.wait_ge(hi_ready, his[0])
                V.tensor_tensor(lo[:, c0:c0 + 4], yT[:, c0:c0 + 4], hi[:, c0:c0 + 4].bitcast(F32), ALU.subtract)\
                    .then_inc(lo_ready, 1)
            turns.skip(2)
            V.wait_ge(rms_ready, 4)
            V.reciprocal(st[:, 2, 8:8 + TT], st[:, 1, 8:8 + TT])
            V.drain()
            for t in range(TT):
                V.scalar_tensor_tensor(xn[:, t, :], xn[:, t, :], st[:, 2, 8 + t:9 + t], post_g[:], ALU.mult, ALU.mult)
            V.drain()
            V.tensor_tensor(xres[:], xres[:], xn[:], ALU.add).then_inc(x1_ready, 1)
            V.drain()

            unit_rows(lambda t: qt[:, t, :], lambda t: xres[:, t, :], TT, 5, 12).then_inc(rows_ready, 1)
            low_parts("attn")

            turns.skip()
            V.wait_ge(iq_ready, 1)
            rope(iqt[:].rearrange("p t (h d) -> p t h d", h=8), 8).then_inc(iq_rows, 1)
            turns.skip()
            V.wait_ge(small_ready, 1)
            ik = smt[:, :, 0:HD]
            V.tensor_tensor(ikt[:, :, 0:HD], ik, ik, ALU.mult)
            V.tensor_scalar(smt[:, :, HD:HD + 8], smt[:, :, HD:HD + 8], 8 ** -0.5, None, ALU.mult)
            V.drain()
            V.tensor_reduce(st[:, 3, 16:20], ikt[:, :, 0:HD], AX.X, ALU.add).then_inc(sq_ready, 1)
            V.wait_ge(rms_ready, 6)
            V.reciprocal(st[:, 5, 16:20], st[:, 4, 16:20])
            V.drain()
            V.tensor_tensor(ik, ik, bc(st[:, 5, 16:20], 2, HD), ALU.mult)
            V.drain()
            V.tensor_tensor(ikt[:, :, 0:HD], ik, bc(ik_g[:], 1, TT), ALU.mult)
            V.drain()
            rope(ikt[:, :, 0:HD].unsqueeze(2), 1)
            V.drain()
            V.tensor_copy(ikt[:, :, HD:P], ikt[:, :, 0:HD]).then_inc(iq_rows, 1)

            def norm_heads(x, heads, gains, root):
                t = x.shape[1]
                x3 = x.rearrange("p t (h d) -> p t h d", h=heads)
                V.tensor_tensor(x3, x3, bc(root, 3, HD), ALU.mult)
                V.drain()
                return V.tensor_tensor(x3, x3, gains[:].unsqueeze(1).unsqueeze(1).broadcast_to([P, t, heads, HD]), ALU.mult)

            turns.skip()
            V.wait_ge(kv_ready, 1)
            k4 = kvt[:, :, 0:256]
            sq_k = sqr[:].rearrange("p a b -> p (a b)")[:, 0:1024].rearrange("p (t n) -> p t n", t=TT)
            V.tensor_tensor(sq_k, k4, k4, ALU.mult)
            V.drain()
            V.tensor_reduce(st[:, 3, 20:36], sq_k.rearrange("p t (h d) -> p t h d", h=4), AX.X, ALU.add).then_inc(sq_ready, 1)
            V.wait_ge(rms_ready, 7)
            V.reciprocal(st[:, 5, 20:36], st[:, 4, 20:36])
            V.drain()
            norm_heads(k4, 4, k_g, st[:, 5, 20:36].rearrange("p (t h) -> p t h", t=TT))
            V.drain()
            rope(k4.rearrange("p t (h d) -> p t h d", h=4), 4).then_inc(k_rows, 1)
            turns.skip(3)

            for i in range(6):
                n, h4 = 1 + i // 2, i % 2
                w = P * (n + 1)
                turns.skip()
                V.wait_ge(rel_ready, i + 1)
                for h in range(4):
                    k = 4 * h4 + h
                    iw = smt[:, n, HD + k:HD + k + 1]
                    if k == 0:
                        last = V.tensor_scalar(score[:, n - 1, 0:w], rel[:, h, 0:w], iw, None, ALU.mult)
                    else:
                        last = V.scalar_tensor_tensor(score[:, n - 1, 0:w], rel[:, h, 0:w], iw, score[:, n - 1, 0:w],
                                                      ALU.mult, ALU.add)
                    if h == 3:
                        last.then_inc(rel_used, 1)
                    V.drain()
            V.memset(sel[:, 0, 0:P], 0.0)
            V.drain()
            V.memset(sel[0:64, 0, 64:P], NEG)
            for n in range(1, TT):
                w = P * (n + 1)
                row = score[:, n - 1, 0:w]
                V.memset(score[0:64, n - 1, P * n + 64:w], -1e38)
                V.drain()
                for r in range(TOPK // 8):
                    V.max(top[:, r % 2, :], row)
                    V.drain()
                    V.match_replace(row, top[:, r % 2, :], row, -3e38)
                    V.drain()
                V.tensor_scalar(sel[:, n, 0:w], row, -2e38, NEG, ALU.is_gt, ALU.mult)
            V.drain()
            turns.skip(3)
            V.wait_ge(q_ready, 2)
            for t in (0, 2):
                V.tensor_tensor(sqr[:], qt[:, t:t + 2, :], qt[:, t:t + 2, :], ALU.mult)
                V.drain()
                last = V.tensor_reduce(st[:, 6, 16 * t:16 * t + 32], sqr[:].rearrange("p t (h d) -> p t h d", h=16), AX.X, ALU.add)
                if t == 2:
                    last.then_inc(sq_ready, 1)
                V.drain()
            V.wait_ge(rms_ready, 8)
            V.reciprocal(st[:, 8, 0:64], st[:, 7, 0:64])
            V.drain()
            norm_heads(qt[:], 16, q_g, st[:, 8, 0:64].rearrange("p (t h) -> p t h", t=TT))
            V.drain()
            rope(qt[:].rearrange("p t (h d) -> p t h d", h=16), 16).then_inc(q_rows, 1)
            turns.skip(3)

            for i in range(16 + 3):
                if i < 16:
                    k, n = i % 4, i // 4
                    width = P * (n + 1)
                    s = turns.see()
                    for h in range(4):
                        V.tensor_tensor_reduce(pr2[:, i % 2, h, 0:width], ps[s][:, h, 0:width], sel[:, n, 0:width],
                                               1.0, -3e38, ALU.add, ALU.max, sm[:, 0, k, h:h + 1])
                    V.drain().then_inc(turn_free[s], 1)
                    V.tensor_scalar(sm[:, 2, k, :], sm[:, 0, k, :], -1.0, None, ALU.mult).then_inc(max_ready, 1)
                if 0 <= i - 2 < 16:
                    probabilities_used(i - 2, 8, yt2, False)
                if 0 <= i - 1 < 16:
                    turns.skip()
                b = i - 3
                if b >= 0:
                    s = turns.see()
                    nn, g = b // 4, b % 4
                    V.wait_ge(yT_ready, 8 + b + 1)
                    o = (slice(None), slice(2 * g, 2 * g + 2), slice(P * nn, P * (nn + 1)))
                    V.tensor_tensor(yal[o], ps[s][:, 0, 0:256].rearrange("p (c t) -> p c t", c=2), yah[o].bitcast(F32), ALU.subtract)\
                        .then_inc(yal_ready, 1)
                    V.drain().then_inc(turn_free[s], 1)
            for c in range(2):
                s = turns.see()
                V.wait_ge(sga_ready, c + 1)
                V.scalar_tensor_tensor(mT[:, 4 * c:4 * c + 4], sg[:, 4 * c:4 * c + 4], 1.0, ps[s][:], ALU.add, ALU.mult)
                V.drain().then_inc(turn_free[s], 1)

            V.tensor_tensor(dtt[:, 0], smt[:, :, 72:SMALL], bc(dt_b[:], 1, TT), ALU.add).then_inc(dt_step, 1)
            V.wait_ge(dt_act, 1)
            V.tensor_scalar(dtt[:, 3], dtt[:, 2], 1.0, None, ALU.add)
            V.drain().then_inc(dt_step, 1)
            V.tensor_scalar(dtt[:, 4], dtt[:, 3], 1.0, None, ALU.is_equal)
            V.drain()
            V.scalar_tensor_tensor(dtt[:, 7], dtt[:, 3], -1.0, dtt[:, 4], ALU.add, ALU.add)
            V.drain()
            V.reciprocal(dtt[:, 7], dtt[:, 7])
            V.drain()
            V.tensor_tensor(dtt[:, 7], dtt[:, 7], dtt[:, 2], ALU.mult)
            V.wait_ge(dt_act, 2)
            V.tensor_tensor(dtt[:, 4], dtt[:, 4], dtt[:, 2], ALU.mult)
            V.drain()
            V.tensor_tensor(dtt[:, 7], dtt[:, 7], dtt[:, 5], ALU.mult)
            V.drain()
            V.tensor_tensor(dtt[:, 7], dtt[:, 7], dtt[:, 4], ALU.add)
            V.drain()
            V.scalar_tensor_tensor(dts[:, 0], dtt[:, 0], 0.0, dtt[:, 7], ALU.max, ALU.add)
            V.tensor_scalar(dtt[:, 6, 1, :], dtt[:, 6, 0, :], -1.0, None, ALU.mult)
            V.drain()
            V.tensor_tensor(dts[:, 1], dts[:, 0], bc(dtt[:, 6, 1, :], 1, TT), ALU.mult).then_inc(dt_step, 1)

            V.memset(cpad[:, :, 0:3], 0.0).then_inc(conv_in, 1)

            def convolve(n, c0, dst):
                V.wait_ge(conv_in, n + 1)
                if dst is xsT and n > 3:
                    V.wait_ge(xtok_ready, n - 2)
                def tap(k, c):
                    j = N_ROWS_A + 24 * k + c0 + c
                    return cols[:, j:j + 1]
                for c in range(4):
                    V.tensor_scalar(dst[:, c, :], cpad[:, c, 0:S], tap(0, c), gain("conv_b", c0 + c), ALU.mult, ALU.add)
                V.drain()
                for k in range(1, 4):
                    for c in range(4):
                        V.scalar_tensor_tensor(dst[:, c, :], cpad[:, c, k:k + S], tap(k, c), dst[:, c, :], ALU.mult, ALU.add)
                    if k < 3:
                        V.drain()
                V.drain().then_inc(conv_out, 1)

            convolve(1, 16, bT)
            convolve(2, 20, cT)
            for j in range(4):
                convolve(3 + j, 4 * j, xsT)
            turns.skip(11)

            V.wait_ge(xtok_ready, 5)
            for c in range(TT):
                s = turns.see()
                V.tensor_copy(st[:, 1, 0:32], ps[s][:, 0, 0:32])
                V.tensor_copy(st[:, 3, 0:32], ps[s][:, 0, 32:64])
                V.tensor_tensor(cb[:], ps[s][:, 1, :].rearrange("p (g l) -> p g l", g=4), bc(tri[:], 1, 4), ALU.mult)
                V.drain().then_inc(turn_free[s], 1)
                V.tensor_tensor(st[:, 2, 0:32], st[:, 3, 0:32], st[:, 1, 0:32], ALU.subtract).then_inc(acs_ready, 1)
                V.tensor_tensor(xd[:], xtok[:, c, :].rearrange("p (h d) -> p h d", h=32), bc(dts[:, 0, c, :], 2, HD), ALU.mult)\
                    .then_inc(xd_ready, 1)
                V.drain()
                V.wait_ge(e_ready, 5 * c + 1)
                V.tensor_tensor(xe[:], xd[:], bc(st[:, 5, 0:32], 2, HD), ALU.mult).then_inc(xe_ready, 1)
                turns.skip(2)
                for g in range(4):
                    V.wait_ge(e_ready, 5 * c + 2 + g)
                    m = decay[:, 8 * g:8 * g + 8, :]
                    V.tensor_tensor(m, m, bc(cb[:, g, :], 1, 8), ALU.mult).then_inc(m_ready, 1)
                y = xtok[:, c, :].rearrange("p (h d) -> p h d", h=32)
                V.tensor_tensor(y, y, bc(d_skip[:], 2, HD), ALU.mult)
                V.drain()
                s = turns.see()
                V.tensor_tensor(xtok[:, c, :], xtok[:, c, :], ps[s][:].rearrange("p g n -> p (g n)"), ALU.add)
                V.drain().then_inc(turn_free[s], 1)
                if c > 0:
                    s = turns.see()
                    V.tensor_tensor(yoff[:], ps[s][:].rearrange("p g (h d) -> p (g h) d", d=HD), bc(st[:, 4, 0:32], 2, HD), ALU.mult)
                    V.drain().then_inc(turn_free[s], 1)
                    V.tensor_tensor(y, y, yoff[:], ALU.add)
                if c < TT - 1:
                    s = turns.see()
                    if c > 0:
                        sh = state[:].rearrange("p (h d) -> p h d", h=32)
                        V.tensor_tensor(sh, sh, bc(st[:, 6, 0:32], 2, HD), ALU.mult)
                        V.drain()
                        V.tensor_tensor(state[:], state[:], ps[s][:].rearrange("p g n -> p (g n)"), ALU.add).then_inc(st_ready, 1)
                    else:
                        V.tensor_copy(state[:], ps[s][:].rearrange("p g n -> p (g n)")).then_inc(st_ready, 1)
                    V.drain().then_inc(turn_free[s], 1)
            turns.skip(2)
            V.drain()
            for g in range(4):
                turns.skip()
                V.wait_ge(sz_ready, g + 1)
                yg = xtok[:, :, 512 * g:512 * (g + 1)]
                V.tensor_tensor(yg, yg, sz[:], ALU.mult).then_inc(gated, 1)
            V.wait_ge(rms_ready, 9)
            V.reciprocal(st[:, 2, 32:48], st[:, 1, 32:48])
            V.drain()
            for g in range(4):
                for t in range(TT):
                    yg = xtok[:, t, 512 * g:512 * (g + 1)]
                    last = V.tensor_scalar(yg, yg, st[:, 2, 32 + 4 * g + t:33 + 4 * g + t], None, ALU.mult)
                if g % 2:
                    last.then_inc(y_rows, 1)
            for r in range(2):
                low_parts("ssd", first=KC * r)
                for c in range(2):
                    s = turns.see()
                    V.wait_ge(sgb_ready, 2)
                    V.scalar_tensor_tensor(sz[:], sgb[:, 4 * c:4 * c + 4], 1.0, ps[s][:], ALU.add, ALU.mult)
                    V.drain().then_inc(turn_free[s], 1)
                    last = V.tensor_tensor(mT[:, 4 * c:4 * c + 4], mT[:, 4 * c:4 * c + 4], sz[:], ALU.add)
                    if r == 1 and c == 1:
                        last.then_inc(mT_ready, 1)
                    V.drain()
            for c0 in (0, 4):
                his[0] += 4
                V.wait_ge(hi_ready, his[0])
                V.scalar_tensor_tensor(lo[:, c0:c0 + 4], mT[:, c0:c0 + 4], 0.5, hi[:, c0:c0 + 4].bitcast(F32),
                                       ALU.mult, ALU.subtract).then_inc(lo_ready, 1)
            V.wait_ge(x1_back, 16)
            for c in range(2):
                s = turns.see()
                V.tensor_tensor(xres[:, :, 512 * c:512 * (c + 1)], xres[:, :, 512 * c:512 * (c + 1)], ps[s][:], ALU.add)
                V.drain().then_inc(turn_free[s], 1)
            V.drain().then_inc(x2_ready, 1)

            unit_rows(lambda t: xn[:, t, :], lambda t: xres[:, t, :], TT, 10, 16).then_inc(rows_ready, 1)
            low_parts("ffn")
            s = turns.see()
            logits = rt[:, 0]
            V.tensor_tensor(logits, ps[s][:, :, 0:36], bc(b_rt[:], 1, TT), ALU.add)
            V.drain().then_inc(turn_free[s], 1)

            def first_max(hot, x, m, key, n):
                V.tensor_tensor(hot, x, bc(m, 2, n), ALU.is_equal)
                V.drain()
                V.tensor_tensor(hot, hot, bc(order[:, 0:n], 1, TT), ALU.mult)
                V.drain()
                V.tensor_reduce(key, hot, AX.X, ALU.max)
                V.drain()
                V.tensor_tensor(hot, hot, bc(key, 2, n), ALU.is_equal)
                V.drain()

            gl, ge, ghot = rt[:, 0, :, 0:4], rt[:, 1, :, 0:4], rt[:, 2, :, 0:4]
            gm, gs, m1, m2, key, p1, p2 = (rt[:, 3, :, i] for i in range(7))
            e_in, hot1, hot2 = rt[:, 4, :, 0:8], rt[:, 5, :, 0:8], rt[:, 6, :, 0:8]
            V.tensor_reduce(gm, gl, AX.X, ALU.max)
            V.drain()
            V.tensor_tensor(ge, gl, bc(gm, 2, 4), ALU.subtract).then_inc(rt_step, 1)
            V.wait_ge(rt_act, 1)
            V.tensor_reduce(gs, ge, AX.X, ALU.add)
            V.drain()
            first_max(ghot, gl, gm, key, 4)
            per_group = rt[:, 7, :, 0:32].rearrange("p t (g e) -> p t g e", g=4)
            V.tensor_tensor(per_group, rt[:, 0, :, 4:36].rearrange("p t (g e) -> p t g e", g=4), bc(ghot, 3, 8), ALU.mult)
            V.drain()
            V.tensor_reduce(e_in, per_group.rearrange("p t g e -> p t e g"), AX.X, ALU.add)
            V.drain()
            V.tensor_reduce(m1, e_in, AX.X, ALU.max)
            V.drain()
            first_max(hot1, e_in, m1, key, 8)
            rest = rt[:, 9, :, 0:8]
            V.tensor_scalar(rest, hot1, NEG, None, ALU.mult)
            V.drain()
            V.tensor_tensor(rest, rest, e_in, ALU.add)
            V.drain()
            V.tensor_reduce(m2, rest, AX.X, ALU.max)
            V.drain()
            first_max(hot2, rest, m2, key, 8)
            V.tensor_tensor(rt[:, 8, :, 0], m2, m1, ALU.subtract).then_inc(rt_step, 1)
            V.wait_ge(rt_act, 2)
            V.tensor_scalar(p1, rt[:, 8, :, 0], 1.0, None, ALU.add)
            V.drain()
            V.tensor_tensor(p1, p1, gs, ALU.mult)
            V.drain()
            V.reciprocal(p1, p1)
            V.drain()
            V.tensor_tensor(p2, p1, rt[:, 8, :, 0], ALU.mult)
            V.drain()
            V.tensor_tensor(hot1, hot1, bc(p1, 2, 8), ALU.mult)
            V.tensor_tensor(hot2, hot2, bc(p2, 2, 8), ALU.mult)
            V.drain()
            V.tensor_tensor(hot1, hot1, hot2, ALU.add)
            V.drain()
            for t in range(TT):
                V.tensor_tensor(comb[:, t, :].rearrange("p (g e) -> p g e", g=4), bc(ghot[:, t, :], 2, 8), bc(hot1[:, t, :], 1, 4), ALU.mult)
            V.drain()
            V.tensor_copy(comb_e[:], comb[:].rearrange("p t e -> p e t"))
            V.drain().then_inc(act_ready, 1)
            with turns.loop(N_EXP // 2, 6) as i:
                for j in range(2):
                    V.tensor_copy(cw[:, j, :], comb_e[:, bass.ds(2 * i + j, 1), :].rearrange("p e t -> p (e t)"))
                    s = turns.see()
                    V.wait_ge(sa_ready, 2 * i + (j + 1))
                    V.tensor_tensor(act[:], sa[:], ps[s][:, 2:4, :], ALU.mult).then_inc(act_ready, 1)
                    V.drain().then_inc(turn_free[s], 1)
                    V.wait_ge(acth_ready, 2 * i + (j + 1))
                    V.tensor_tensor(act_lo[j][:], act[:], act_hi[j][:].bitcast(F32), ALU.subtract).then_inc(actl_ready, 1)
                    for c in range(2):
                        s = turns.see()
                        for t in range(TT):
                            o = xres[:, t, 512 * c:512 * (c + 1)]
                            V.scalar_tensor_tensor(o, ps[s][:, t, :], cw[:, j, t:t + 1], o, ALU.mult, ALU.add)
                        V.drain().then_inc(turn_free[s], 1)
            V.drain().then_inc(x2_ready, 1)



def kernel(**inputs):
    import concourse.bacc as bacc
    from concourse.bass_utils import run_bass_kernel_spmd

    nc = bacc.Bacc("TRN2", target_bir_lowering=False, num_devices=1)
    arrays = {n: np.ascontiguousarray(a) for n, a in inputs.items()}
    arrays.update(consts())
    d = {n: nc.dram_tensor(n, a.shape, mybir.dt.from_np(a.dtype), kind="ExternalInput").ap() for n, a in arrays.items()}
    out = nc.dram_tensor("out", [1, S, D], F32, kind="ExternalOutput").ap()
    program(nc, d, out)
    return run_bass_kernel_spmd(nc, [arrays], core_ids=[0]).results[0]["out"]
```

```python
from contextlib import ExitStack, contextmanager

import numpy as np

import concourse.bass as bass
from concourse import mybir

F32 = mybir.dt.float32
F32R = mybir.dt.float32r
ALU = mybir.AluOpType
ACT = mybir.ActivationFunctionType
AX = mybir.AxisListType

P = 128
S = 512
D = 1024
TT = S // P
KC = D // P
HALF = KC // 2
EPS = 1e-6
NEG = -1e30
MEM = 256
HD = 64

A_U, A_V, SQKV, MQ, Z1 = 0, 512, 1024, 1536, 1792
Q2, KV2, IQ2, IK2, Z2, XBC2, DT2, GA2, GB2 = 0, 1024, 1536, 2048, 2120, 4168, 7240, 7272, 8296
SMALL = 104
TOPK = 128
ARENA = 198
N_EXP = 32
HID = 256
SLOTS = (2 * S - N_EXP) // P + N_EXP

ROWS_A = {"pre": 0, "mem": 8, "attn": 16, "ffn": 24, "ssd": 32, "conv_b": 48}
N_ROWS_A, N_ROWS_B = 72, 96


class Turns:

    def __init__(self, eng, full, free):
        self.eng, self.full, self.free = eng, full, free
        self.k, self.off, self.half = 0, 0, 0

    def take(self):
        s = self.k % 2
        if self.k >= 2:
            self.eng.wait_ge(self.free[s], self.half + self.k // 2)
        self.k += 1
        return s

    def see(self):
        s = self.k % 2
        self.k += 1
        self.eng.wait_ge(self.full, self.off + self.k)
        return s

    def skip(self, n=1):
        self.k += n

    @contextmanager
    def loop(self, count, per):
        first = self.k
        with self.eng.Fori(0, count) as i:
            self.off, self.half = i * per, i * (per // 2)
            yield i
        assert self.k == first + per and per % 2 == 0
        self.off = self.half = 0
        self.k = first + per * count


def consts():
    k = np.arange(P)
    c = {"c_ident": np.eye(P), "c_tri": (k[:, None] <= k[None, :]), "c_flip": np.eye(P)[::-1]}
    dist = 255 - np.arange(384)
    ok = (dist >= 0) & (dist < 128)
    n = np.maximum(dist, 0)
    large = 16 + (np.log(np.maximum(n, 1) / 16) / np.log(128 / 16) * 16).astype(np.int32)
    bucket = np.where(n < 16, n, np.minimum(large, 31))
    c["c_bucket"] = (bucket[None, :] == np.arange(32)[:, None]) & ok[None, :]
    c["c_outside"] = np.broadcast_to(np.where(ok, 0.0, NEG), (4, 384))
    inv = np.float32(500000.0) ** (-np.arange(8, dtype=np.float32) * np.float32(2.0) / np.float32(16))
    ang = (np.arange(S, dtype=np.float32)[:, None] * inv[None, :].astype(np.float32)).astype(np.float32)
    c["c_cos"] = np.cos(ang)
    c["c_sin"] = np.sin(ang)
    c["c_iota"] = np.broadcast_to(k, (P, P))
    c["c_token"] = k[:, None] + P * np.arange(TT)[None, :]
    c["c_order"] = np.broadcast_to(np.arange(8, 0, -1), (P, 8))
    return {n: np.ascontiguousarray(a, dtype=np.float32) for n, a in c.items()}


def bc(ap, axis, n):
    a = ap.unsqueeze(axis)
    shape = list(a.shape)
    shape[axis] = n
    return a.broadcast_to(shape)



def matmul3(pe, out, x, w, first, last):
    pe.matmul(out, x[0], w[0], start=first, stop=False)
    pe.matmul(out, x[1], w[0], start=False, stop=False)
    return pe.matmul(out, x[0], w[1], start=False, stop=last)


def slot_steps(eng, step):
    rounds = (SLOTS - 1) // 3
    step(0, 0)
    with eng.Fori(0, rounds) as i:
        for j in (1, 2, 3):
            step(3 * i + j, j % 3)
    for s in range(3 * rounds + 1, SLOTS):
        step(s, s % 3)


def program(nc, d, out):
    w1, w2 = d["w_in"][0], d["w_in_2"][0]
    x1_dram = nc.dram_tensor("x1_scratch", [S, D], F32, kind="Internal").ap()
    bias_dram = nc.dram_tensor("bias_scratch", [4, 384], F32, kind="Internal").ap()
    rows_dram = nc.dram_tensor("rows_scratch", [S, D], F32, kind="Internal").ap()
    y_dram = nc.dram_tensor("y_scratch", [SLOTS * P, D], F32, kind="Internal").ap()
    e_gate, e_up, e_down = (d[n][0].rearrange("g e k n -> (g e) k n") for n in ("w_gate_2", "w_up_2", "w_down_2"))

    with ExitStack() as ctx:
        def sb(name, shape, dt=F32):
            return ctx.enter_context(nc.sbuf_tensor(name, shape, dt))

        def sem(name):
            return ctx.enter_context(nc.semaphore(name))

        ident, tri, flip, ones = (sb(n, [P, P]) for n in ("ident", "tri", "flip", "ones"))
        cols = sb("cols", [P, N_ROWS_A + N_ROWS_B])
        cos, sin = sb("cos", [P, TT, 8]), sb("sin", [P, TT, 8])
        unit = sb("unit", [P, 1])
        order = sb("order", [P, 8])
        iota, token = sb("iota", [P, P]), sb("token", [P, TT])
        ffn_kp = sb("ffn_kp", [P, KC])
        sinks = sb("sinks", [P, 4])
        q_g, k_g, ik_g = sb("q_g", [P, HD]), sb("k_g", [P, HD]), sb("ik_g", [P, HD])
        dt_b, a_log, d_skip = sb("dt_b", [P, 32]), sb("a_log", [P, 32]), sb("d_skip", [P, 32])
        b_rt = sb("b_rt", [P, 36])
        w_rt = sb("w_rt", [P, KC, 36])
        st = sb("st", [P, 10, 64])
        top = sb("top", [P, 2, 8])
        sm = sb("sm", [P, 6, 4, 4])
        ps = [ctx.enter_context(nc.psum_tensor(f"ps{i}", [P, 4, 512], F32)) for i in range(2)]

        base = -(-nc.sbuf_base // 64) * 64
        assert base + ARENA * 1024 <= nc.sbuf_top, (base, nc.sbuf_top)

        def at(name, kib, shape, dt=F32):
            size = int(np.prod(shape[1:])) * 4
            assert kib * 1024 + size <= ARENA * 1024, name
            return nc.alloc_sbuf_tensor_at(name, shape, dt, offset=base + int(kib * 1024))

        xres = at("xres", 0, [P, TT, D])
        hi = at("hi", 118, [P, KC, S], F32R)
        lo = at("lo", 134, [P, KC, S], F32R)
        stage = at("stage", 150, [P, 2, HALF, 512])
        w_hi, w_lo = at("w_hi", 166, [P, 2, HALF, 512], F32R), at("w_lo", 182, [P, 2, HALF, 512], F32R)
        xn = at("xn", 16, [P, TT, D])
        pr1, pT1 = at("pr1", 16, [P, 2, 4, 256]), at("pT1", 24, [P, 4, 256])
        vtmp = at("vtmp", 16, [P, TT, 512])
        yT = at("yT", 32, [P, KC, S])
        relb, bucket = at("relb", 32, [32, 4]), at("bucket", 33, [32, 384])
        outside, brow = at("outside", 35, [4, 384]), at("brow", 37, [4, 384])
        rows_a, rows_b = at("rows_a", 40, [N_ROWS_A, P]), at("rows_b", 41, [N_ROWS_B, P])
        uT, vt = at("uT", 48, [P, 4, S]), at("vt", 56, [P, TT, 512])
        zT = at("zT", 64, [P, KC, S])
        memb = at("memb", 64, [P, 2, D])
        qT1, mqT = at("qT1", 80, [P, 2, S]), at("mqT", 84, [P, 2, S])
        kT1, sv1 = at("kT1", 88, [P, S]), at("sv1", 90, [P, TT, P])
        mkT, mv = at("mkT", 92, [P, 2, MEM]), at("mv", 94, [P, 2, MEM])
        v_g, v_b, b_s = at("v_g", 96, [P, 512]), at("v_b", 98, [P, 512]), at("b_s", 100, [P, 4, P])
        post_g = at("post_g", 102, [P, D])
        wsp, wspT = at("wsp", 106, [P, 4, P]), at("wspT", 108, [P, 4, P])
        bias, bias_r = at("bias", 106, [P, 4, 256]), at("bias_r", 110, [P, 4, 256])
        yt1 = at("yt1", 114, [P, 2, 256])
        junk1 = at("junk1", 116, [P, 512])
        sg = at("sg", 0, [P, KC, S])
        qt = at("qt", 16, [P, TT, 1024])
        yah = at("yah", 16, [P, KC, S], F32R)
        iqt, iqT = at("iqt", 32, [P, TT, 512]), at("iqT", 40, [P, 4, S])
        yal = at("yal", 32, [P, KC, S], F32R)
        kvt, kT2 = at("kvt", 48, [P, TT, 512]), at("kT2", 56, [P, 2, S])
        qT2, sel = at("qT2", 60, [P, 8, S]), at("sel", 76, [P, TT, S])
        yt2, rot = at("yt2", 84, [P, 2, 256]), at("rot", 86, [P, 2, TT, 128])
        ikt = at("ikt", 90, [P, TT, P])
        pT2, pr2 = at("pT2", 92, [P, 4, 512]), at("pr2", 100, [P, 2, 4, 512])
        dtt = at("dtt", 0, [P, 8, TT, 32])
        sqr, rel = at("sqr", 92, [P, 2, 1024]), at("rel", 100, [P, 4, 512])
        score, ikT = at("score", 108, [P, 3, 512]), at("ikT", 114, [P, S])
        smt = at("smt", 116, [P, TT, SMALL])
        mT = at("mT", 100, [P, KC, S])
        xd, xe = at("xd", 0, [P, 32, HD]), at("xe", 8, [P, 32, HD])
        yoff = at("yoff", 0, [P, 32, HD])
        xtok = at("xtok", 16, [P, TT, 2048])
        bT, cT, btok = at("bT", 48, [P, 4, S]), at("cT", 56, [P, 4, S]), at("btok", 64, [P, TT, 512])
        cpad, xsT = at("cpad", 72, [P, 4, 3 + S]), at("xsT", 80.125, [P, 4, S])
        decay = at("decay", 72, [P, 32, P])
        state = at("state", 88.25, [P, 2048])
        cb = at("cb", 96.25, [P, 4, P])
        dts = at("dts", 98.25, [P, 3, TT, 32])
        sgb, sz = at("sgb", 48, [P, KC, S]), at("sz", 64, [P, TT, 512])
        junk3 = at("junk3", 72, [P, 1024])
        ssm = st
        hT = at("hT", 118, [P, KC, S])
        rt = at("rt", 34, [P, 16, TT, 36])
        hot = at("hot", 44, [P, 2, TT, N_EXP])
        cnt = at("cnt", 32, [P, 8, 32])
        pos = at("pos", 33, [P, 4, 2 * TT])
        pos_u = nc.alloc_sbuf_tensor_at("pos_u", [P, 2 * TT], mybir.dt.uint32, offset=base + 33 * 1024 + 128)
        tab_u = nc.alloc_sbuf_tensor_at("tab_u", [P, SLOTS], mybir.dt.uint32, offset=base + 33 * 1024 + 256)
        slot_e = nc.alloc_sbuf_tensor_at("slot_e", [1, SLOTS], mybir.dt.int32, offset=base + 33 * 1024 + 512)
        slot_f = at("slot_f", 45, [1, SLOTS])
        hot_r, hot_b = at("hot_r", 134, [P, 2 * TT, P]), at("hot_b", 138, [P, 2 * TT, SLOTS])
        ends = at("ends", 140, [1, SLOTS, N_EXP])
        w_gu = [at(f"w_gu{i}", 46 + 24 * i, [P, 2, KC, HID]) for i in range(3)]
        w_dn = [at(f"w_dn{i}", 62 + 24 * i, [P, 2, D]) for i in range(3)]
        xg = [at(f"xg{i}", 134 + 4 * i, [P, D]) for i in range(3)]
        xT = at("xT", 146, [P, KC, P])
        yg = [at(f"yg{i}", 150 + 4 * i, [P, D]) for i in range(3)]
        sa, act, actT = at("sa", 162, [P, HID]), at("act", 163, [P, HID]), at("actT", 164, [P, 2, P])
        back = at("back", 46, [P, 2 * TT, D])

        def gain(name, k):
            return cols[:, ROWS_A[name] + k:ROWS_A[name] + k + 1]

        x_in, mem_in, par_in = sem("x_in"), sem("mem_in"), sem("par_in")
        w_in_sem = [sem("w_even_in"), sem("w_odd_in")]
        w_split = sem("w_split")
        w_used = sem("w_used")
        turn_full = sem("turn_full")
        turn_free = [sem("turn_free0"), sem("turn_free1")]
        cols_ready, setup_done = sem("cols_ready"), sem("setup_done")
        ss_ready, rms_ready, rows_ready = sem("ss_ready"), sem("rms_ready"), sem("rows_ready")
        hi_ready, lo_ready = sem("hi_ready"), sem("lo_ready")
        brow_ready, bias_out, bias_in = sem("brow_ready"), sem("bias_out"), sem("bias_in")
        wspT_ready, u_ready, v_ready, v_normed = sem("wspT_ready"), sem("u_ready"), sem("v_ready"), sem("v_normed")
        qkv1_ready, mkv_ready, z1_ready = sem("qkv1_ready"), sem("mkv_ready"), sem("z1_ready")
        max_ready, exp_ready, sink_ready = sem("max_ready"), sem("exp_ready"), sem("sink_ready")
        pT_ready, yt_ready, yT_ready = sem("pT_ready"), sem("yt_ready"), sem("yT_ready")
        wo_ready, x1_ready, x1_saved, x1_back = sem("wo_ready"), sem("x1_ready"), sem("x1_saved"), sem("x1_back")
        iq_ready, small_ready, kv_ready, q_ready = sem("iq_ready"), sem("small_ready"), sem("kv_ready"), sem("q_ready")
        iq_rows, k_rows, q_rows = sem("iq_rows"), sem("k_rows"), sem("q_rows")
        iqT_ready, kT_ready, qT_ready, rel_ready = sem("iqT_ready"), sem("kT_ready"), sem("qT_ready"), sem("rel_ready")
        sq_ready, rel_used, sel_ready, sga_ready = sem("sq_ready"), sem("rel_used"), sem("sel_ready"), sem("sga_ready")
        conv_in, conv_out, xs_ready, xtok_ready = sem("conv_in"), sem("conv_out"), sem("xs_ready"), sem("xtok_ready")
        dt_step, dt_act = sem("dt_step"), sem("dt_act")
        acs_ready, e_ready, m_ready = sem("acs_ready"), sem("e_ready"), sem("m_ready")
        xd_ready, xe_ready, st_ready = sem("xd_ready"), sem("xe_ready"), sem("st_ready")
        sgb_ready, sz_ready, gated, y_rows = sem("sgb_ready"), sem("sz_ready"), sem("gated"), sem("y_rows")
        rt_step, rt_act = sem("rt_step"), sem("rt_act")
        rows_saved, slots_ready, table_ready = sem("rows_saved"), sem("slots_ready"), sem("table_ready")
        gu_in, dn_in, xg_in, y_out = ([sem(f"{n}{i}") for i in range(3)] for n in ("gu_in", "dn_in", "xg_in", "y_out"))
        turned, xT_ready, gu_done, sa_ready, act_ready = (sem(n) for n in ("turned", "xT_ready", "gu_done", "sa_ready", "act_ready"))
        act_turned, actT_ready, dn_done, y_ready = (sem(n) for n in ("act_turned", "actT_ready", "dn_done", "y_ready"))
        back_in = [sem(f"back_in{t}") for t in range(TT)]
        out_ready = sem("out_ready")
        x2_ready, out_done = sem("x2_ready"), sem("out_done")
        mT_ready = sem("mT_ready")
        yal_ready = sem("yal_ready")

        JOBS = 36
        TILES = 2 * JOBS
        PARAMS = 0

        block = ctx.enter_context(nc.Block())

        params = [
            (ident[:], d["c_ident"]), (tri[:], d["c_tri"]), (flip[:], d["c_flip"]), (bucket[:], d["c_bucket"]), (outside[:], d["c_outside"]),
            (cos[:], d["c_cos"].rearrange("(t p) f -> p t f", p=P)), (sin[:], d["c_sin"].rearrange("(t p) f -> p t f", p=P)),
            (order[:], d["c_order"]), (iota[:], d["c_iota"]), (token[:], d["c_token"]),
            (ffn_kp[:], d["ffn_norm_2"][0].rearrange("(p k) -> p k", p=P)), (relb[:], d["rel_bias"]),
            (rows_b[:], d["conv_w_2"][0].rearrange("k (c p) -> (k c) p", p=P)),
            (wsp[:], d["w_spatial"][0].rearrange("g t s -> t g s")),
            (w_rt[:, :, 0:4], d["w_route_group_2"][0].rearrange("(k p) n -> p k n", p=P)),
            (w_rt[:, :, 4:36], d["w_route_expert_2"][0].rearrange("(k p) n -> p k n", p=P)),
        ]
        for name, key in (("pre", "pre_norm_g"), ("mem", "mem_norm_g"), ("attn", "attn_norm_2"), ("ffn", "ffn_norm_2"),
                          ("ssd", "ssd_norm_2"), ("conv_b", "conv_b_2")):
            v = d[key][0].rearrange("(c p) -> c p", p=P)
            params.append((rows_a[ROWS_A[name]:ROWS_A[name] + v.shape[0], :], v))
        for dst, v in ((v_g[:], d["v_norm_g"][0]), (v_b[:], d["v_norm_b"][0]), (post_g[:], d["post_norm_g"][0]),
                       (b_s[:], d["b_spatial"][0].rearrange("g t -> (g t)")),
                       (sinks[:], d["attn_sinks"][0]), (q_g[:], d["q_norm_2"][0]), (k_g[:], d["k_norm_2"][0]),
                       (ik_g[:], d["idx_k_norm_2"][0]), (dt_b[:], d["dt_bias_2"][0]), (a_log[:], d["a_log_2"][0]),
                       (d_skip[:], d["d_skip_2"][0]), (b_rt[:, 0:4], d["b_route_group_2"][0]),
                       (b_rt[:, 4:36], d["b_route_expert_2"][0])):
            src = v.partition_broadcast(P)
            if len(dst.shape) == 3:
                dst = dst.rearrange("p g t -> p (g t)")
            params.append((dst, src))
        PARAMS = 16 * len(params)

        @block.sync
        def _(sp):
            tiles = [0]

            def tile(parts):
                n = tiles[0]
                if n >= 2:
                    sp.wait_ge(w_split, n - 1)
                for dst, src in parts(stage[:, n % 2]):
                    sp.dma_start(dst, src).then_inc(w_in_sem[n % 2], 16)
                tiles[0] += 1

            def halves(w, r0, c0, ncols=512):
                for h in range(2):
                    src = w[r0 + 512 * h:r0 + 512 * (h + 1), c0:c0 + ncols].rearrange("(k p) n -> p k n", p=P)
                    tile(lambda t, src=src: [(t[:, a:a + 2, 0:ncols], src[:, a:a + 2, :]) for a in (0, 2)])

            sp.dma_start(memb[:], d["mem"][0].rearrange("(t p) n -> p t n", p=P)).then_inc(mem_in, 16)
            halves(d["w_mem_kv"][0], 0, 0)
            sp.dma_start(xres[:], d["x"][0].rearrange("(t p) n -> p t n", p=P)).then_inc(x_in, 16)
            for c0, n in ((SQKV, 512), (A_V, 512), (A_U, 512), (MQ, 256), (Z1, 512), (Z1 + 512, 512)):
                halves(w1, 0, c0, n)
            sp.wait_ge(brow_ready, 1)
            sp.dma_start(bias_dram, brow[:]).then_inc(bias_out, 16)
            sp.wait_ge(bias_out, 16)
            for h in range(4):
                shifted = bass.AP(bias_dram.tensor, h * 384, [[1, P], [1, 256]])
                sp.dma_start(bias_r[:, h, :], shifted).then_inc(bias_in, 16)
            for c in range(2):
                halves(d["w_out"][0], 0, 512 * c)
            halves(w2, 0, IQ2)
            for h in range(2):
                rows = slice(512 * h, 512 * (h + 1))
                a = w2[rows, IK2:IK2 + 72].rearrange("(k p) n -> p k n", p=P)
                b = w2[rows, DT2:DT2 + 32].rearrange("(k p) n -> p k n", p=P)
                tile(lambda t, a=a, b=b: [(t[:, :, 0:72], a), (t[:, :, 72:SMALL], b)])
            for c0 in (KV2, Q2, Q2 + 512, GA2, GA2 + 512):
                halves(w2, 0, c0)
                if c0 == KV2:
                    sp.wait_ge(x1_ready, 1)
                    sp.dma_start(x1_dram.rearrange("(t p) n -> p t n", p=P), xres[:]).then_inc(x1_saved, 16)
            for c in range(2):
                halves(d["w_attn_branch_2"][0], 0, 512 * c)
            for c0 in (XBC2 + 2048, XBC2 + 2560, XBC2, XBC2 + 512, XBC2 + 1024, XBC2 + 1536, GB2, GB2 + 512):
                halves(w2, 0, c0)
            for g in range(4):
                halves(w2, 0, Z2 + 512 * g)
            sp.wait_ge(x1_saved, 16)
            sp.wait_ge(gated, 1)
            sp.dma_start(xres[:], x1_dram.rearrange("(t p) n -> p t n", p=P)).then_inc(x1_back, 16)
            for r in range(2):
                for c in range(2):
                    halves(d["w_ssd_branch_2"][0], 1024 * r, 512 * c)
            for c in range(2):
                halves(d["w_out_2"][0], 0, 512 * c)
            assert tiles[0] == 2 * JOBS

            sp.wait_ge(rows_ready, 4)
            sp.dma_start(rows_dram.rearrange("(t p) n -> p t n", p=P), xn[:]).then_inc(rows_saved, 16)

            def gate_up(e, b):
                for c, w in ((0, e_gate), (1, e_up)):
                    sp.dma_start(w_gu[b][:, c], w[bass.ds(e, 1)].rearrange("e (p k) n -> p (e k) n", p=P)).then_inc(gu_in[b], 16)

            def down(e, b):
                sp.dma_start(w_dn[b][:], e_down[bass.ds(e, 1)].rearrange("e (f p) n -> p (e f) n", p=P)).then_inc(dn_in[b], 16)

            def expert(s):
                return nc.sync.value_load(slot_e[0:1, bass.ds(s, 1)], min_val=0, max_val=N_EXP - 1)

            def store(s, b):
                sp.dma_start(y_dram[bass.ds(s * P, P), :], yg[b][:]).then_inc(y_out[b], 16)

            sp.wait_ge(slots_ready, 1)
            for s in range(3):
                e = expert(s)
                gate_up(e, s)
                down(e, s)
            rounds = SLOTS // 3 - 1
            with sp.Fori(0, rounds) as i:
                for b in range(3):
                    s = 3 * i + b
                    e = expert(s + 3)
                    sp.wait_ge(gu_done, s + 1)
                    gate_up(e, b)
                    sp.wait_ge(dn_done, s + 1)
                    down(e, b)
                    sp.wait_ge(y_ready, s + 1)
                    store(s, b)
            for s in range(3 * rounds, SLOTS):
                sp.wait_ge(y_ready, s + 1)
                store(s, s % 3)
            for t in range(TT):
                sp.wait_ge(out_ready, t + 1)
                sp.dma_start(out[0, P * t:P * (t + 1), :], xres[:, t, :]).then_inc(out_done, 16)
            sp.wait_ge(out_done, 16 * TT)

        @block.gpsimd
        def _(pool):
            def split(b):
                nc.gpsimd.tensor_tensor(w_hi[:, b], stage[:, b], unit[:].unsqueeze(1).broadcast_to([P, HALF, 512]), ALU.mult)
                pool.drain()
                nc.gpsimd.tensor_tensor(w_lo[:, b], stage[:, b], w_hi[:, b].bitcast(F32), ALU.subtract).then_inc(w_split, 1)

            nc.gpsimd.memset(unit[:], 1.0)
            pool.drain()
            for b in range(2):
                pool.wait_ge(w_in_sem[b], 32)
                split(b)
            with pool.Fori(1, TILES // 2) as i:
                for b in range(2):
                    pool.wait_ge(w_in_sem[b], 32 * i + 32)
                    pool.wait_ge(w_used, 2 * i + (b - 1))
                    split(b)

            pool.wait_ge(rows_saved, 16)
            pool.wait_ge(table_ready, 1)
            for s in range(SLOTS):
                if s >= 3:
                    pool.wait_ge(turned, s - 2)
                nc.gpsimd.indirect_dma_start(xg[s % 3][:], None, rows_dram, bass.IndirectOffsetOnAxis(ap=tab_u[:, s:s + 1], axis=0))\
                    .then_inc(xg_in[s % 3], 16)
            for b in range(3):
                pool.wait_ge(y_out[b], 16 * len(range(b, SLOTS, 3)))
            for t in range(TT):
                for k in range(2):
                    i = TT * k + t
                    nc.gpsimd.indirect_dma_start(back[:, i, :], None, y_dram, bass.IndirectOffsetOnAxis(ap=pos_u[:, i:i + 1], axis=0))\
                        .then_inc(back_in[t], 16)

        @block.tensor
        def _(pe):
            turns = Turns(pe, turn_full, turn_free)
            tile = [0, 0]

            def parts(t, *ix):
                return t[0][ix], t[1][ix]

            x_parts, w_parts, ya_parts = (hi, lo), (w_hi, w_lo), (yah, yal)
            everything = slice(None)

            def weights():
                b = tile[0] % 2
                pe.wait_ge(w_split, tile[1] + tile[0] + 1)
                tile[0] += 1
                return b

            def features(x=x_parts, chunks=4, n=S, more=None):
                s = turns.take()
                for half in range(2):
                    b = weights()
                    for m in range(chunks):
                        for k in range(HALF):
                            w = parts(w_parts, everything, b, k)
                            w = tuple(a[:, P * m:P * (m + 1)] for a in w)
                            last = matmul3(pe, ps[s][:, m, 0:n], w, parts(x, everything, HALF * half + k, slice(0, n)),
                                           half == 0 and k == 0, half == 1 and k == HALF - 1)
                    if more:
                        last = more(s, b, half)
                    last.then_inc(w_used, 1)
                pe.drain().then_inc(turn_full, 1)

            def tokens(x=x_parts, n=512, tiles=TT):
                s = turns.take()
                for half in range(2):
                    b = weights()
                    for t in range(tiles):
                        for k in range(HALF):
                            last = matmul3(pe, ps[s][:, t, 0:n],
                                           parts(x, everything, HALF * half + k, slice(P * t, P * (t + 1))),
                                           parts(w_parts, everything, b, k, slice(0, n)),
                                           half == 0 and k == 0, half == 1 and k == HALF - 1)
                    last.then_inc(w_used, 1)
                pe.drain().then_inc(turn_full, 1)

            def turn_rows(rows, tiles=TT, chunks=KC):
                for c0 in range(0, chunks, 4):
                    s = turns.take()
                    for c in range(4):
                        for t in range(tiles):
                            last = pe.transpose(ps[s][:, c, P * t:P * (t + 1)], rows(t, c0 + c), ident[:])
                    last.then_inc(turn_full, 1)

            pe.wait_ge(par_in, PARAMS)
            s = turns.take()
            pe.transpose(ps[s][:, 0, 0:N_ROWS_A], rows_a[:], ident[0:N_ROWS_A, 0:N_ROWS_A])
            pe.transpose(ps[s][:, 0, N_ROWS_A:N_ROWS_A + N_ROWS_B], rows_b[:], ident[0:N_ROWS_B, 0:N_ROWS_B])
            pe.matmul(ps[s][0:4, 1, 0:384], relb[:], bucket[:], start=True, stop=True)
            for g in range(4):
                last = pe.transpose(ps[s][:, 2, P * g:P * (g + 1)], wsp[:, g, :], ident[:])
            last.then_inc(turn_full, 1)

            pe.wait_ge(rows_ready, 1)
            turn_rows(lambda t, c: xn[:, t, P * c:P * (c + 1)], tiles=2)
            pe.wait_ge(lo_ready, 2)

            def mem_values(s, b, half):
                for t in range(2):
                    for k in range(HALF):
                        last = matmul3(pe, ps[s][:, 2 + t, 0:MEM],
                                       parts(x_parts, everything, HALF * half + k, slice(P * t, P * (t + 1))),
                                       parts(w_parts, everything, b, k, slice(256, 512)),
                                       half == 0 and k == 0, half == 1 and k == HALF - 1)
                return last

            features(chunks=2, n=MEM, more=mem_values)

            pe.wait_ge(rows_ready, 2)
            turn_rows(lambda t, c: xn[:, t, P * c:P * (c + 1)])
            pe.wait_ge(lo_ready, 4)

            def swa_values(s, b, half):
                for t in range(TT):
                    for k in range(HALF):
                        last = matmul3(pe, ps[s][:, 3, P * t:P * (t + 1)],
                                       parts(x_parts, everything, HALF * half + k, slice(P * t, P * (t + 1))),
                                       parts(w_parts, everything, b, k, slice(384, 512)),
                                       half == 0 and k == 0 and t == 0, half == 1 and k == HALF - 1 and t == TT - 1)
                return last

            features(chunks=3, more=swa_values)
            tokens()
            features()
            features(chunks=2)
            features()
            features()

            pe.wait_ge(v_normed, 1)
            pe.wait_ge(wspT_ready, 1)
            s = turns.take()
            for g in range(4):
                for n in range(TT):
                    last = pe.matmul(ps[s][:, g, P * n:P * (n + 1)], vt[:, n, P * g:P * (g + 1)], wspT[:, g, :],
                                     start=True, stop=True)
            last.then_inc(turn_full, 1)

            pe.wait_ge(bias_in, 64)
            s = turns.take()
            for h in range(4):
                last = pe.matmul(ps[s][:, h, 0:256], flip[:], bias_r[:, h, :], start=True, stop=True)
            last.then_inc(turn_full, 1)

            def attention(batches, scores, values, nkb, pr, pT, yt, base):
                for i in range(batches + 3):
                    if i < batches:
                        s = turns.take()
                        scores(i, s).then_inc(turn_full, 1)
                    b = i - 2
                    if 0 <= b < batches:
                        s = turns.take()
                        pe.wait_ge(pT_ready, base + b + 1)
                        for h in range(4):
                            for kb in range(nkb(b)):
                                last = pe.matmul(ps[s][:, 0, HD * h:HD * (h + 1)], pT(b)[:, h, P * kb:P * (kb + 1)],
                                                 values(b, h, kb), start=(kb == 0), stop=(kb == nkb(b) - 1))
                        last.then_inc(turn_full, 1)
                    b = i - 1
                    if 0 <= b < batches:
                        s = turns.take()
                        pe.wait_ge(exp_ready, base + b + 1)
                        for h in range(4):
                            for kb in range(nkb(b)):
                                last = pe.transpose(ps[s][:, h, P * kb:P * (kb + 1)],
                                                    pr(b)[:, h, P * kb:P * (kb + 1)], ident[:])
                        last.then_inc(turn_full, 1)
                    b = i - 3
                    if 0 <= b < batches:
                        s = turns.take()
                        pe.wait_ge(yt_ready, base + b + 1)
                        for c in range(2):
                            last = pe.transpose(ps[s][:, 0, P * c:P * (c + 1)], yt[:, b % 2, P * c:P * (c + 1)], ident[:])
                        last.then_inc(turn_full, 1)

            def scores1(b, s):
                n = b % 4
                for h in range(4):
                    if b < 4:
                        lanes = slice(HD * (h // 2), HD * (h // 2 + 1))
                        q, k = qT1[lanes, h % 2, P * n:P * (n + 1)], kT1[lanes, P * max(n - 1, 0):P * (n + 1)]
                    else:
                        lanes = slice(HD * (h % 2), HD * (h % 2 + 1))
                        q, k = mqT[lanes, h // 2, P * n:P * (n + 1)], mkT[lanes, h // 2, :]
                    last = pe.matmul(ps[s][:, h, 0:k.shape[1]], q, k, start=True, stop=True)
                return last

            def values1(b, h, kb):
                if b < 4:
                    return sv1[:, max(b - 1, 0) + kb, HD * (h // 2):HD * (h // 2 + 1)]
                return mv[:, kb, HD * h:HD * (h + 1)]

            pe.wait_ge(qkv1_ready, 2)
            pe.wait_ge(mkv_ready, 1)
            attention(8, scores1, values1, lambda b: 1 if b == 0 else 2, lambda b: pr1[:, b % 2], lambda b: pT1, yt1, 0)

            pe.wait_ge(lo_ready, 6)
            tokens()
            tokens()

            pe.wait_ge(rows_ready, 3)
            turn_rows(lambda t, c: qt[:, t, P * c:P * (c + 1)])
            pe.wait_ge(lo_ready, 8)
            tokens()
            tokens(n=SMALL)
            tokens()
            pe.wait_ge(iq_rows, 1)
            turn_rows(lambda t, c: iqt[:, t, P * c:P * (c + 1)], chunks=4)
            pe.wait_ge(iq_rows, 2)
            s = turns.take()
            for t in range(TT):
                last = pe.transpose(ps[s][:, 0, P * t:P * (t + 1)], ikt[:, t, :], ident[:])
            last.then_inc(turn_full, 1)
            tokens()
            pe.wait_ge(iqT_ready, 2)
            for n in range(1, TT):
                for h4 in range(2):
                    s = turns.take()
                    for h in range(4):
                        i = 4 * h4 + h
                        lanes = slice(HD * (i % 2), HD * (i % 2 + 1))
                        last = pe.matmul(ps[s][:, h, 0:P * (n + 1)], iqT[lanes, i // 2, P * n:P * (n + 1)],
                                         ikT[lanes, 0:P * (n + 1)], start=True, stop=True)
                    last.then_inc(turn_full, 1)
            tokens()
            features()
            features()
            pe.wait_ge(k_rows, 1)
            s = turns.take()
            for c in range(2):
                for t in range(TT):
                    last = pe.transpose(ps[s][:, c, P * t:P * (t + 1)], kvt[:, t, P * c:P * (c + 1)], ident[:])
            last.then_inc(turn_full, 1)
            pe.wait_ge(q_rows, 1)
            turn_rows(lambda t, c: qt[:, t, P * c:P * (c + 1)])

            def scores2(b, s):
                n, g = b // 4, b % 4
                lanes = slice(HD * (g % 2), HD * (g % 2 + 1))
                for i in range(4):
                    last = pe.matmul(ps[s][:, i, 0:P * (n + 1)], qT2[lanes, 4 * (g // 2) + i, P * n:P * (n + 1)],
                                     kT2[lanes, g // 2, 0:P * (n + 1)], start=True, stop=True)
                return last

            pe.wait_ge(kT_ready, 1)
            pe.wait_ge(qT_ready, 2)
            attention(16, scores2, lambda b, h, kb: kvt[:, kb, 256 + HD * (b % 4):256 + HD * (b % 4 + 1)],
                      lambda b: b // 4 + 1, lambda b: pr2[:, b % 2], lambda b: pT2, yt2, 8)
            pe.wait_ge(yal_ready, 16)
            features(ya_parts)
            features(ya_parts)

            def turn_back(n):
                pe.wait_ge(xs_ready, n)
                s = turns.take()
                src = bT if n == 1 else xsT
                for t in range(TT):
                    for c in range(4):
                        last = pe.transpose(ps[s][:, t, P * c:P * (c + 1)], src[:, c, P * t:P * (t + 1)], ident[:])
                last.then_inc(turn_full, 1)

            features()
            features()
            turn_back(1)
            for j in range(4):
                features()
                turn_back(3 + j)

            pe.wait_ge(dt_step, 3)
            for c in range(TT):
                tok = slice(P * c, P * (c + 1))
                s = turns.take()
                pe.matmul(ps[s][:, 0, 0:32], tri[:], dts[:, 1, c, :], start=True, stop=True)
                pe.matmul(ps[s][:, 0, 32:64], ones[:], dts[:, 1, c, :], start=True, stop=True)
                for g in range(4):
                    last = pe.matmul(ps[s][:, 1, P * g:P * (g + 1)], bT[:, g, tok], cT[:, g, tok], start=True, stop=True)
                last.then_inc(turn_full, 1)
                for half in range(2):
                    s = turns.take()
                    for h in range(16):
                        col = dts[:, 1, c, 16 * half + h:16 * half + h + 1].broadcast_to([P, P])
                        last = pe.matmul(ps[s][:, h // 4, P * (h % 4):P * (h % 4 + 1)], col, tri[:], start=True, stop=True)
                    last.then_inc(turn_full, 1)
                pe.wait_ge(m_ready, 4 * (c + 1))
                pe.wait_ge(xd_ready, c + 1)
                s = turns.take()
                for h in range(32):
                    last = pe.matmul(ps[s][:, h // 8, HD * (h % 8):HD * (h % 8 + 1)], decay[:, h, :], xd[:, h, :],
                                     start=True, stop=True)
                last.then_inc(turn_full, 1)
                if c > 0:
                    pe.wait_ge(st_ready, c)
                    s = turns.take()
                    for g in range(4):
                        last = pe.matmul(ps[s][:, g, :], cT[:, g, tok], state[:, 512 * g:512 * (g + 1)], start=True, stop=True)
                    last.then_inc(turn_full, 1)
                if c < TT - 1:
                    pe.wait_ge(xe_ready, c + 1)
                    s = turns.take()
                    for g in range(4):
                        last = pe.matmul(ps[s][:, g, :], btok[:, c, P * g:P * (g + 1)], xe[:, 8 * g:8 * (g + 1), :],
                                         start=True, stop=True)
                    last.then_inc(turn_full, 1)

            features()
            features()
            for g in range(4):
                tokens()
            for r in range(2):
                pe.wait_ge(y_rows, r + 1)
                turn_rows(lambda t, c, r=r: xtok[:, t, 1024 * r + P * c:1024 * r + P * (c + 1)])
                pe.wait_ge(lo_ready, 10 + 2 * r)
                features()
                features()
            pe.wait_ge(lo_ready, 14)
            tokens()
            tokens()

            pe.wait_ge(rows_ready, 4)
            turn_rows(lambda t, c: xn[:, t, P * c:P * (c + 1)])
            pe.wait_ge(hi_ready, 60)
            pe.wait_ge(lo_ready, 15)
            s = turns.take()
            for t in range(TT):
                for k in range(KC):
                    last = pe.matmul(ps[s][:, t, 0:36], hT[:, k, P * t:P * (t + 1)], w_rt[:, k, :],
                                     start=(k == 0), stop=(k == KC - 1))
            last.then_inc(turn_full, 1)
            pe.wait_ge(rt_step, 3)
            s = turns.take()
            for t in range(TT):
                for u in range(t):
                    pe.matmul(ps[s][:, 0, 32 * t:32 * (t + 1)], ones[:], rt[:, 10, u, 0:32], start=(u == 0), stop=False)
                pe.matmul(ps[s][:, 0, 32 * t:32 * (t + 1)], tri[:], rt[:, 10, t, 0:32], start=(t == 0), stop=True)
            for t in range(TT):
                last = pe.matmul(ps[s][:, 1, 0:32], ones[:], rt[:, 10, t, 0:32], start=(t == 0), stop=(t == TT - 1))
            last.then_inc(turn_full, 1)
            pe.wait_ge(rt_step, 4)
            s = turns.take()
            for i in range(2 * TT):
                last = pe.matmul(ps[s][:, 0, 0:SLOTS], hot_r[:, i, :], hot_b[:, i, :], start=(i == 0), stop=(i == 2 * TT - 1))
            last.then_inc(turn_full, 1)

            p_gu, p_act, p_rows, p_dn = ps[0][:, 0, :], ps[0][:, 1, 0:2 * P], ps[0][:, 2:4, :], ps[1][:, 0:2, :]

            def turn_slot(s, b, first=False):

                for k in range(KC):
                    last = pe.transpose(p_rows[:, k // 4, P * (k % 4):P * (k % 4 + 1)], xg[b][:, k:D:KC], ident[:])
                last.then_inc(turned, 1)

            def project(b):
                for k in range(KC):
                    last = pe.matmul(p_gu, xT[:, k, :], w_gu[b][:, :, k, :], start=(k == 0), stop=(k == KC - 1))
                last.then_inc(gu_done, 1)

            def down(s, b):
                pe.wait_ge(actT_ready, s + 1)
                for c in range(2):
                    for f in range(2):
                        last = pe.matmul(p_dn[:, c, :], actT[:, f, :], w_dn[b][:, f, 512 * c:512 * (c + 1)], start=(f == 0), stop=(f == 1))
                last.then_inc(dn_done, 1)

            pe.wait_ge(table_ready, 1)
            pe.wait_ge(xg_in[0], 16)
            turn_slot(0, 0)
            rounds = (SLOTS - 1) // 3

            def step(s, b, arrivals, next_arrivals, first=False, last=False):
                pe.wait_ge(xT_ready, s + 1)
                pe.wait_ge(gu_in[b], 32 * arrivals)
                if not first:
                    pe.wait_ge(act_ready, s)
                project(b)
                if not last:
                    n = (b + 1) % 3
                    pe.wait_ge(xg_in[n], 16 * next_arrivals)
                    turn_slot(s + 1, n)
                if not first:
                    m = (b - 1) % 3
                    pe.wait_ge(dn_in[m], 16 * (arrivals if m < b else arrivals - 1))
                    if not (isinstance(s, int) and s == 1):
                        pe.wait_ge(y_ready, s - 1)
                    down(s - 1, m)
                pe.wait_ge(act_ready, s + 1)
                for f in range(2):
                    t = pe.transpose(p_act[:, P * f:P * (f + 1)], act[:, P * f:P * (f + 1)], ident[:])
                t.then_inc(act_turned, 1)

            step(0, 0, 1, 1, first=True)
            step(1, 1, 1, 1)
            with pe.Fori(0, (SLOTS - 3) // 3) as i:
                for j in (2, 3, 4):
                    step(3 * i + j, j % 3, i + (1 + j // 3), i + (1 + (j + 1) // 3))
            step(SLOTS - 1, (SLOTS - 1) % 3, SLOTS // 3, None, last=True)
            pe.wait_ge(dn_in[(SLOTS - 1) % 3], 16 * (SLOTS // 3))
            pe.wait_ge(y_ready, SLOTS - 1)
            down(SLOTS - 1, (SLOTS - 1) % 3)

        @block.scalar
        def _(act_eng):
            A = act_eng
            turns = Turns(A, turn_full, turn_free)
            for dst, src in params:
                A.dma_start(dst, src).then_inc(par_in, 16)

            def norm(rows, n, junk, k):
                for t in range(n):
                    A.activation(junk, rows(t), ACT.Square, accum_out=st[:, 0, k + t:k + t + 1])
                    A.drain()
                A.drain()
                A.activation(st[:, 1, k:k + n], st[:, 0, k:k + n], ACT.Sqrt, scale=1.0 / D, bias=st[:, 9, 0:1]).then_inc(rms_ready, 1)

            def high_parts(name, first=0, n=S, chunks=KC):
                for c0 in range(0, chunks, 4):
                    s = turns.see()
                    for c in range(4):
                        A.activation(hi[:, c0 + c, 0:n], ps[s][:, c, 0:n], ACT.Copy, scale=gain(name, first + c0 + c))\
                            .then_inc(hi_ready, 1)

            def softmax(b, base, width, src, dst, sinks_too):
                k = b % 4
                A.wait_ge(max_ready, base + b + 1)
                for h in range(4):
                    last = A.activation(dst[:, h, 0:width], src[:, h, 0:width], ACT.Exp, bias=sm[:, 2, k, h:h + 1],
                                        accum_out=sm[:, 1, k, h:h + 1])
                if sinks_too:
                    last = A.activation(sm[:, 4, k, :], sm[:, 3, k, :], ACT.Exp)
                last.then_inc(exp_ready, 1)

            A.wait_ge(setup_done, 1)
            A.wait_ge(mem_in, 16)
            norm(lambda t: memb[:, t, :], 2, yT[:, 6:8, :].rearrange("p c n -> p (c n)"), 0)
            A.wait_ge(cols_ready, 1)
            turns.skip()
            high_parts("mem", n=MEM)
            A.wait_ge(x_in, 16)
            norm(lambda t: xres[:, t, :], TT, yT[:, 6:8, :].rearrange("p c n -> p (c n)"), 4)
            s = turns.see()
            A.activation(mkT[:], ps[s][:, 0:2, 0:MEM], ACT.Copy)
            A.activation(mv[:], ps[s][:, 2:4, 0:MEM], ACT.Copy).then_inc(mkv_ready, 1)
            A.drain().then_inc(turn_free[s], 1)
            high_parts("pre")
            s = turns.see()
            for h in range(4):
                A.activation(qT1[HD * (h // 2):HD * (h // 2 + 1), h % 2, :], ps[s][HD * (h % 2):HD * (h % 2 + 1), h // 2, :],
                             ACT.Copy, scale=HD ** -0.5)
            A.activation(kT1[:], ps[s][:, 2, :], ACT.Copy)
            A.activation(sv1[:], ps[s][:, 3, :].rearrange("p (t n) -> p t n", t=TT), ACT.Copy).then_inc(qkv1_ready, 1)
            A.drain().then_inc(turn_free[s], 1)
            s = turns.see()
            A.activation(vt[:], ps[s][:], ACT.Gelu_apprx_tanh).then_inc(v_ready, 1)
            A.drain().then_inc(turn_free[s], 1)
            A.wait_ge(v_ready, 2)
            A.activation(st[:, 4, 0:16], st[:, 3, 0:16], ACT.Sqrt, scale=1.0 / P, bias=st[:, 9, 0:1]).then_inc(rms_ready, 1)
            s = turns.see()
            A.activation(uT[:], ps[s][:], ACT.Gelu_apprx_tanh).then_inc(u_ready, 1)
            A.drain().then_inc(turn_free[s], 1)
            s = turns.see()
            A.activation(mqT[:], ps[s][:, 0:2, :], ACT.Copy, scale=HD ** -0.5).then_inc(qkv1_ready, 1)
            A.drain().then_inc(turn_free[s], 1)
            for c in range(2):
                s = turns.see()
                A.activation(zT[:, 4 * c:4 * c + 4, :], ps[s][:], ACT.Silu).then_inc(z1_ready, 1)
                A.drain().then_inc(turn_free[s], 1)
            turns.skip(2)

            for i in range(8 + 3):
                if i < 8:
                    width = P if i == 0 else 256
                    if i < 4:
                        turns.skip()
                        softmax(i, 0, width, pr1[:, i % 2], pr1[:, i % 2], True)
                    else:
                        s = turns.see()
                        softmax(i, 0, width, ps[s], pr1[:, i % 2], False)
                        A.drain().then_inc(turn_free[s], 1)
                if 0 <= i - 2 < 8:
                    turns.skip()
                if 0 <= i - 1 < 8:
                    width = P if i == 1 else 256
                    s = turns.see()
                    A.activation(pT1[:, :, 0:width], ps[s][:, :, 0:width], ACT.Copy).then_inc(pT_ready, 1)
                    A.drain().then_inc(turn_free[s], 1)
                b = i - 3
                if b >= 0:
                    s = turns.see()
                    c0, n = (4, b) if b < 4 else (6, b - 4)
                    A.activation(yT[:, c0:c0 + 2, P * n:P * (n + 1)],
                                 ps[s][:, 0, 0:256].rearrange("p (c t) -> p c t", c=2), ACT.Copy).then_inc(yT_ready, 1)
                    A.drain().then_inc(turn_free[s], 1)
            for c0 in (0, 4):
                A.wait_ge(z1_ready, 3 + c0 // 4)
                A.activation(hi[:, c0:c0 + 4, :], yT[:, c0:c0 + 4, :], ACT.Copy).then_inc(hi_ready, 4)
            for c in range(2):
                s = turns.see()
                A.activation(xn[:, :, 512 * c:512 * (c + 1)], ps[s][:], ACT.Copy).then_inc(wo_ready, 1)
                A.drain().then_inc(turn_free[s], 1)
            norm(lambda t: xn[:, t, :], TT, yT[:, 0:2, :].rearrange("p c n -> p (c n)"), 8)

            A.wait_ge(x1_ready, 1)
            norm(lambda t: xres[:, t, :], TT, iqt[:, 0:2, :].rearrange("p c n -> p (c n)"), 12)
            high_parts("attn")
            s = turns.see()
            A.activation(iqt[:], ps[s][:], ACT.Copy).then_inc(iq_ready, 1)
            A.drain().then_inc(turn_free[s], 1)
            s = turns.see()
            A.activation(smt[:], ps[s][:, :, 0:SMALL], ACT.Copy).then_inc(small_ready, 1)
            A.drain().then_inc(turn_free[s], 1)
            A.wait_ge(sq_ready, 1)
            A.activation(st[:, 4, 16:20], st[:, 3, 16:20], ACT.Sqrt, scale=1.0 / HD, bias=st[:, 9, 0:1]).then_inc(rms_ready, 1)
            s = turns.see()
            A.activation(kvt[:], ps[s][:], ACT.Copy).then_inc(kv_ready, 1)
            A.drain().then_inc(turn_free[s], 1)
            s = turns.see()
            A.activation(iqT[:], ps[s][:], ACT.Copy, scale=HD ** -0.5).then_inc(iqT_ready, 1)
            A.drain().then_inc(turn_free[s], 1)
            s = turns.see()
            A.activation(ikT[:], ps[s][:, 0, :], ACT.Copy).then_inc(iqT_ready, 1)
            A.drain().then_inc(turn_free[s], 1)
            A.wait_ge(sq_ready, 2)
            A.activation(st[:, 4, 20:36], st[:, 3, 20:36], ACT.Sqrt, scale=1.0 / HD, bias=st[:, 9, 0:1]).then_inc(rms_ready, 1)
            s = turns.see()
            A.activation(qt[:, :, 0:512], ps[s][:], ACT.Copy).then_inc(q_ready, 1)
            A.drain().then_inc(turn_free[s], 1)
            for i in range(6):
                s = turns.see()
                n = 1 + i // 2
                if i > 0:
                    A.wait_ge(rel_used, i)
                A.activation(rel[:, :, 0:P * (n + 1)], ps[s][:, :, 0:P * (n + 1)], ACT.Relu).then_inc(rel_ready, 1)
                A.drain().then_inc(turn_free[s], 1)
            s = turns.see()
            A.activation(qt[:, :, 512:1024], ps[s][:], ACT.Copy).then_inc(q_ready, 1)
            A.drain().then_inc(turn_free[s], 1)
            A.wait_ge(x1_saved, 16)
            for c in range(2):
                s = turns.see()
                A.activation(sg[:, 4 * c:4 * c + 4, :], ps[s][:], ACT.Tanh, scale=0.5).then_inc(sga_ready, 1)
                A.drain().then_inc(turn_free[s], 1)
            A.wait_ge(sq_ready, 3)
            A.activation(st[:, 7, 0:64], st[:, 6, 0:64], ACT.Sqrt, scale=1.0 / HD, bias=st[:, 9, 0:1]).then_inc(rms_ready, 1)
            s = turns.see()
            A.activation(kT2[:], ps[s][:, 0:2, :], ACT.Copy).then_inc(kT_ready, 1)
            A.drain().then_inc(turn_free[s], 1)
            for c in range(2):
                s = turns.see()
                for j in range(2):
                    for odd in range(2):
                        last = A.activation(qT2[HD * j:HD * (j + 1), 4 * c + odd:4 * c + odd + 3:2, :],
                                            ps[s][HD * odd:HD * (odd + 1), 2 * j:2 * j + 2, :], ACT.Copy, scale=HD ** -0.5)
                last.then_inc(qT_ready, 1)
                A.drain().then_inc(turn_free[s], 1)
            for i in range(16 + 3):
                if i < 16:
                    turns.skip()
                    softmax(i, 8, P * (i // 4 + 1), pr2[:, i % 2], pr2[:, i % 2], False)
                if 0 <= i - 2 < 16:
                    turns.skip()
                if 0 <= i - 1 < 16:
                    width = P * ((i - 1) // 4 + 1)
                    s = turns.see()
                    A.activation(pT2[:, :, 0:width], ps[s][:, :, 0:width], ACT.Copy).then_inc(pT_ready, 1)
                    A.drain().then_inc(turn_free[s], 1)
                b = i - 3
                if b >= 0:
                    s = turns.see()
                    n, g = b // 4, b % 4
                    A.activation(yah[:, 2 * g:2 * g + 2, P * n:P * (n + 1)],
                                 ps[s][:, 0, 0:256].rearrange("p (c t) -> p c t", c=2), ACT.Copy).then_inc(yT_ready, 1)
            turns.skip(2)

            A.wait_ge(dt_step, 1)
            A.activation(dtt[:, 1], dtt[:, 0], ACT.Abs)
            A.activation(dtt[:, 6, 0, :], a_log[:], ACT.Exp)
            A.drain()
            A.activation(dtt[:, 2], dtt[:, 1], ACT.Exp, scale=-1.0).then_inc(dt_act, 1)
            A.wait_ge(dt_step, 2)
            A.activation(dtt[:, 5], dtt[:, 3], ACT.Ln).then_inc(dt_act, 1)

            def into_conv(n):
                s = turns.see()
                if n > 1:
                    A.wait_ge(conv_out, n - 1)
                A.activation(cpad[:, :, 3:3 + S], ps[s][:], ACT.Copy).then_inc(conv_in, 1)
                A.drain().then_inc(turn_free[s], 1)

            def out_of_conv(n, dst):
                A.wait_ge(conv_out, n)
                A.activation(dst[:], dst[:], ACT.Silu).then_inc(xs_ready, 1)

            def rows_back(dst):
                s = turns.see()
                A.activation(dst, ps[s][:], ACT.Copy).then_inc(xtok_ready, 1)
                A.drain().then_inc(turn_free[s], 1)

            A.wait_ge(conv_in, 1)
            into_conv(1)
            out_of_conv(1, bT)
            into_conv(2)
            out_of_conv(2, cT)
            rows_back(btok[:])
            for j in range(4):
                into_conv(3 + j)
                out_of_conv(3 + j, xsT)
                rows_back(xtok[:, :, 512 * j:512 * (j + 1)])

            for c in range(TT):
                turns.skip()
                A.wait_ge(acs_ready, c + 1)
                A.activation(st[:, 5, 0:32], st[:, 2, 0:32], ACT.Exp)
                A.activation(st[:, 4, 0:32], st[:, 1, 0:32], ACT.Exp)
                A.activation(st[:, 6, 0:32], st[:, 3, 0:32], ACT.Exp).then_inc(e_ready, 1)
                for half in range(2):
                    s = turns.see()
                    for h in range(16):
                        hh = 16 * half + h
                        A.activation(decay[:, hh, :], ps[s][:, h // 4, P * (h % 4):P * (h % 4 + 1)], ACT.Relu,
                                     bias=st[:, 1, hh:hh + 1], scale=-1.0)
                    A.drain()
                    for g in (2 * half, 2 * half + 1):
                        e = decay[:, 8 * g:8 * g + 8, :]
                        A.activation(e, e, ACT.Exp, scale=-1.0).then_inc(e_ready, 1)
                    A.drain().then_inc(turn_free[s], 1)
                turns.skip(1 + (c > 0) + (c < TT - 1))

            for c in range(2):
                s = turns.see()
                A.activation(sgb[:, 4 * c:4 * c + 4, :], ps[s][:], ACT.Tanh, scale=0.5).then_inc(sgb_ready, 1)
                A.drain().then_inc(turn_free[s], 1)
            for g in range(4):
                s = turns.see()
                if g > 0:
                    A.wait_ge(gated, g)
                A.activation(sz[:], ps[s][:], ACT.Silu).then_inc(sz_ready, 1)
                A.drain().then_inc(turn_free[s], 1)
            A.wait_ge(gated, 4)
            for g in range(4):
                for t in range(TT):
                    A.activation(junk3[:, 0:512], xtok[:, t, 512 * g:512 * (g + 1)], ACT.Square,
                                 accum_out=st[:, 0, 32 + 4 * g + t:33 + 4 * g + t])
                    A.drain()
            A.drain()
            A.activation(st[:, 1, 32:48], st[:, 0, 32:48], ACT.Sqrt, scale=1.0 / 512, bias=st[:, 9, 0:1]).then_inc(rms_ready, 1)
            for r in range(2):
                high_parts("ssd", first=KC * r)
                turns.skip(2)
            for c0 in (0, 4):
                A.wait_ge(mT_ready, 1)
                A.activation(hi[:, c0:c0 + 4, :], mT[:, c0:c0 + 4, :], ACT.Copy, scale=0.5).then_inc(hi_ready, 4)
            turns.skip(2)

            A.wait_ge(x2_ready, 1)
            norm(lambda t: xres[:, t, :], TT, junk3[:], 16)
            s = turns.see()
            for c in range(4):
                A.activation(hT[:, c, :], ps[s][:, c, :], ACT.Copy, scale=gain("ffn", c)).then_inc(hi_ready, 1)
            A.drain().then_inc(turn_free[s], 1)
            turns.skip(4)
            A.wait_ge(rt_step, 1)
            A.activation(rt[:, 1, :, 0:4], rt[:, 1, :, 0:4], ACT.Exp).then_inc(rt_act, 1)
            A.wait_ge(rt_step, 2)
            A.activation(rt[:, 8, :, 0:1], rt[:, 8, :, 0:1], ACT.Exp).then_inc(rt_act, 1)

            def evacuate(s, b, stored):
                A.wait_ge(dn_done, s + 1)
                if stored is not None:
                    A.wait_ge(y_out[b], 16 * stored)
                A.activation(yg[b][:].rearrange("p (c n) -> p c n", c=2), ps[1][:, 0:2, :], ACT.Copy).then_inc(y_ready, 1)

            def step(s, b, stored, first=False):
                A.wait_ge(gu_done, s + 1)
                if not first:
                    A.wait_ge(act_ready, s)
                A.activation(sa[:], ps[0][:, 0, 0:HID], ACT.Silu).then_inc(sa_ready, 1)
                if not first:
                    evacuate(s - 1, (b - 1) % 3, stored)
                A.wait_ge(act_turned, s + 1)
                A.activation(actT[:].rearrange("p f n -> p (f n)"), ps[0][:, 1, 0:2 * P], ACT.Copy).then_inc(actT_ready, 1)

            step(0, 0, None, first=True)
            for s in (1, 2, 3):
                step(s, s % 3, None)
            with A.Fori(0, (SLOTS - 6) // 3) as i:
                for j in (4, 5, 6):
                    step(3 * i + j, j % 3, i + 1)
            for s in range(SLOTS - 2, SLOTS):
                step(s, s % 3, (s - 1) // 3)
            evacuate(SLOTS - 1, (SLOTS - 1) % 3, (SLOTS - 1) // 3)

        @block.vector
        def _(V):
            turns = Turns(V, turn_full, turn_free)
            his = [0]

            def unit_rows(dst, rows, n, count, k):
                V.wait_ge(rms_ready, count)
                V.reciprocal(st[:, 2, k:k + n], st[:, 1, k:k + n])
                V.drain()
                for t in range(n):
                    last = V.tensor_scalar(dst(t), rows(t), st[:, 2, k + t:k + t + 1], None, ALU.mult)
                return last

            def low_parts(name, first=0, n=S, chunks=KC):
                for c0 in range(0, chunks, 4):
                    s = turns.see()
                    for c in range(4):
                        his[0] += 1
                        V.wait_ge(hi_ready, his[0])
                        last = V.scalar_tensor_tensor(lo[:, c0 + c, 0:n], ps[s][:, c, 0:n], gain(name, first + c0 + c),
                                                      hi[:, c0 + c, 0:n].bitcast(F32), ALU.mult, ALU.subtract)
                    last.then_inc(lo_ready, 1)
                    V.drain().then_inc(turn_free[s], 1)

            def rope(x, heads):
                a, b = x[:, :, :, 0:8], x[:, :, :, 8:16]
                c, s = bc(cos[:], 2, heads), bc(sin[:], 2, heads)
                a_s, b_s_ = (rot[:, i, :, 0:8 * heads].rearrange("p t (h f) -> p t h f", h=heads) for i in range(2))
                V.tensor_tensor(a_s, a, s, ALU.mult)
                V.tensor_tensor(b_s_, b, s, ALU.mult)
                V.drain()
                V.tensor_tensor(a, a, c, ALU.mult)
                V.tensor_tensor(b, b, c, ALU.mult)
                V.drain()
                V.tensor_tensor(a, a, b_s_, ALU.subtract)
                return V.tensor_tensor(b, b, a_s, ALU.add)

            V.memset(st[:, 9, :], EPS).then_inc(setup_done, 1)
            V.memset(ones[:], 1.0)
            V.wait_ge(par_in, PARAMS)
            s = turns.see()
            V.tensor_copy(cols[:], ps[s][:, 0, 0:N_ROWS_A + N_ROWS_B]).then_inc(cols_ready, 1)
            V.tensor_tensor(brow[:], ps[s][0:4, 1, 0:384], outside[:], ALU.add).then_inc(brow_ready, 1)
            V.tensor_tensor(wspT[:], ps[s][:, 2, :].rearrange("p (g t) -> p g t", g=4), bc(tri[:], 1, 4), ALU.mult)\
                .then_inc(wspT_ready, 1)
            V.drain().then_inc(turn_free[s], 1)

            unit_rows(lambda t: xn[:, t, :], lambda t: memb[:, t, :], 2, 1, 0).then_inc(rows_ready, 1)
            V.drain()
            low_parts("mem", n=MEM)
            unit_rows(lambda t: xn[:, t, :], lambda t: xres[:, t, :], TT, 2, 4).then_inc(rows_ready, 1)
            turns.skip()
            low_parts("pre")
            turns.skip()

            turns.skip()
            V.wait_ge(v_ready, 1)
            v4 = vt[:].rearrange("p t (g c) -> p (t g) c", g=4)
            t4 = vtmp[:].rearrange("p t (g c) -> p (t g) c", g=4)
            V.tensor_reduce(st[:, 3, 0:16], v4, AX.X, ALU.add)
            V.drain()
            V.tensor_scalar(st[:, 5, 0:16], st[:, 3, 0:16], 1.0 / P, None, ALU.mult)
            V.drain()
            V.tensor_tensor(v4, v4, bc(st[:, 5, 0:16], 2, P), ALU.subtract)
            V.drain()
            V.tensor_tensor(t4, v4, v4, ALU.mult)
            V.drain()
            V.tensor_reduce(st[:, 3, 0:16], t4, AX.X, ALU.add).then_inc(v_ready, 1)
            V.wait_ge(rms_ready, 3)
            V.reciprocal(st[:, 5, 0:16], st[:, 4, 0:16])
            V.drain()
            V.tensor_tensor(v4, v4, bc(st[:, 5, 0:16], 2, P), ALU.mult)
            V.drain()
            V.tensor_tensor(vt[:], vt[:], bc(v_g[:], 1, TT), ALU.mult)
            V.drain()
            V.tensor_tensor(vt[:], vt[:], bc(v_b[:], 1, TT), ALU.add).then_inc(v_normed, 1)
            turns.skip(4)
            V.wait_ge(bias_in, 64)
            s = turns.see()
            for g in range(4):
                last = V.tensor_tensor(yT[:, g, :].rearrange("p (n t) -> p n t", n=TT),
                                       ps[s][:, g, :].rearrange("p (n t) -> p n t", n=TT), bc(b_s[:, g, :], 1, TT), ALU.add)
            V.drain().then_inc(turn_free[s], 1)
            V.wait_ge(u_ready, 1)
            V.tensor_tensor(yT[:, 0:4], yT[:, 0:4], uT[:], ALU.mult)
            V.drain()
            V.wait_ge(z1_ready, 1)
            V.tensor_tensor(yT[:, 0:4], yT[:, 0:4], zT[:, 0:4], ALU.mult)

            s = turns.see()
            V.tensor_copy(bias[:], ps[s][:, :, 0:256])
            V.drain().then_inc(turn_free[s], 1)

            def probabilities_used(b, base, yt, sinks_too):
                s = turns.see()
                k = b % 4
                V.wait_ge(exp_ready, base + b + 1)
                den = sm[:, 1, k, :]
                if sinks_too:
                    V.tensor_tensor(den, den, sm[:, 4, k, :], ALU.add)
                    V.drain()
                V.reciprocal(sm[:, 5, k, :], den)
                V.drain()
                V.tensor_tensor(yt[:, b % 2, :].rearrange("p (h d) -> p h d", h=4),
                                ps[s][:, 0, 0:256].rearrange("p (h d) -> p h d", h=4), bc(sm[:, 5, k, :], 2, HD), ALU.mult)\
                    .then_inc(yt_ready, 1)
                V.drain().then_inc(turn_free[s], 1)

            for i in range(8 + 3):
                if i < 8:
                    k, n = i % 4, i
                    s = turns.see()
                    if i < 4:
                        width = P if n == 0 else 256
                        for h in range(4):
                            V.tensor_tensor_reduce(pr1[:, i % 2, h, 0:width], ps[s][:, h, 0:width], bias[:, h, 256 - width:256],
                                                   1.0, -3e38, ALU.add, ALU.max, sm[:, 0, k, h:h + 1])
                        V.drain().then_inc(turn_free[s], 1)
                        V.tensor_tensor(sm[:, 0, k, :], sm[:, 0, k, :], sinks[:], ALU.max)
                        V.drain()
                        V.tensor_tensor(sm[:, 3, k, :], sinks[:], sm[:, 0, k, :], ALU.subtract)
                    else:
                        V.tensor_reduce(sm[:, 0, k, :], ps[s][:, :, 0:MEM], AX.X, ALU.max)
                        V.drain()
                    V.tensor_scalar(sm[:, 2, k, :], sm[:, 0, k, :], -1.0, None, ALU.mult).then_inc(max_ready, 1)
                if 0 <= i - 2 < 8:
                    probabilities_used(i - 2, 0, yt1, i - 2 < 4)
                if 0 <= i - 1 < 8:
                    turns.skip()
                if i >= 3:
                    turns.skip()
            V.drain().then_inc(z1_ready, 1)
            V.wait_ge(z1_ready, 3)
            V.wait_ge(yT_ready, 8)
            V.tensor_tensor(yT[:, 4:8], yT[:, 4:8], zT[:, 4:8], ALU.mult).then_inc(z1_ready, 1)
            for c0 in (0, 4):
                his[0] += 4
                V.wait_ge(z1_ready, 3 + c0 // 4)
                V.wait_ge(hi_ready, his[0])
                V.tensor_tensor(lo[:, c0:c0 + 4], yT[:, c0:c0 + 4], hi[:, c0:c0 + 4].bitcast(F32), ALU.subtract)\
                    .then_inc(lo_ready, 1)
            turns.skip(2)
            V.wait_ge(rms_ready, 4)
            V.reciprocal(st[:, 2, 8:8 + TT], st[:, 1, 8:8 + TT])
            V.drain()
            for t in range(TT):
                V.scalar_tensor_tensor(xn[:, t, :], xn[:, t, :], st[:, 2, 8 + t:9 + t], post_g[:], ALU.mult, ALU.mult)
            V.drain()
            V.tensor_tensor(xres[:], xres[:], xn[:], ALU.add).then_inc(x1_ready, 1)
            V.drain()

            unit_rows(lambda t: qt[:, t, :], lambda t: xres[:, t, :], TT, 5, 12).then_inc(rows_ready, 1)
            low_parts("attn")

            turns.skip()
            V.wait_ge(iq_ready, 1)
            rope(iqt[:].rearrange("p t (h d) -> p t h d", h=8), 8).then_inc(iq_rows, 1)
            turns.skip()
            V.wait_ge(small_ready, 1)
            ik = smt[:, :, 0:HD]
            V.tensor_tensor(ikt[:, :, 0:HD], ik, ik, ALU.mult)
            V.tensor_scalar(smt[:, :, HD:HD + 8], smt[:, :, HD:HD + 8], 8 ** -0.5, None, ALU.mult)
            V.drain()
            V.tensor_reduce(st[:, 3, 16:20], ikt[:, :, 0:HD], AX.X, ALU.add).then_inc(sq_ready, 1)
            V.wait_ge(rms_ready, 6)
            V.reciprocal(st[:, 5, 16:20], st[:, 4, 16:20])
            V.drain()
            V.tensor_tensor(ik, ik, bc(st[:, 5, 16:20], 2, HD), ALU.mult)
            V.drain()
            V.tensor_tensor(ikt[:, :, 0:HD], ik, bc(ik_g[:], 1, TT), ALU.mult)
            V.drain()
            rope(ikt[:, :, 0:HD].unsqueeze(2), 1)
            V.drain()
            V.tensor_copy(ikt[:, :, HD:P], ikt[:, :, 0:HD]).then_inc(iq_rows, 1)

            def norm_heads(x, heads, gains, root):
                t = x.shape[1]
                x3 = x.rearrange("p t (h d) -> p t h d", h=heads)
                V.tensor_tensor(x3, x3, bc(root, 3, HD), ALU.mult)
                V.drain()
                return V.tensor_tensor(x3, x3, gains[:].unsqueeze(1).unsqueeze(1).broadcast_to([P, t, heads, HD]), ALU.mult)

            turns.skip()
            V.wait_ge(kv_ready, 1)
            k4 = kvt[:, :, 0:256]
            sq_k = sqr[:].rearrange("p a b -> p (a b)")[:, 0:1024].rearrange("p (t n) -> p t n", t=TT)
            V.tensor_tensor(sq_k, k4, k4, ALU.mult)
            V.drain()
            V.tensor_reduce(st[:, 3, 20:36], sq_k.rearrange("p t (h d) -> p t h d", h=4), AX.X, ALU.add).then_inc(sq_ready, 1)
            V.wait_ge(rms_ready, 7)
            V.reciprocal(st[:, 5, 20:36], st[:, 4, 20:36])
            V.drain()
            norm_heads(k4, 4, k_g, st[:, 5, 20:36].rearrange("p (t h) -> p t h", t=TT))
            V.drain()
            rope(k4.rearrange("p t (h d) -> p t h d", h=4), 4).then_inc(k_rows, 1)
            turns.skip(3)

            for i in range(6):
                n, h4 = 1 + i // 2, i % 2
                w = P * (n + 1)
                turns.skip()
                V.wait_ge(rel_ready, i + 1)
                for h in range(4):
                    k = 4 * h4 + h
                    iw = smt[:, n, HD + k:HD + k + 1]
                    if k == 0:
                        last = V.tensor_scalar(score[:, n - 1, 0:w], rel[:, h, 0:w], iw, None, ALU.mult)
                    else:
                        last = V.scalar_tensor_tensor(score[:, n - 1, 0:w], rel[:, h, 0:w], iw, score[:, n - 1, 0:w],
                                                      ALU.mult, ALU.add)
                    if h == 3:
                        last.then_inc(rel_used, 1)
                    V.drain()
            V.memset(sel[:, 0, 0:P], 0.0)
            V.drain()
            V.memset(sel[0:64, 0, 64:P], NEG)
            for n in range(1, TT):
                w = P * (n + 1)
                row = score[:, n - 1, 0:w]
                V.memset(score[0:64, n - 1, P * n + 64:w], -1e38)
                V.drain()
                for r in range(TOPK // 8):
                    V.max(top[:, r % 2, :], row)
                    V.drain()
                    V.match_replace(row, top[:, r % 2, :], row, -3e38)
                    V.drain()
                V.tensor_scalar(sel[:, n, 0:w], row, -2e38, NEG, ALU.is_gt, ALU.mult)
            V.drain()
            turns.skip(3)
            V.wait_ge(q_ready, 2)
            for t in (0, 2):
                V.tensor_tensor(sqr[:], qt[:, t:t + 2, :], qt[:, t:t + 2, :], ALU.mult)
                V.drain()
                last = V.tensor_reduce(st[:, 6, 16 * t:16 * t + 32], sqr[:].rearrange("p t (h d) -> p t h d", h=16), AX.X, ALU.add)
                if t == 2:
                    last.then_inc(sq_ready, 1)
                V.drain()
            V.wait_ge(rms_ready, 8)
            V.reciprocal(st[:, 8, 0:64], st[:, 7, 0:64])
            V.drain()
            norm_heads(qt[:], 16, q_g, st[:, 8, 0:64].rearrange("p (t h) -> p t h", t=TT))
            V.drain()
            rope(qt[:].rearrange("p t (h d) -> p t h d", h=16), 16).then_inc(q_rows, 1)
            turns.skip(3)

            for i in range(16 + 3):
                if i < 16:
                    k, n = i % 4, i // 4
                    width = P * (n + 1)
                    s = turns.see()
                    for h in range(4):
                        V.tensor_tensor_reduce(pr2[:, i % 2, h, 0:width], ps[s][:, h, 0:width], sel[:, n, 0:width],
                                               1.0, -3e38, ALU.add, ALU.max, sm[:, 0, k, h:h + 1])
                    V.drain().then_inc(turn_free[s], 1)
                    V.tensor_scalar(sm[:, 2, k, :], sm[:, 0, k, :], -1.0, None, ALU.mult).then_inc(max_ready, 1)
                if 0 <= i - 2 < 16:
                    probabilities_used(i - 2, 8, yt2, False)
                if 0 <= i - 1 < 16:
                    turns.skip()
                b = i - 3
                if b >= 0:
                    s = turns.see()
                    nn, g = b // 4, b % 4
                    V.wait_ge(yT_ready, 8 + b + 1)
                    o = (slice(None), slice(2 * g, 2 * g + 2), slice(P * nn, P * (nn + 1)))
                    V.tensor_tensor(yal[o], ps[s][:, 0, 0:256].rearrange("p (c t) -> p c t", c=2), yah[o].bitcast(F32), ALU.subtract)\
                        .then_inc(yal_ready, 1)
                    V.drain().then_inc(turn_free[s], 1)
            for c in range(2):
                s = turns.see()
                V.wait_ge(sga_ready, c + 1)
                V.scalar_tensor_tensor(mT[:, 4 * c:4 * c + 4], sg[:, 4 * c:4 * c + 4], 1.0, ps[s][:], ALU.add, ALU.mult)
                V.drain().then_inc(turn_free[s], 1)

            V.tensor_tensor(dtt[:, 0], smt[:, :, 72:SMALL], bc(dt_b[:], 1, TT), ALU.add).then_inc(dt_step, 1)
            V.wait_ge(dt_act, 1)
            V.tensor_scalar(dtt[:, 3], dtt[:, 2], 1.0, None, ALU.add)
            V.drain().then_inc(dt_step, 1)
            V.tensor_scalar(dtt[:, 4], dtt[:, 3], 1.0, None, ALU.is_equal)
            V.drain()
            V.scalar_tensor_tensor(dtt[:, 7], dtt[:, 3], -1.0, dtt[:, 4], ALU.add, ALU.add)
            V.drain()
            V.reciprocal(dtt[:, 7], dtt[:, 7])
            V.drain()
            V.tensor_tensor(dtt[:, 7], dtt[:, 7], dtt[:, 2], ALU.mult)
            V.wait_ge(dt_act, 2)
            V.tensor_tensor(dtt[:, 4], dtt[:, 4], dtt[:, 2], ALU.mult)
            V.drain()
            V.tensor_tensor(dtt[:, 7], dtt[:, 7], dtt[:, 5], ALU.mult)
            V.drain()
            V.tensor_tensor(dtt[:, 7], dtt[:, 7], dtt[:, 4], ALU.add)
            V.drain()
            V.scalar_tensor_tensor(dts[:, 0], dtt[:, 0], 0.0, dtt[:, 7], ALU.max, ALU.add)
            V.tensor_scalar(dtt[:, 6, 1, :], dtt[:, 6, 0, :], -1.0, None, ALU.mult)
            V.drain()
            V.tensor_tensor(dts[:, 1], dts[:, 0], bc(dtt[:, 6, 1, :], 1, TT), ALU.mult).then_inc(dt_step, 1)

            V.memset(cpad[:, :, 0:3], 0.0).then_inc(conv_in, 1)

            def convolve(n, c0, dst):
                V.wait_ge(conv_in, n + 1)
                if dst is xsT and n > 3:
                    V.wait_ge(xtok_ready, n - 2)
                def tap(k, c):
                    j = N_ROWS_A + 24 * k + c0 + c
                    return cols[:, j:j + 1]
                for c in range(4):
                    V.tensor_scalar(dst[:, c, :], cpad[:, c, 0:S], tap(0, c), gain("conv_b", c0 + c), ALU.mult, ALU.add)
                V.drain()
                for k in range(1, 4):
                    for c in range(4):
                        V.scalar_tensor_tensor(dst[:, c, :], cpad[:, c, k:k + S], tap(k, c), dst[:, c, :], ALU.mult, ALU.add)
                    if k < 3:
                        V.drain()
                V.drain().then_inc(conv_out, 1)

            convolve(1, 16, bT)
            convolve(2, 20, cT)
            for j in range(4):
                convolve(3 + j, 4 * j, xsT)
            turns.skip(11)

            V.wait_ge(xtok_ready, 5)
            for c in range(TT):
                s = turns.see()
                V.tensor_copy(st[:, 1, 0:32], ps[s][:, 0, 0:32])
                V.tensor_copy(st[:, 3, 0:32], ps[s][:, 0, 32:64])
                V.tensor_tensor(cb[:], ps[s][:, 1, :].rearrange("p (g l) -> p g l", g=4), bc(tri[:], 1, 4), ALU.mult)
                V.drain().then_inc(turn_free[s], 1)
                V.tensor_tensor(st[:, 2, 0:32], st[:, 3, 0:32], st[:, 1, 0:32], ALU.subtract).then_inc(acs_ready, 1)
                V.tensor_tensor(xd[:], xtok[:, c, :].rearrange("p (h d) -> p h d", h=32), bc(dts[:, 0, c, :], 2, HD), ALU.mult)\
                    .then_inc(xd_ready, 1)
                V.drain()
                V.wait_ge(e_ready, 5 * c + 1)
                V.tensor_tensor(xe[:], xd[:], bc(st[:, 5, 0:32], 2, HD), ALU.mult).then_inc(xe_ready, 1)
                turns.skip(2)
                for g in range(4):
                    V.wait_ge(e_ready, 5 * c + 2 + g)
                    m = decay[:, 8 * g:8 * g + 8, :]
                    V.tensor_tensor(m, m, bc(cb[:, g, :], 1, 8), ALU.mult).then_inc(m_ready, 1)
                y = xtok[:, c, :].rearrange("p (h d) -> p h d", h=32)
                V.tensor_tensor(y, y, bc(d_skip[:], 2, HD), ALU.mult)
                V.drain()
                s = turns.see()
                V.tensor_tensor(xtok[:, c, :], xtok[:, c, :], ps[s][:].rearrange("p g n -> p (g n)"), ALU.add)
                V.drain().then_inc(turn_free[s], 1)
                if c > 0:
                    s = turns.see()
                    V.tensor_tensor(yoff[:], ps[s][:].rearrange("p g (h d) -> p (g h) d", d=HD), bc(st[:, 4, 0:32], 2, HD), ALU.mult)
                    V.drain().then_inc(turn_free[s], 1)
                    V.tensor_tensor(y, y, yoff[:], ALU.add)
                if c < TT - 1:
                    s = turns.see()
                    if c > 0:
                        sh = state[:].rearrange("p (h d) -> p h d", h=32)
                        V.tensor_tensor(sh, sh, bc(st[:, 6, 0:32], 2, HD), ALU.mult)
                        V.drain()
                        V.tensor_tensor(state[:], state[:], ps[s][:].rearrange("p g n -> p (g n)"), ALU.add).then_inc(st_ready, 1)
                    else:
                        V.tensor_copy(state[:], ps[s][:].rearrange("p g n -> p (g n)")).then_inc(st_ready, 1)
                    V.drain().then_inc(turn_free[s], 1)
            turns.skip(2)
            V.drain()
            for g in range(4):
                turns.skip()
                V.wait_ge(sz_ready, g + 1)
                yg = xtok[:, :, 512 * g:512 * (g + 1)]
                V.tensor_tensor(yg, yg, sz[:], ALU.mult).then_inc(gated, 1)
            V.wait_ge(rms_ready, 9)
            V.reciprocal(st[:, 2, 32:48], st[:, 1, 32:48])
            V.drain()
            for g in range(4):
                for t in range(TT):
                    yg = xtok[:, t, 512 * g:512 * (g + 1)]
                    last = V.tensor_scalar(yg, yg, st[:, 2, 32 + 4 * g + t:33 + 4 * g + t], None, ALU.mult)
                if g % 2:
                    last.then_inc(y_rows, 1)
            for r in range(2):
                low_parts("ssd", first=KC * r)
                for c in range(2):
                    s = turns.see()
                    V.wait_ge(sgb_ready, 2)
                    V.scalar_tensor_tensor(sz[:], sgb[:, 4 * c:4 * c + 4], 1.0, ps[s][:], ALU.add, ALU.mult)
                    V.drain().then_inc(turn_free[s], 1)
                    last = V.tensor_tensor(mT[:, 4 * c:4 * c + 4], mT[:, 4 * c:4 * c + 4], sz[:], ALU.add)
                    if r == 1 and c == 1:
                        last.then_inc(mT_ready, 1)
                    V.drain()
            for c0 in (0, 4):
                his[0] += 4
                V.wait_ge(hi_ready, his[0])
                V.scalar_tensor_tensor(lo[:, c0:c0 + 4], mT[:, c0:c0 + 4], 0.5, hi[:, c0:c0 + 4].bitcast(F32),
                                       ALU.mult, ALU.subtract).then_inc(lo_ready, 1)
            V.wait_ge(x1_back, 16)
            for c in range(2):
                s = turns.see()
                V.tensor_tensor(xres[:, :, 512 * c:512 * (c + 1)], xres[:, :, 512 * c:512 * (c + 1)], ps[s][:], ALU.add)
                V.drain().then_inc(turn_free[s], 1)
            V.drain().then_inc(x2_ready, 1)

            unit_rows(lambda t: xn[:, t, :], lambda t: xres[:, t, :], TT, 10, 16).then_inc(rows_ready, 1)
            turns.skip()
            s = turns.see()
            for c in range(4):
                last = V.tensor_scalar(hT[:, 4 + c, :], ps[s][:, c, :], gain("ffn", 4 + c), None, ALU.mult)
            last.then_inc(lo_ready, 1)
            V.drain().then_inc(turn_free[s], 1)
            s = turns.see()
            logits = rt[:, 0]
            V.tensor_tensor(logits, ps[s][:, :, 0:36], bc(b_rt[:], 1, TT), ALU.add)
            V.drain().then_inc(turn_free[s], 1)

            def first_max(hot, x, m, key, n):
                V.tensor_tensor(hot, x, bc(m, 2, n), ALU.is_equal)
                V.drain()
                V.tensor_tensor(hot, hot, bc(order[:, 0:n], 1, TT), ALU.mult)
                V.drain()
                V.tensor_reduce(key, hot, AX.X, ALU.max)
                V.drain()
                V.tensor_tensor(hot, hot, bc(key, 2, n), ALU.is_equal)
                V.drain()

            gl, ge, ghot = rt[:, 0, :, 0:4], rt[:, 1, :, 0:4], rt[:, 2, :, 0:4]
            gm, gs, m1, m2, key, p1, p2 = (rt[:, 3, :, i] for i in range(7))
            e_in, hot1, hot2 = rt[:, 4, :, 0:8], rt[:, 5, :, 0:8], rt[:, 6, :, 0:8]
            V.tensor_reduce(gm, gl, AX.X, ALU.max)
            V.drain()
            V.tensor_tensor(ge, gl, bc(gm, 2, 4), ALU.subtract).then_inc(rt_step, 1)
            V.wait_ge(rt_act, 1)
            V.tensor_reduce(gs, ge, AX.X, ALU.add)
            V.drain()
            first_max(ghot, gl, gm, key, 4)
            per_group = rt[:, 7, :, 0:32].rearrange("p t (g e) -> p t g e", g=4)
            V.tensor_tensor(per_group, rt[:, 0, :, 4:36].rearrange("p t (g e) -> p t g e", g=4), bc(ghot, 3, 8), ALU.mult)
            V.drain()
            V.tensor_reduce(e_in, per_group.rearrange("p t g e -> p t e g"), AX.X, ALU.add)
            V.drain()
            V.tensor_reduce(m1, e_in, AX.X, ALU.max)
            V.drain()
            first_max(hot1, e_in, m1, key, 8)
            rest = rt[:, 9, :, 0:8]
            V.tensor_scalar(rest, hot1, NEG, None, ALU.mult)
            V.drain()
            V.tensor_tensor(rest, rest, e_in, ALU.add)
            V.drain()
            V.tensor_reduce(m2, rest, AX.X, ALU.max)
            V.drain()
            first_max(hot2, rest, m2, key, 8)
            V.tensor_tensor(rt[:, 8, :, 0], m2, m1, ALU.subtract).then_inc(rt_step, 1)
            V.wait_ge(rt_act, 2)
            V.tensor_scalar(p1, rt[:, 8, :, 0], 1.0, None, ALU.add)
            V.drain()
            V.tensor_tensor(p1, p1, gs, ALU.mult)
            V.drain()
            V.reciprocal(p1, p1)
            V.drain()
            V.tensor_tensor(p2, p1, rt[:, 8, :, 0], ALU.mult)
            V.drain()
            for k, h in enumerate((hot1, hot2)):
                V.tensor_tensor(hot[:, k].rearrange("p t (g e) -> p t g e", g=4), bc(ghot, 3, 8), bc(h, 2, 4), ALU.mult)
            V.drain()
            V.tensor_tensor(rt[:, 10, :, 0:32], hot[:, 0], hot[:, 1], ALU.add).then_inc(rt_step, 1)
            s = turns.see()
            pairs, slots = ps[s][:, 1, 0:32], cnt[:, 0, :]
            V.tensor_scalar(slots, pairs, 0.0, None, ALU.is_gt)
            V.drain()
            for full in range(P, S, P):
                V.scalar_tensor_tensor(slots, pairs, float(full), slots, ALU.is_gt, ALU.add)
                V.drain()
            end = slots
            for i, shift in enumerate((1, 2, 4, 8, 16)):
                V.tensor_copy(cnt[:, 1 + i, 0:shift], end[:, 0:shift])
                V.tensor_tensor(cnt[:, 1 + i, shift:32], end[:, shift:32], end[:, 0:32 - shift], ALU.add)
                V.drain()
                end = cnt[:, 1 + i, :]
            V.tensor_tensor(ends[:], bc(end[0:1, :], 1, SLOTS), bc(iota[0:1, 0:SLOTS], 2, N_EXP), ALU.is_le)
            V.drain()
            V.tensor_reduce(slot_f[:], ends[:], AX.X, ALU.add)
            V.drain()
            V.tensor_scalar(slot_e[:], slot_f[:], float(N_EXP - 1), None, ALU.min).then_inc(slots_ready, 1)
            row0 = cnt[:, 6, :]
            V.tensor_tensor(row0, end, slots, ALU.subtract)
            V.drain()
            V.tensor_scalar(row0, row0, float(P), -1.0, ALU.mult, ALU.add)
            V.drain()
            where = rt[:, 11, :, 0:32]
            V.tensor_tensor(where, ps[s][:, 0, 0:32 * TT].rearrange("p (t e) -> p t e", t=TT), bc(row0, 1, TT), ALU.add)
            V.drain().then_inc(turn_free[s], 1)
            V.tensor_tensor(hot[:], hot[:], bc(where, 1, 2), ALU.mult)
            V.drain()
            V.tensor_reduce(pos[:, 0, :], hot[:].rearrange("p k t e -> p (k t) e"), AX.X, ALU.add)
            V.drain()
            V.tensor_copy(pos_u[:], pos[:, 0, :])
            starts = rt[:, 12, 0:2, :].rearrange("p a b -> p (a b)")[:, 0:SLOTS]
            V.tensor_scalar(starts, iota[:, 0:SLOTS], float(P), None, ALU.mult)
            V.drain()
            V.tensor_tensor(hot_b[:], bc(starts, 1, 2 * TT), bc(pos[:, 0, :], 2, SLOTS), ALU.is_le)
            V.drain()
            V.tensor_reduce(pos[:, 1, :], hot_b[:], AX.X, ALU.add)
            V.drain()
            V.tensor_scalar(pos[:, 1, :], pos[:, 1, :], -1.0, None, ALU.add)
            V.drain()
            V.scalar_tensor_tensor(pos[:, 2, :], pos[:, 1, :], -float(P), pos[:, 0, :], ALU.mult, ALU.add)
            V.tensor_tensor(hot_b[:], bc(iota[:, 0:SLOTS], 1, 2 * TT), bc(pos[:, 1, :], 2, SLOTS), ALU.is_equal)
            V.drain()
            V.tensor_tensor(hot_r[:], bc(iota[:], 1, 2 * TT), bc(pos[:, 2, :], 2, P), ALU.is_equal)
            for k in range(2):
                V.tensor_tensor(hot_b[:, TT * k:TT * (k + 1), :], hot_b[:, TT * k:TT * (k + 1), :], bc(token[:], 2, SLOTS), ALU.mult)
            V.drain().then_inc(rt_step, 1)
            s = turns.see()
            V.tensor_copy(tab_u[:], ps[s][:, 0, 0:SLOTS])
            V.drain().then_inc(table_ready, 1)

            def rows_slot(s):
                V.wait_ge(turned, s + 1)
                V.tensor_tensor(xT[:], ps[0][:, 2:4, :].rearrange("p c (k t) -> p (c k) t", t=P), bc(ffn_kp[:], 2, P), ALU.mult)\
                    .then_inc(xT_ready, 1)

            def step(s, b, last=False):
                if not last:
                    rows_slot(s + 1)
                V.wait_ge(sa_ready, s + 1)
                if not (isinstance(s, int) and s == 0):
                    V.wait_ge(act_turned, s)
                V.tensor_tensor(act[:], sa[:], ps[0][:, 0, HID:2 * HID], ALU.mult).then_inc(act_ready, 1)

            rows_slot(0)
            step(0, 0)
            with V.Fori(0, (SLOTS - 3) // 3) as i:
                for j in (1, 2, 3):
                    step(3 * i + j, j % 3)
            step(SLOTS - 2, 1)
            step(SLOTS - 1, 2, last=True)
            for t in range(TT):
                V.wait_ge(back_in[t], 32)
                for k, share in enumerate((p1, p2)):
                    last = V.scalar_tensor_tensor(xres[:, t, :], back[:, TT * k + t, :], share[:, t:t + 1], xres[:, t, :], ALU.mult, ALU.add)
                    if k == 0:
                        V.drain()
                last.then_inc(out_ready, 1)



def kernel(**inputs):
    import concourse.bacc as bacc
    from concourse.bass_utils import run_bass_kernel_spmd

    nc = bacc.Bacc("TRN2", target_bir_lowering=False, num_devices=1)
    arrays = {n: np.ascontiguousarray(a) for n, a in inputs.items()}
    arrays.update(consts())
    d = {n: nc.dram_tensor(n, a.shape, mybir.dt.from_np(a.dtype), kind="ExternalInput").ap() for n, a in arrays.items()}
    out = nc.dram_tensor("out", [1, S, D], F32, kind="ExternalOutput").ap()
    program(nc, d, out)
    return run_bass_kernel_spmd(nc, [arrays], core_ids=[0]).results[0]["out"]
```

```python
from contextlib import ExitStack, contextmanager

import numpy as np

import concourse.bass as bass
from concourse import mybir

F32 = mybir.dt.float32
F32R = mybir.dt.float32r
ALU = mybir.AluOpType
ACT = mybir.ActivationFunctionType
AX = mybir.AxisListType

P = 128
S = 512
D = 1024
TT = S // P
KC = D // P
HALF = KC // 2
EPS = 1e-6
NEG = -1e30
MEM = 256
HD = 64

A_U, A_V, SQKV, MQ, Z1 = 0, 512, 1024, 1536, 1792
Q2, KV2, IQ2, IK2, Z2, XBC2, DT2, GA2, GB2 = 0, 1024, 1536, 2048, 2120, 4168, 7240, 7272, 8296
SMALL = 104
TOPK = 128
ARENA = 198
N_EXP = 32
HID = 256
SLOTS = (2 * S - N_EXP) // P + N_EXP

ROWS_A = {"pre": 0, "mem": 8, "attn": 16, "ffn": 24, "ssd": 32, "conv_b": 48}
N_ROWS_A, N_ROWS_B = 72, 96


class Turns:

    def __init__(self, eng, full, free):
        self.eng, self.full, self.free = eng, full, free
        self.k, self.off, self.half = 0, 0, 0

    def take(self):
        s = self.k % 2
        if self.k >= 2:
            self.eng.wait_ge(self.free[s], self.half + self.k // 2)
        self.k += 1
        return s

    def settle(self):
        for s in range(2):
            self.eng.wait_ge(self.free[s], (self.k + 1 - s) // 2)

    def see(self):
        s = self.k % 2
        self.k += 1
        self.eng.wait_ge(self.full, self.off + self.k)
        return s

    def skip(self, n=1):
        self.k += n

    @contextmanager
    def loop(self, count, per):
        first = self.k
        with self.eng.Fori(0, count) as i:
            self.off, self.half = i * per, i * (per // 2)
            yield i
        assert self.k == first + per and per % 2 == 0
        self.off = self.half = 0
        self.k = first + per * count


def query_block(b):
    return TT - 1 - b // 4


def consts():
    k = np.arange(P)
    c = {"c_ident": np.eye(P), "c_tri": (k[:, None] <= k[None, :]), "c_flip": np.eye(P)[::-1]}
    dist = 255 - np.arange(384)
    ok = (dist >= 0) & (dist < 128)
    n = np.maximum(dist, 0)
    large = 16 + (np.log(np.maximum(n, 1) / 16) / np.log(128 / 16) * 16).astype(np.int32)
    bucket = np.where(n < 16, n, np.minimum(large, 31))
    c["c_bucket"] = (bucket[None, :] == np.arange(32)[:, None]) & ok[None, :]
    c["c_outside"] = np.broadcast_to(np.where(ok, 0.0, NEG), (4, 384))
    inv = np.float32(500000.0) ** (-np.arange(8, dtype=np.float32) * np.float32(2.0) / np.float32(16))
    ang = (np.arange(S, dtype=np.float32)[:, None] * inv[None, :].astype(np.float32)).astype(np.float32)
    c["c_cos"] = np.cos(ang)
    c["c_sin"] = np.sin(ang)
    c["c_iota"] = np.broadcast_to(k, (P, P))
    c["c_token"] = k[:, None] + P * np.arange(TT)[None, :]
    c["c_order"] = np.broadcast_to(np.arange(8, 0, -1), (P, 8))
    return {n: np.ascontiguousarray(a, dtype=np.float32) for n, a in c.items()}


def bc(ap, axis, n):
    a = ap.unsqueeze(axis)
    shape = list(a.shape)
    shape[axis] = n
    return a.broadcast_to(shape)



def matmul3(pe, out, x, w, first, last):
    pe.matmul(out, x[0], w[0], start=first, stop=False)
    pe.matmul(out, x[1], w[0], start=False, stop=False)
    return pe.matmul(out, x[0], w[1], start=False, stop=last)


def program(nc, d, out):
    w1, w2 = d["w_in"][0], d["w_in_2"][0]
    x1_dram = nc.dram_tensor("x1_scratch", [S, D], F32, kind="Internal").ap()
    bias_dram = nc.dram_tensor("bias_scratch", [4, 384], F32, kind="Internal").ap()
    rows_dram = nc.dram_tensor("rows_scratch", [S, D], F32, kind="Internal").ap()
    y_dram = nc.dram_tensor("y_scratch", [SLOTS * P, D], F32, kind="Internal").ap()
    mT_dram = nc.dram_tensor("merged_scratch", [P, KC, S], F32, kind="Internal").ap()
    gates_dram = [nc.dram_tensor(f"gate_scratch{i}", [P, 4, 512], F32, kind="Internal").ap() for i in range(4)]
    e_gate, e_up, e_down = (d[n][0].rearrange("g e k n -> (g e) k n") for n in ("w_gate_2", "w_up_2", "w_down_2"))

    with ExitStack() as ctx:
        def sb(name, shape, dt=F32):
            return ctx.enter_context(nc.sbuf_tensor(name, shape, dt))

        def sem(name):
            return ctx.enter_context(nc.semaphore(name))

        ident, tri, flip, ones = (sb(n, [P, P]) for n in ("ident", "tri", "flip", "ones"))
        cols = sb("cols", [P, N_ROWS_A + N_ROWS_B])
        cos, sin = sb("cos", [P, TT, 8]), sb("sin", [P, TT, 8])
        unit = sb("unit", [P, 1])
        order = sb("order", [P, 8])
        iota, token = sb("iota", [P, P]), sb("token", [P, TT])
        ffn_kp = sb("ffn_kp", [P, KC])
        sinks = sb("sinks", [P, 4])
        q_g, k_g, ik_g = sb("q_g", [P, HD]), sb("k_g", [P, HD]), sb("ik_g", [P, HD])
        dt_b, a_log, d_skip = sb("dt_b", [P, 32]), sb("a_log", [P, 32]), sb("d_skip", [P, 32])
        b_rt = sb("b_rt", [P, 36])
        w_rt = sb("w_rt", [P, KC, 36])
        st = sb("st", [P, 10, 64])
        top = sb("top", [P, 2, 8])
        sm = sb("sm", [P, 6, 4, 4])
        ps = [ctx.enter_context(nc.psum_tensor(f"ps{i}", [P, 4, 512], F32)) for i in range(2)]

        p_s, p_t, p_v, p_yt = ps[0], ps[1][:, 0:2, :], ps[1][:, 2, :], ps[1][:, 3, :]

        base = -(-nc.sbuf_base // 64) * 64
        assert base + ARENA * 1024 <= nc.sbuf_top, (base, nc.sbuf_top)

        def at(name, kib, shape, dt=F32):
            size = int(np.prod(shape[1:])) * 4
            assert kib * 1024 + size <= ARENA * 1024, name
            return nc.alloc_sbuf_tensor_at(name, shape, dt, offset=base + int(kib * 1024))

        xres = at("xres", 0, [P, TT, D])
        hi = at("hi", 118, [P, KC, S], F32R)
        lo = at("lo", 134, [P, KC, S], F32R)
        stage = at("stage", 150, [P, 2, HALF, 512])
        w_hi, w_lo = at("w_hi", 166, [P, 2, HALF, 512], F32R), at("w_lo", 182, [P, 2, HALF, 512], F32R)
        xn = at("xn", 16, [P, TT, D])
        pr1, pT1 = at("pr1", 16, [P, 2, 4, 256]), at("pT1", 24, [P, 4, 256])
        vtmp = at("vtmp", 16, [P, TT, 512])
        yT = at("yT", 32, [P, KC, S])
        relb, bucket = at("relb", 32, [32, 4]), at("bucket", 33, [32, 384])
        outside, brow = at("outside", 35, [4, 384]), at("brow", 37, [4, 384])
        rows_a, rows_b = at("rows_a", 40, [N_ROWS_A, P]), at("rows_b", 41, [N_ROWS_B, P])
        uT, vt = at("uT", 48, [P, 4, S]), at("vt", 56, [P, TT, 512])
        zT = at("zT", 64, [P, KC, S])
        memb = at("memb", 64, [P, 2, D])
        qT1, mqT = at("qT1", 80, [P, 2, S]), at("mqT", 84, [P, 2, S])
        kT1, sv1 = [at("kT1_lower", 88, [P, S]), at("kT1_upper", 28, [P, S])], at("sv1", 90, [P, TT, P])
        mkT, mv = [at("mkT_lower", 92, [P, 2, MEM]), at("mkT_upper", 116, [P, 2, MEM])], at("mv", 94, [P, 2, MEM])
        v_g, v_b, b_s = at("v_g", 96, [P, 512]), at("v_b", 98, [P, 512]), at("b_s", 100, [P, 4, P])
        post_g = at("post_g", 102, [P, D])
        wsp, wspT = at("wsp", 106, [P, 4, P]), at("wspT", 108, [P, 4, P])
        bias, bias_r = at("bias", 106, [P, 4, 256]), at("bias_r", 110, [P, 4, 256])
        yt1 = at("yt1", 114, [P, 2, 256])
        sg = at("sg", 0, [P, KC, S])
        qt = at("qt", 16, [P, TT, 1024])
        yah = at("yah", 16, [P, KC, S], F32R)
        iqt, iqT = at("iqt", 32, [P, TT, 512]), at("iqT", 40, [P, 4, S])
        yal = at("yal", 32, [P, KC, S], F32R)
        kvt = at("kvt", 48, [P, TT, 512])
        kT2 = [[at("kT2_lower0", 56, [P, TT, P]), at("kT2_lower1", 58, [P, TT, P])], [kvt[:, :, 0:P], at("kT2_upper1", 90, [P, TT, P])]]
        qT2, sel = at("qT2", 60, [P, 8, S]), at("sel", 76, [P, TT, S])
        yt2, rot = at("yt2", 84, [P, 2, 256]), at("rot", 86, [P, 2, TT, 128])
        ikt = at("ikt", 90, [P, TT, P])
        pT2, pr2 = at("pT2", 92, [P, 4, 512]), at("pr2", 100, [P, 2, 4, 512])
        dtt = at("dtt", 0, [P, 8, TT, 32])
        sqr, rel = at("sqr", 92, [P, TT, 512]), at("rel", 100, [P, 4, 512])
        score, ikT = at("score", 108, [P, 3, 512]), at("ikT", 114, [P, S])
        smt = at("smt", 116, [P, TT, SMALL])
        mT = at("mT", 100, [P, KC, S])
        xd, xe = at("xd", 0, [P, 32, HD]), at("xe", 8, [P, 32, HD])
        yoff = at("yoff", 0, [P, 32, HD])
        xtok = at("xtok", 16, [P, TT, 2048])
        bT, cT, btok = at("bT", 48, [P, 4, S]), at("cT", 56, [P, 4, S]), at("btok", 64, [P, TT, 512])
        cpad, xsT = at("cpad", 72, [P, 4, 3 + S]), at("xsT", 80.125, [P, 4, S])
        decay = at("decay", 72, [P, 32, P])
        state = at("state", 88.25, [P, 2048])
        cb = at("cb", 96.25, [P, 4, P])
        dts = at("dts", 98.25, [P, 3, TT, 32])
        gate_late = at("gate_late", 100, [P, 4, 512])
        gate_early = at("gate_early", 60, [P, 4, 512])
        gate_out = [at(f"gate_out{i}", 100 + 4 * i, [P, TT, 256]) for i in range(4)]
        sgb = at("sgb", 48, [P, KC, S])
        sz = [at(f"sz{g}", k, [P, TT, 512]) for g, k in enumerate((64, 72, 80, 88.25))]
        both = at("both", 64, [P, 4, 512])
        junk3, junk4 = at("junk3", 96.25, [P, 512]), at("junk4", 48, [P, D])
        hT = at("hT", 118, [P, KC, S])
        rt = at("rt", 34, [P, 16, TT, 36])
        hot = at("hot", 44, [P, 2, TT, N_EXP])
        cnt = at("cnt", 32, [P, 8, 32])
        pos = at("pos", 33, [P, 4, 2 * TT])
        pos_u = nc.alloc_sbuf_tensor_at("pos_u", [P, 2 * TT], mybir.dt.uint32, offset=base + 33 * 1024 + 128)
        tab_u = nc.alloc_sbuf_tensor_at("tab_u", [P, SLOTS], mybir.dt.uint32, offset=base + 33 * 1024 + 256)
        slot_e = nc.alloc_sbuf_tensor_at("slot_e", [1, SLOTS], mybir.dt.int32, offset=base + 33 * 1024 + 512)
        slot_f = at("slot_f", 45, [1, SLOTS])
        hot_r, hot_b = at("hot_r", 134, [P, 2 * TT, P]), at("hot_b", 138, [P, 2 * TT, SLOTS])
        ends = at("ends", 140, [1, SLOTS, N_EXP])
        w_gu = [at(f"w_gu{i}", 46 + 24 * i, [P, 2, KC, HID]) for i in range(3)]
        w_dn = [at(f"w_dn{i}", 62 + 24 * i, [P, 2, D]) for i in range(3)]
        xg = [at(f"xg{i}", 134 + 4 * i, [P, D]) for i in range(3)]
        xT = at("xT", 146, [P, KC, P])
        yg = [at(f"yg{i}", 150 + 4 * i, [P, D]) for i in range(3)]
        sa, act, actT = at("sa", 162, [P, HID]), at("act", 163, [P, HID]), at("actT", 164, [P, 2, P])
        back = at("back", 46, [P, 2 * TT, D])

        def gain(name, k):
            return cols[:, ROWS_A[name] + k:ROWS_A[name] + k + 1]

        x_in, mem_in, par_in, more_in = sem("x_in"), sem("mem_in"), sem("par_in"), sem("more_in")
        w_in_sem = [sem("w_even_in"), sem("w_odd_in")]
        w_split = sem("w_split")
        w_used = sem("w_used")
        turn_full = sem("turn_full")
        turn_free = [sem("turn_free0"), sem("turn_free1")]
        cols_ready, setup_done = sem("cols_ready"), sem("setup_done")
        rms_ready, rows_ready = sem("rms_ready"), sem("rows_ready")
        tile_ready, root_ready, recip_ready, tile_rows = (sem(n) for n in ("tile_ready", "root_ready", "recip_ready", "tile_rows"))
        hi_ready, lo_ready = sem("hi_ready"), sem("lo_ready")
        brow_ready, bias_out, bias_in = sem("brow_ready"), sem("bias_out"), sem("bias_in")
        wspT_ready, u_ready, v_ready, v_normed = sem("wspT_ready"), sem("u_ready"), sem("v_ready"), sem("v_normed")
        ya_ready = sem("ya_ready")
        qkv1_ready, mkv_ready, z1_ready = sem("qkv1_ready"), sem("mkv_ready"), sem("z1_ready")
        max_ready, exp_ready = sem("max_ready"), sem("exp_ready")
        s_full, s_free, t_full, v_full, yt_full = (sem(n) for n in ("s_full", "s_free", "t_full", "v_full", "yt_full"))
        pT_ready = [sem("pT_ready_first"), sem("pT_ready_second")]
        yt_ready, yT_ready = sem("yt_ready"), sem("yT_ready")
        ss_ready = sem("ss_ready")
        wo_ready, x1_saved, x1_back = sem("wo_ready"), sem("x1_saved"), sem("x1_back")
        iq_ready, small_ready, kv_ready, q_ready = sem("iq_ready"), sem("small_ready"), sem("kv_ready"), sem("q_ready")
        iq_rows, k_rows, q_rows = sem("iq_rows"), sem("k_rows"), sem("q_rows")
        iqT_ready, kT_ready, qT_ready, rel_ready = sem("iqT_ready"), sem("kT_ready"), sem("qT_ready"), sem("rel_ready")
        sq_q_ready, sq_q_used = sem("sq_q_ready"), sem("sq_q_used")
        sq_ready, rel_used, sga_ready = sem("sq_ready"), sem("rel_used"), sem("sga_ready")
        conv_in, conv_out, xs_ready, xtok_ready = sem("conv_in"), sem("conv_out"), sem("xs_ready"), sem("xtok_ready")
        dt_step, dt_act = sem("dt_step"), sem("dt_act")
        acs_ready, e_ready, m_ready = sem("acs_ready"), sem("e_ready"), sem("m_ready")
        xd_ready, xe_ready, st_ready = sem("xd_ready"), sem("xe_ready"), sem("st_ready")
        mT_saved, mT_back, ssd_done, sgb_back = sem("mT_saved"), sem("mT_back"), sem("ssd_done"), sem("sgb_back")
        sz_back = [sem(f"sz_back{g}") for g in range(2)]
        gate_saved = [sem(f"gate_saved{i}") for i in range(6)]
        mT_half, sz_ready, gated, y_rows = sem("mT_half"), sem("sz_ready"), sem("gated"), sem("y_rows")
        rt_step, rt_act = sem("rt_step"), sem("rt_act")
        rows_saved, slots_ready, table_ready = sem("rows_saved"), sem("slots_ready"), sem("table_ready")
        gu_in, dn_in, xg_in, y_out = ([sem(f"{n}{i}") for i in range(3)] for n in ("gu_in", "dn_in", "xg_in", "y_out"))
        turned, xT_ready, gu_done, sa_ready, act_ready = (sem(n) for n in ("turned", "xT_ready", "gu_done", "sa_ready", "act_ready"))
        act_turned, actT_ready, dn_done, y_ready = (sem(n) for n in ("act_turned", "actT_ready", "dn_done", "y_ready"))
        back_in = [sem(f"back_in{t}") for t in range(TT)]
        out_ready = sem("out_ready")
        out_done = sem("out_done")
        mT_ready = sem("mT_ready")
        yal_ready = sem("yal_ready")

        JOBS = 38
        JOB_MQ, JOB_SMALL, JOB_Z = 4, 10, 26

        block = ctx.enter_context(nc.Block())

        params = [
            (ident[:], d["c_ident"]),
            (rows_b[:], d["conv_w_2"][0].rearrange("k (c p) -> (k c) p", p=P)),
        ]
        for name, key in (("pre", "pre_norm_g"), ("mem", "mem_norm_g"), ("attn", "attn_norm_2"), ("ffn", "ffn_norm_2"),
                          ("ssd", "ssd_norm_2"), ("conv_b", "conv_b_2")):
            v = d[key][0].rearrange("(c p) -> c p", p=P)
            params.append((rows_a[ROWS_A[name]:ROWS_A[name] + v.shape[0], :], v))
        PARAMS = 16 * len(params)
        more_params = [
            (tri[:], d["c_tri"]), (flip[:], d["c_flip"]), (bucket[:], d["c_bucket"]), (outside[:], d["c_outside"]),
            (relb[:], d["rel_bias"]), (wsp[:], d["w_spatial"][0].rearrange("g t s -> t g s")),
            (cos[:], d["c_cos"].rearrange("(t p) f -> p t f", p=P)), (sin[:], d["c_sin"].rearrange("(t p) f -> p t f", p=P)),
            (order[:], d["c_order"]), (iota[:], d["c_iota"]), (token[:], d["c_token"]),
            (ffn_kp[:], d["ffn_norm_2"][0].rearrange("(p k) -> p k", p=P)),
            (w_rt[:, :, 0:4], d["w_route_group_2"][0].rearrange("(k p) n -> p k n", p=P)),
            (w_rt[:, :, 4:36], d["w_route_expert_2"][0].rearrange("(k p) n -> p k n", p=P)),
        ]
        for dst, v in ((v_g[:], d["v_norm_g"][0]), (v_b[:], d["v_norm_b"][0]), (post_g[:], d["post_norm_g"][0]),
                       (b_s[:], d["b_spatial"][0].rearrange("g t -> (g t)")),
                       (sinks[:], d["attn_sinks"][0]), (q_g[:], d["q_norm_2"][0]), (k_g[:], d["k_norm_2"][0]),
                       (ik_g[:], d["idx_k_norm_2"][0]), (dt_b[:], d["dt_bias_2"][0]), (a_log[:], d["a_log_2"][0]),
                       (d_skip[:], d["d_skip_2"][0]), (b_rt[:, 0:4], d["b_route_group_2"][0]),
                       (b_rt[:, 4:36], d["b_route_expert_2"][0])):
            src = v.partition_broadcast(P)
            if len(dst.shape) == 3:
                dst = dst.rearrange("p g t -> p (g t)")
            more_params.append((dst, src))
        MORE_PARAMS = 16 * len(more_params)

        @block.sync
        def _(sp):
            tiles = [0]

            def tile(parts):
                n = tiles[0]
                if n >= 2:
                    sp.wait_ge(w_split, n - 1)
                for dst, src in parts(stage[:, n % 2]):
                    sp.dma_start(dst, src).then_inc(w_in_sem[n % 2], 16)
                tiles[0] += 1

            def halves(w, r0, c0, ncols=512):
                for h in range(2):
                    src = w[r0 + 512 * h:r0 + 512 * (h + 1), c0:c0 + ncols].rearrange("(k p) n -> p k n", p=P)
                    tile(lambda t, src=src: [(t[:, a:a + 2, 0:ncols], src[:, a:a + 2, :]) for a in (0, 2)])

            for dst, src in params[1::2]:
                sp.dma_start(dst, src).then_inc(par_in, 16)
            sp.dma_start(memb[:], d["mem"][0].rearrange("(t p) n -> p t n", p=P)).then_inc(mem_in, 16)
            sp.wait_ge(par_in, PARAMS)
            halves(d["w_mem_kv"][0], 0, 0)
            sp.dma_start(xres[:], d["x"][0].rearrange("(t p) n -> p t n", p=P)).then_inc(x_in, 16)
            for c0, n in ((SQKV, 512), (A_V, 512), (A_U, 512)):
                halves(w1, 0, c0, n)
            sp.wait_ge(brow_ready, 1)
            sp.dma_start(bias_dram, brow[:]).then_inc(bias_out, 16)
            sp.wait_ge(bias_out, 16)
            for h in range(4):
                shifted = bass.AP(bias_dram.tensor, h * 384, [[1, P], [1, 256]])
                sp.dma_start(bias_r[:, h, :], shifted).then_inc(bias_in, 16)
            for c0, n in ((MQ, 256), (Z1, 512), (Z1 + 512, 512)):
                halves(w1, 0, c0, n)
            for c in range(2):
                halves(d["w_out"][0], 0, 512 * c)
            halves(w2, 0, IQ2)
            for h in range(2):
                rows = slice(512 * h, 512 * (h + 1))
                a = w2[rows, IK2:IK2 + 72].rearrange("(k p) n -> p k n", p=P)
                b = w2[rows, DT2:DT2 + 32].rearrange("(k p) n -> p k n", p=P)
                tile(lambda t, a=a, b=b: [(t[:, :, 0:72], a), (t[:, :, 72:SMALL], b)])
            for c0 in (KV2, Q2, Q2 + 512, GA2, GB2, GA2 + 512):
                halves(w2, 0, c0)
                if c0 == KV2:
                    sp.wait_ge(tile_ready, TT)
                    sp.dma_start(x1_dram.rearrange("(t p) n -> p t n", p=P), xres[:]).then_inc(x1_saved, 16)
            for c in range(2):
                halves(d["w_attn_branch_2"][0], 0, 512 * c)
            for c0 in (XBC2 + 2048, XBC2 + 2560, XBC2):
                halves(w2, 0, c0)
            sp.wait_ge(mT_half, 2)
            sp.dma_start(mT_dram, mT[:]).then_inc(mT_saved, 16)
            for c0 in (XBC2 + 512, XBC2 + 1024, XBC2 + 1536, GB2 + 512):
                halves(w2, 0, c0)
            for i in range(4):
                halves(w2, 0, Z2 + 256 * i, 256)
            for g in (2, 3):
                halves(w2, 0, Z2 + 512 * g)
            sp.wait_ge(ssd_done, 1)
            for i in range(6):
                sp.wait_ge(gate_saved[i], 16)
            for g in range(2):
                sp.dma_start(sz[g][:], gates_dram[2 + g]).then_inc(sz_back[g], 16)
            for i in range(2):
                sp.dma_start(sgb[:, 4 * i:4 * i + 4, :], gates_dram[i]).then_inc(sgb_back, 16)
            sp.wait_ge(mT_saved, 16)
            sp.dma_start(mT[:], mT_dram).then_inc(mT_back, 16)
            sp.wait_ge(x1_saved, 16)
            sp.dma_start(xres[:], x1_dram.rearrange("(t p) n -> p t n", p=P)).then_inc(x1_back, 16)
            for r in range(2):
                for c in range(2):
                    halves(d["w_ssd_branch_2"][0], 1024 * r, 512 * c)
            for c in range(2):
                halves(d["w_out_2"][0], 0, 512 * c)
            assert tiles[0] == 2 * JOBS

            sp.wait_ge(tile_rows, 2 * TT)
            sp.dma_start(rows_dram.rearrange("(t p) n -> p t n", p=P), xn[:]).then_inc(rows_saved, 16)

            def gate_up(e, b):
                for c, w in ((0, e_gate), (1, e_up)):
                    sp.dma_start(w_gu[b][:, c], w[bass.ds(e, 1)].rearrange("e (p k) n -> p (e k) n", p=P)).then_inc(gu_in[b], 16)

            def down(e, b):
                sp.dma_start(w_dn[b][:], e_down[bass.ds(e, 1)].rearrange("e (f p) n -> p (e f) n", p=P)).then_inc(dn_in[b], 16)

            def expert(s):
                return nc.sync.value_load(slot_e[0:1, bass.ds(s, 1)], min_val=0, max_val=N_EXP - 1)

            def store(s, b):
                sp.dma_start(y_dram[bass.ds(s * P, P), :], yg[b][:]).then_inc(y_out[b], 16)

            sp.wait_ge(slots_ready, 1)
            for s in range(3):
                e = expert(s)
                if s == 1:
                    sp.wait_ge(xg_in[0], 16)
                gate_up(e, s)
                down(e, s)
            rounds = SLOTS // 3 - 1
            with sp.Fori(0, rounds) as i:
                for b in range(3):
                    s = 3 * i + b
                    e = expert(s + 3)
                    sp.wait_ge(gu_done, s + 1)
                    gate_up(e, b)
                    sp.wait_ge(dn_done, s + 1)
                    down(e, b)
                    sp.wait_ge(y_ready, s + 1)
                    store(s, b)
            for s in range(3 * rounds, SLOTS):
                sp.wait_ge(y_ready, s + 1)
                store(s, s % 3)
            for t in range(TT):
                sp.wait_ge(out_ready, t + 1)
                sp.dma_start(out[0, P * t:P * (t + 1), :], xres[:, t, :]).then_inc(out_done, 16)
            sp.wait_ge(out_done, 16 * TT)

        @block.gpsimd
        def _(pool):
            def split(b, n):
                hi_, lo_, whole = w_hi[:, b, :, 0:n], w_lo[:, b, :, 0:n], stage[:, b, :, 0:n]
                nc.gpsimd.tensor_tensor(hi_, whole, unit[:].unsqueeze(1).broadcast_to([P, HALF, n]), ALU.mult)
                pool.drain()
                nc.gpsimd.tensor_tensor(lo_, whole, hi_.bitcast(F32), ALU.subtract).then_inc(w_split, 1)

            def split_job(i, n=512):
                for b in range(2):
                    pool.wait_ge(w_in_sem[b], 32 * i + 32)
                    pool.wait_ge(w_used, 2 * i + (b - 1))
                    split(b, n)

            nc.gpsimd.memset(unit[:], 1.0)
            pool.drain()
            for b in range(2):
                pool.wait_ge(w_in_sem[b], 32)
                split(b, 512)
            with pool.Fori(1, JOB_MQ) as i:
                split_job(i)
            split_job(JOB_MQ, 256)
            with pool.Fori(JOB_MQ + 1, JOB_SMALL) as i:
                split_job(i)
            split_job(JOB_SMALL, SMALL)
            with pool.Fori(JOB_SMALL + 1, JOB_Z) as i:
                split_job(i)
            with pool.Fori(JOB_Z, JOB_Z + 4) as i:
                split_job(i, 256)
            with pool.Fori(JOB_Z + 4, JOBS) as i:
                split_job(i)
            pool.wait_ge(rows_saved, 16)
            pool.wait_ge(table_ready, 1)
            for s in range(SLOTS):
                if s >= 3:
                    pool.wait_ge(turned, s - 2)
                nc.gpsimd.indirect_dma_start(xg[s % 3][:], None, rows_dram, bass.IndirectOffsetOnAxis(ap=tab_u[:, s:s + 1], axis=0))\
                    .then_inc(xg_in[s % 3], 16)
            for b in range(3):
                pool.wait_ge(y_out[b], 16 * len(range(b, SLOTS, 3)))
            for t in range(TT):
                for k in range(2):
                    i = TT * k + t
                    nc.gpsimd.indirect_dma_start(back[:, i, :], None, y_dram, bass.IndirectOffsetOnAxis(ap=pos_u[:, i:i + 1], axis=0))\
                        .then_inc(back_in[t], 16)

        @block.tensor
        def _(pe):
            turns = Turns(pe, turn_full, turn_free)
            tile = [0, 0]

            def parts(t, *ix):
                return t[0][ix], t[1][ix]

            x_parts, w_parts, ya_parts = (hi, lo), (w_hi, w_lo), (yah, yal)
            everything = slice(None)

            def weights():
                b = tile[0] % 2
                pe.wait_ge(w_split, tile[1] + tile[0] + 1)
                tile[0] += 1
                return b

            def features(x=x_parts, chunks=4, n=S, more=None, ready=None):
                s = turns.take()
                for half in range(2):
                    if ready:
                        pe.wait_ge(lo_ready, ready - 1 + half)
                    b = weights()
                    for m in range(chunks):
                        for k in range(HALF):
                            w = parts(w_parts, everything, b, k)
                            w = tuple(a[:, P * m:P * (m + 1)] for a in w)
                            last = matmul3(pe, ps[s][:, m, 0:n], w, parts(x, everything, HALF * half + k, slice(0, n)),
                                           half == 0 and k == 0, half == 1 and k == HALF - 1)
                    if more:
                        last = more(s, b, half)
                    last.then_inc(w_used, 1)
                pe.drain().then_inc(turn_full, 1)

            def tokens(x=x_parts, n=512, tiles=TT, ready=None):
                s = turns.take()
                for half in range(2):
                    if ready:
                        pe.wait_ge(lo_ready, ready - 1 + half)
                    b = weights()
                    for t in range(tiles):
                        for k in range(HALF):
                            last = matmul3(pe, ps[s][:, t, 0:n],
                                           parts(x, everything, HALF * half + k, slice(P * t, P * (t + 1))),
                                           parts(w_parts, everything, b, k, slice(0, n)),
                                           half == 0 and k == 0, half == 1 and k == HALF - 1)
                    last.then_inc(w_used, 1)
                pe.drain().then_inc(turn_full, 1)

            def turn_rows(rows, tiles=TT, chunks=KC):
                for c0 in range(0, chunks, 4):
                    s = turns.take()
                    for c in range(4):
                        for t in range(tiles):
                            last = pe.transpose(ps[s][:, c, P * t:P * (t + 1)], rows(t, c0 + c), ident[:])
                    last.then_inc(turn_full, 1)

            def turn_tiles(rows, base):
                for c0 in (0, 4):
                    s = turns.take()
                    for t in range(TT):
                        pe.wait_ge(tile_rows, base + t + 1)
                        for c in range(4):
                            last = pe.transpose(ps[s][:, c, P * t:P * (t + 1)], rows(t, c0 + c), ident[:])
                    last.then_inc(turn_full, 1)

            pe.wait_ge(par_in, PARAMS)
            s = turns.take()
            pe.transpose(ps[s][:, 0, 0:N_ROWS_A], rows_a[:], ident[0:N_ROWS_A, 0:N_ROWS_A])
            pe.transpose(ps[s][:, 0, N_ROWS_A:N_ROWS_A + N_ROWS_B], rows_b[:], ident[0:N_ROWS_B, 0:N_ROWS_B])\
                .then_inc(turn_full, 1)

            pe.wait_ge(rows_ready, 1)
            turn_rows(lambda t, c: xn[:, t, P * c:P * (c + 1)], tiles=2)

            def mem_values(s, b, half):
                for t in range(2):
                    for k in range(HALF):
                        last = matmul3(pe, ps[s][:, 2 + t, 0:MEM],
                                       parts(x_parts, everything, HALF * half + k, slice(P * t, P * (t + 1))),
                                       parts(w_parts, everything, b, k, slice(256, 512)),
                                       half == 0 and k == 0, half == 1 and k == HALF - 1)
                return last

            features(chunks=2, n=MEM, more=mem_values, ready=2)

            pe.wait_ge(rows_ready, 2)
            turn_rows(lambda t, c: xn[:, t, P * c:P * (c + 1)])

            def swa_values(s, b, half):
                for t in range(TT):
                    for k in range(HALF):
                        last = matmul3(pe, ps[s][:, 3, P * t:P * (t + 1)],
                                       parts(x_parts, everything, HALF * half + k, slice(P * t, P * (t + 1))),
                                       parts(w_parts, everything, b, k, slice(384, 512)),
                                       half == 0 and k == 0 and t == 0, half == 1 and k == HALF - 1 and t == TT - 1)
                return last

            features(chunks=3, more=swa_values, ready=4)
            pe.wait_ge(more_in, MORE_PARAMS)
            s = turns.take()
            pe.matmul(ps[s][0:4, 1, 0:384], relb[:], bucket[:], start=True, stop=True)
            for g in range(4):
                last = pe.transpose(ps[s][:, 2, P * g:P * (g + 1)], wsp[:, g, :], ident[:])
            last.then_inc(turn_full, 1)
            tokens()
            features()
            features(chunks=2)
            features()

            pe.wait_ge(v_normed, 1)
            pe.wait_ge(wspT_ready, 1)
            s = turns.take()
            for g in range(4):
                for n in range(TT):
                    last = pe.matmul(ps[s][:, g, P * n:P * (n + 1)], vt[:, n, P * g:P * (g + 1)], wspT[:, g, :],
                                     start=True, stop=True)
            last.then_inc(turn_full, 1)

            pe.wait_ge(bias_in, 64)
            s = turns.take()
            for h in range(4):
                last = pe.matmul(ps[s][:, h, 0:256], flip[:], bias_r[:, h, :], start=True, stop=True)
            last.then_inc(turn_full, 1)
            features()

            def attention(batches, scores, values, nkb, pr, pT, yt, base, yt_free):
                turns.settle()
                for i in range(batches + 3):
                    if i < batches:
                        if base + i > 0:
                            pe.wait_ge(s_free, base + i)
                        scores(i, p_s).then_inc(s_full, 1)
                    for half in range(2):
                        b = i - 2
                        if 0 <= b < batches:
                            pe.wait_ge(pT_ready[half], base + b + 1)
                            if base + b > 0 and half == 0:
                                pe.wait_ge(yt_ready, base + b)
                            for h in (2 * half, 2 * half + 1):
                                for kb in range(nkb(b)):
                                    last = pe.matmul(p_v[:, HD * h:HD * (h + 1)], pT(b)[:, h, P * kb:P * (kb + 1)],
                                                     values(b, h, kb), start=(kb == 0), stop=(kb == nkb(b) - 1))
                            if half == 1:
                                last.then_inc(v_full, 1)
                        b = i - 1
                        if 0 <= b < batches:
                            if half == 0:
                                pe.wait_ge(exp_ready, base + b + 1)
                            if base + b + half > 0:
                                pe.wait_ge(pT_ready[1 - half], base + b + half)
                            for h in (2 * half, 2 * half + 1):
                                for kb in range(nkb(b)):
                                    last = pe.transpose(p_t[:, h % 2, P * kb:P * (kb + 1)],
                                                        pr(b)[:, h, P * kb:P * (kb + 1)], ident[:])
                            last.then_inc(t_full, 1)
                    b = i - 3
                    if 0 <= b < batches:
                        pe.wait_ge(yt_ready, base + b + 1)
                        if base + b > 0:
                            yt_free(b)
                        for c in range(2):
                            last = pe.transpose(p_yt[:, P * c:P * (c + 1)], yt[:, b % 2, P * c:P * (c + 1)], ident[:])
                        last.then_inc(yt_full, 1)
                pe.wait_ge(s_free, base + batches)
                yt_free(batches)

            def scores1(b, s):
                n = b % 4
                for h in range(4):
                    if b < 4:
                        q, k = qT1[:, h % 2, P * n:P * (n + 1)], kT1[h // 2][:, P * max(n - 1, 0):P * (n + 1)]
                    else:
                        q, k = mqT[:, h // 2, P * n:P * (n + 1)], mkT[h % 2][:, h // 2, :]
                    last = pe.matmul(s[:, h, 0:k.shape[1]], q, k, start=True, stop=True)
                return last

            def values1(b, h, kb):
                if b < 4:
                    return sv1[:, max(b - 1, 0) + kb, HD * (h // 2):HD * (h // 2 + 1)]
                return mv[:, kb, HD * h:HD * (h + 1)]

            pe.wait_ge(qkv1_ready, 2)
            pe.wait_ge(mkv_ready, 1)
            attention(8, scores1, values1, lambda b: 1 if b == 0 else 2, lambda b: pr1[:, b % 2], lambda b: pT1, yt1, 0,
                      lambda b: pe.wait_ge(yT_ready, b))

            tokens(ready=6)
            tokens()

            turn_tiles(lambda t, c: qt[:, t, P * c:P * (c + 1)], 0)
            tokens(ready=8)
            tokens(n=SMALL)
            tokens()
            pe.wait_ge(iq_rows, 1)
            turn_rows(lambda t, c: iqt[:, t, P * c:P * (c + 1)], chunks=4)
            pe.wait_ge(iq_rows, 2)
            s = turns.take()
            for t in range(TT):
                last = pe.transpose(ps[s][:, 0, P * t:P * (t + 1)], ikt[:, t, :], ident[:])
            last.then_inc(turn_full, 1)
            pe.wait_ge(iqT_ready, 2)
            for n in range(1, TT):
                for h4 in range(2):
                    s = turns.take()
                    for h in range(4):
                        i = 4 * h4 + h
                        lanes = slice(HD * (i % 2), HD * (i % 2 + 1))
                        last = pe.matmul(ps[s][:, h, 0:P * (n + 1)], iqT[lanes, i // 2, P * n:P * (n + 1)],
                                         ikT[lanes, 0:P * (n + 1)], start=True, stop=True)
                    last.then_inc(turn_full, 1)
                if n < TT - 1:
                    tokens()
            pe.wait_ge(k_rows, 1)
            s = turns.take()
            for c in range(2):
                for t in range(TT):
                    last = pe.transpose(ps[s][:, c, P * t:P * (t + 1)], kvt[:, t, P * c:P * (c + 1)], ident[:])
            last.then_inc(turn_full, 1)
            features()
            features()
            pe.wait_ge(q_rows, 1)
            turn_rows(lambda t, c: qt[:, t, P * c:P * (c + 1)])
            features()

            def scores2(b, s):
                n, g = query_block(b), b % 4
                for i in range(4):
                    last = pe.matmul(s[:, i, 0:P * (n + 1)].rearrange("p (t k) -> p t k", k=P), qT2[:, 4 * (g // 2) + i, P * n:P * (n + 1)],
                                     kT2[g % 2][g // 2][:, 0:n + 1, :], start=True, stop=True)
                return last

            pe.wait_ge(kT_ready, 1)
            pe.wait_ge(qT_ready, 2)
            attention(16, scores2, lambda b, h, kb: kvt[:, kb, 256 + HD * (b % 4):256 + HD * (b % 4 + 1)],
                      lambda b: query_block(b) + 1, lambda b: pr2[:, b % 2], lambda b: pT2, yt2, 8,
                      lambda b: pe.wait_ge(yal_ready, b) if b else pe.wait_ge(yT_ready, 8))
            pe.wait_ge(yal_ready, 16)
            features(ya_parts)
            features(ya_parts)

            def turn_back(n):
                pe.wait_ge(xs_ready, n)
                s = turns.take()
                src = bT if n == 1 else xsT
                for t in range(TT):
                    for c in range(4):
                        last = pe.transpose(ps[s][:, t, P * c:P * (c + 1)], src[:, c, P * t:P * (t + 1)], ident[:])
                last.then_inc(turn_full, 1)

            features()
            features()
            turn_back(1)
            features()
            for j in range(4):
                features()
                turn_back(3 + j)

            pe.wait_ge(dt_step, 3)
            def cumulative(c):
                tok = slice(P * c, P * (c + 1))
                s = turns.take()
                pe.matmul(ps[s][:, 0, 0:32], tri[:], dts[:, 1, c, :], start=True, stop=True)
                pe.matmul(ps[s][:, 0, 32:64], ones[:], dts[:, 1, c, :], start=True, stop=True)
                for g in range(4):
                    last = pe.matmul(ps[s][:, 1, P * g:P * (g + 1)], bT[:, g, tok], cT[:, g, tok], start=True, stop=True)
                last.then_inc(turn_full, 1)

            cumulative(0)
            for c in range(TT):
                tok = slice(P * c, P * (c + 1))
                for half in range(2):
                    s = turns.take()
                    for h in range(16):
                        col = dts[:, 1, c, 16 * half + h:16 * half + h + 1].broadcast_to([P, P])
                        last = pe.matmul(ps[s][:, h // 4, P * (h % 4):P * (h % 4 + 1)], col, tri[:], start=True, stop=True)
                    last.then_inc(turn_full, 1)
                tokens(n=256)
                pe.wait_ge(m_ready, 4 * (c + 1))
                pe.wait_ge(xd_ready, c + 1)
                s = turns.take()
                for h in range(32):
                    last = pe.matmul(ps[s][:, h // 8, HD * (h % 8):HD * (h % 8 + 1)], decay[:, h, :], xd[:, h, :],
                                     start=True, stop=True)
                last.then_inc(turn_full, 1)
                if c > 0:
                    pe.wait_ge(st_ready, c)
                    s = turns.take()
                    for g in range(4):
                        last = pe.matmul(ps[s][:, g, :], cT[:, g, tok], state[:, 512 * g:512 * (g + 1)], start=True, stop=True)
                    last.then_inc(turn_full, 1)
                if c < TT - 1:
                    cumulative(c + 1)
                    pe.wait_ge(xe_ready, c + 1)
                    s = turns.take()
                    for g in range(4):
                        last = pe.matmul(ps[s][:, g, :], btok[:, c, P * g:P * (g + 1)], xe[:, 8 * g:8 * (g + 1), :],
                                         start=True, stop=True)
                    last.then_inc(turn_full, 1)

            tokens()
            tokens()
            for r in range(2):
                pe.wait_ge(y_rows, r + 1)
                turn_rows(lambda t, c, r=r: xtok[:, t, 1024 * r + P * c:1024 * r + P * (c + 1)])
                features(ready=10 + 2 * r)
                features()
            tokens(ready=14)
            tokens()

            turn_tiles(lambda t, c: xn[:, t, P * c:P * (c + 1)], TT)
            s = turns.take()
            for half, (ready, count) in enumerate(((hi_ready, 60), (lo_ready, 15))):
                pe.wait_ge(ready, count)
                for t in range(TT):
                    for k in range(HALF * half, HALF * (half + 1)):
                        last = pe.matmul(ps[s][:, t, 0:36], hT[:, k, P * t:P * (t + 1)], w_rt[:, k, :],
                                         start=(k == 0), stop=(k == KC - 1))
            last.then_inc(turn_full, 1)
            pe.wait_ge(rt_step, 1)
            s = turns.take()
            for t in range(TT):
                for u in range(t):
                    pe.matmul(ps[s][:, 0, 32 * t:32 * (t + 1)], ones[:], rt[:, 10, u, 0:32], start=(u == 0), stop=False)
                pe.matmul(ps[s][:, 0, 32 * t:32 * (t + 1)], tri[:], rt[:, 10, t, 0:32], start=(t == 0), stop=True)
            for t in range(TT):
                last = pe.matmul(ps[s][:, 1, 0:32], ones[:], rt[:, 10, t, 0:32], start=(t == 0), stop=(t == TT - 1))
            last.then_inc(turn_full, 1)
            pe.wait_ge(rt_step, 3)
            s = turns.take()
            for i in range(2 * TT):
                last = pe.matmul(ps[s][:, 0, 0:SLOTS], hot_r[:, i, :], hot_b[:, i, :], start=(i == 0), stop=(i == 2 * TT - 1))
            last.then_inc(turn_full, 1)

            p_gu, p_act, p_rows, p_dn = ps[0][:, 0, :], ps[0][:, 1, 0:2 * P], ps[0][:, 2:4, :], ps[1][:, 0:2, :]

            def turn_slot(s, b, first=False):

                for k in range(KC):
                    last = pe.transpose(p_rows[:, k // 4, P * (k % 4):P * (k % 4 + 1)], xg[b][:, k:D:KC], ident[:])
                last.then_inc(turned, 1)

            def project(b):
                for k in range(KC):
                    last = pe.matmul(p_gu, xT[:, k, :], w_gu[b][:, :, k, :], start=(k == 0), stop=(k == KC - 1))
                last.then_inc(gu_done, 1)

            def down(s, b):
                pe.wait_ge(actT_ready, s + 1)
                for c in range(2):
                    for f in range(2):
                        last = pe.matmul(p_dn[:, c, :], actT[:, f, :], w_dn[b][:, f, 512 * c:512 * (c + 1)], start=(f == 0), stop=(f == 1))
                last.then_inc(dn_done, 1)

            pe.wait_ge(table_ready, 1)
            pe.wait_ge(xg_in[0], 16)
            turn_slot(0, 0)
            rounds = (SLOTS - 1) // 3

            def step(s, b, arrivals, next_arrivals, first=False, last=False):
                pe.wait_ge(xT_ready, s + 1)
                pe.wait_ge(gu_in[b], 32 * arrivals)
                if not first:
                    pe.wait_ge(act_ready, s)
                project(b)
                if not last:
                    n = (b + 1) % 3
                    pe.wait_ge(xg_in[n], 16 * next_arrivals)
                    turn_slot(s + 1, n)
                if not first:
                    m = (b - 1) % 3
                    pe.wait_ge(dn_in[m], 16 * (arrivals if m < b else arrivals - 1))
                    if not (isinstance(s, int) and s == 1):
                        pe.wait_ge(y_ready, s - 1)
                    down(s - 1, m)
                pe.wait_ge(act_ready, s + 1)
                for f in range(2):
                    t = pe.transpose(p_act[:, P * f:P * (f + 1)], act[:, P * f:P * (f + 1)], ident[:])
                t.then_inc(act_turned, 1)

            step(0, 0, 1, 1, first=True)
            step(1, 1, 1, 1)
            with pe.Fori(0, (SLOTS - 3) // 3) as i:
                for j in (2, 3, 4):
                    step(3 * i + j, j % 3, i + (1 + j // 3), i + (1 + (j + 1) // 3))
            step(SLOTS - 1, (SLOTS - 1) % 3, SLOTS // 3, None, last=True)
            pe.wait_ge(dn_in[(SLOTS - 1) % 3], 16 * (SLOTS // 3))
            pe.wait_ge(y_ready, SLOTS - 1)
            down(SLOTS - 1, (SLOTS - 1) % 3)

        @block.scalar
        def _(act_eng):
            A = act_eng
            turns = Turns(A, turn_full, turn_free)
            for dst, src in params[0::2]:
                A.dma_start(dst, src).then_inc(par_in, 16)

            def norm(rows, n, junk, k):
                for t in range(n):
                    A.activation(junk, rows(t), ACT.Square, accum_out=st[:, 0, k + t:k + t + 1])
                    A.drain()
                A.drain()
                A.activation(st[:, 1, k:k + n], st[:, 0, k:k + n], ACT.Sqrt, scale=1.0 / D, bias=st[:, 9, 0:1]).then_inc(rms_ready, 1)

            def high_parts(name, first=0, n=S, chunks=KC):
                for c0 in range(0, chunks, 4):
                    s = turns.see()
                    for c in range(4):
                        A.activation(hi[:, c0 + c, 0:n], ps[s][:, c, 0:n], ACT.Copy, scale=gain(name, first + c0 + c))\
                            .then_inc(hi_ready, 1)

            def softmax(b, base, width, src, dst, sinks_too):
                k = b % 4
                A.wait_ge(max_ready, base + b + 1)
                for h in range(4):
                    last = A.activation(dst[:, h, 0:width], src[:, h, 0:width], ACT.Exp, bias=sm[:, 2, k, h:h + 1],
                                        accum_out=sm[:, 1, k, h:h + 1])
                if sinks_too:
                    last = A.activation(sm[:, 4, k, :], sm[:, 3, k, :], ACT.Exp)
                last.then_inc(exp_ready, 1)

            def norm_tiles(rows, dst, junk, k, base):
                for t in range(TT + 1):
                    if t < TT:
                        A.wait_ge(tile_ready, base + t + 1)
                        A.activation(junk, rows(t), ACT.Square, accum_out=st[:, 0, k + t:k + t + 1])
                        A.drain()
                        A.activation(st[:, 1, k + t:k + t + 1], st[:, 0, k + t:k + t + 1], ACT.Sqrt, scale=1.0 / D,
                                     bias=st[:, 9, 0:1]).then_inc(root_ready, 1)
                    if t > 0:
                        A.wait_ge(recip_ready, base + t)
                        A.activation(dst(t - 1), rows(t - 1), ACT.Copy, scale=st[:, 2, k + t - 1:k + t]).then_inc(tile_rows, 1)

            A.wait_ge(setup_done, 1)
            A.wait_ge(mem_in, 16)
            norm(lambda t: memb[:, t, :], 2, yT[:, 6:8, :].rearrange("p c n -> p (c n)"), 0)
            A.wait_ge(cols_ready, 1)
            turns.skip()
            high_parts("mem", n=MEM)
            A.wait_ge(x_in, 16)
            norm(lambda t: xres[:, t, :], TT, yT[:, 6:8, :].rearrange("p c n -> p (c n)"), 4)
            s = turns.see()
            for j in range(2):
                lanes = slice(HD * j, HD * (j + 1))
                A.activation(mkT[j][lanes], ps[s][lanes, 0:2, 0:MEM], ACT.Copy)
            A.activation(mv[:], ps[s][:, 2:4, 0:MEM], ACT.Copy).then_inc(mkv_ready, 1)
            A.drain().then_inc(turn_free[s], 1)
            high_parts("pre")
            for dst, src in more_params:
                A.dma_start(dst, src).then_inc(more_in, 16)
            s = turns.see()
            for h in range(4):
                A.activation(qT1[HD * (h // 2):HD * (h // 2 + 1), h % 2, :], ps[s][HD * (h % 2):HD * (h % 2 + 1), h // 2, :],
                             ACT.Copy, scale=HD ** -0.5)
            for j in range(2):
                lanes = slice(HD * j, HD * (j + 1))
                A.activation(kT1[j][lanes], ps[s][lanes, 2, :], ACT.Copy)
            A.activation(sv1[:], ps[s][:, 3, :].rearrange("p (t n) -> p t n", t=TT), ACT.Copy).then_inc(qkv1_ready, 1)
            A.drain().then_inc(turn_free[s], 1)
            turns.skip()
            s = turns.see()
            A.activation(vt[:], ps[s][:], ACT.Gelu_apprx_tanh).then_inc(v_ready, 1)
            A.drain().then_inc(turn_free[s], 1)
            A.wait_ge(v_ready, 2)
            A.activation(st[:, 4, 0:16], st[:, 3, 0:16], ACT.Sqrt, scale=1.0 / P, bias=st[:, 9, 0:1]).then_inc(rms_ready, 1)
            s = turns.see()
            A.activation(uT[:], ps[s][:], ACT.Gelu_apprx_tanh).then_inc(u_ready, 1)
            A.drain().then_inc(turn_free[s], 1)
            s = turns.see()
            A.activation(mqT[:], ps[s][:, 0:2, :], ACT.Copy, scale=HD ** -0.5).then_inc(qkv1_ready, 1)
            A.drain().then_inc(turn_free[s], 1)
            for c in range(2):
                s = turns.see()
                A.activation(zT[:, 4 * c:4 * c + 4, :], ps[s][:], ACT.Silu).then_inc(z1_ready, 1)
                A.drain().then_inc(turn_free[s], 1)
                if c == 0:
                    turns.skip(2)

            def turned_probabilities(b, base, width, dst):
                A.wait_ge(t_full, 2 * (base + b) + 2)
                A.activation(dst[:, 2:4, 0:width], p_t[:, :, 0:width], ACT.Copy).then_inc(pT_ready[1], 1)

            for i in range(8 + 3):
                if i < 4:
                    softmax(i, 0, P if i == 0 else 256, pr1[:, i % 2], pr1[:, i % 2], True)
                elif i < 8:
                    softmax(i, 0, 256, p_s, pr1[:, i % 2], False)
                    A.drain().then_inc(s_free, 1)
                if i == 1:
                    A.wait_ge(ya_ready, 1)
                    A.activation(hi[:, 0:4, :], yT[:, 0:4, :], ACT.Copy).then_inc(hi_ready, 4)
                if 0 <= i - 1 < 8:
                    turned_probabilities(i - 1, 0, P if i == 1 else 256, pT1)
                b = i - 3
                if b >= 0:
                    A.wait_ge(yt_full, b + 1)
                    c0, n = (4, b) if b < 4 else (6, b - 4)
                    A.activation(yT[:, c0:c0 + 2, P * n:P * (n + 1)],
                                 p_yt[:, 0:256].rearrange("p (c t) -> p c t", c=2), ACT.Copy).then_inc(yT_ready, 1)
            A.wait_ge(z1_ready, 3)
            A.activation(hi[:, 4:8, :], yT[:, 4:8, :], ACT.Copy).then_inc(hi_ready, 4)
            for c in range(2):
                s = turns.see()
                for t in range(TT):
                    A.activation(yT[:, 0, :], ps[s][:, t, :], ACT.Square, accum_out=st[:, 0, 8 + t + 12 * c:9 + t + 12 * c])
                    A.drain()
                if c == 0:
                    A.activation(xn[:, :, 0:512], ps[s][:], ACT.Copy).then_inc(wo_ready, 1)
                    A.drain().then_inc(turn_free[s], 1)
                    A.activation(st[:, 9, 1:2], st[:, 9, 0:1], ACT.Sqrt)
                else:
                    A.drain().then_inc(wo_ready, 1)
            A.wait_ge(ss_ready, 1)
            A.activation(st[:, 1, 8:8 + TT], st[:, 0, 8:8 + TT], ACT.Sqrt, scale=1.0 / D, bias=st[:, 9, 0:1]).then_inc(rms_ready, 1)

            norm_tiles(lambda t: xres[:, t, :], lambda t: qt[:, t, :], iqt[:, 0:2, :].rearrange("p c n -> p (c n)"), 12, 0)
            high_parts("attn")
            s = turns.see()
            A.activation(iqt[:], ps[s][:], ACT.Copy).then_inc(iq_ready, 1)
            A.drain().then_inc(turn_free[s], 1)
            s = turns.see()
            A.activation(smt[:], ps[s][:, :, 0:SMALL], ACT.Copy).then_inc(small_ready, 1)
            A.drain().then_inc(turn_free[s], 1)
            A.wait_ge(sq_ready, 1)
            A.activation(st[:, 4, 16:20], st[:, 3, 16:20], ACT.Sqrt, scale=1.0 / HD, bias=st[:, 9, 0:1]).then_inc(rms_ready, 1)
            s = turns.see()
            A.activation(kvt[:], ps[s][:], ACT.Copy).then_inc(kv_ready, 1)
            A.drain().then_inc(turn_free[s], 1)
            s = turns.see()
            A.activation(iqT[:], ps[s][:], ACT.Copy, scale=HD ** -0.5).then_inc(iqT_ready, 1)
            A.drain().then_inc(turn_free[s], 1)
            s = turns.see()
            A.activation(ikT[:], ps[s][:, 0, :], ACT.Copy).then_inc(iqT_ready, 1)
            A.drain().then_inc(turn_free[s], 1)
            A.wait_ge(sq_ready, 2)
            A.activation(st[:, 4, 20:36], st[:, 3, 20:36], ACT.Sqrt, scale=1.0 / HD, bias=st[:, 9, 0:1]).then_inc(rms_ready, 1)
            for i in range(6):
                s = turns.see()
                n = 1 + i // 2
                if i > 0:
                    A.wait_ge(rel_used, i)
                A.activation(rel[:, :, 0:P * (n + 1)], ps[s][:, :, 0:P * (n + 1)], ACT.Relu).then_inc(rel_ready, 1)
                A.drain().then_inc(turn_free[s], 1)
                if i in (1, 3):
                    s = turns.see()
                    A.activation(qt[:, :, 256 * (i - 1):256 * (i - 1) + 512], ps[s][:], ACT.Copy).then_inc(q_ready, 1)
                    if i == 3:
                        A.wait_ge(sq_q_used, 1)
                    A.activation(sqr[:], ps[s][:], ACT.Square).then_inc(sq_q_ready, 1)
                    A.drain().then_inc(turn_free[s], 1)
            s = turns.see()
            for j in range(2):
                lanes = slice(HD * j, HD * (j + 1))
                for c in range(2):
                    last = A.activation(kT2[j][c][lanes], ps[s][lanes, c, :].rearrange("p (t n) -> p t n", t=TT), ACT.Copy)
            last.then_inc(kT_ready, 1)
            A.drain().then_inc(turn_free[s], 1)
            A.wait_ge(x1_saved, 16)

            def gate_a(c):
                s = turns.see()
                A.activation(sg[:, 4 * c:4 * c + 4, :], ps[s][:], ACT.Tanh, scale=0.5).then_inc(sga_ready, 1)
                A.drain().then_inc(turn_free[s], 1)

            gate_a(0)
            A.wait_ge(sq_ready, 3)
            A.activation(st[:, 7, 0:64], st[:, 6, 0:64], ACT.Sqrt, scale=1.0 / HD, bias=st[:, 9, 0:1]).then_inc(rms_ready, 1)
            s = turns.see()
            A.activation(gate_early[:], ps[s][:], ACT.Tanh, scale=0.5)
            A.drain().then_inc(turn_free[s], 1)
            A.dma_start(gates_dram[0], gate_early[:]).then_inc(gate_saved[0], 16)
            A.wait_ge(gate_saved[0], 16)
            for c in range(2):
                s = turns.see()
                for j in range(2):
                    for odd in range(2):
                        last = A.activation(qT2[HD * j:HD * (j + 1), 4 * c + odd:4 * c + odd + 3:2, :],
                                            ps[s][HD * odd:HD * (odd + 1), 2 * j:2 * j + 2, :], ACT.Copy, scale=HD ** -0.5)
                last.then_inc(qT_ready, 1)
                A.drain().then_inc(turn_free[s], 1)
            gate_a(1)
            for i in range(16 + 3):
                if i < 16:
                    softmax(i, 8, P * (query_block(i) + 1), pr2[:, i % 2], pr2[:, i % 2], False)
                if 0 <= i - 1 < 16:
                    turned_probabilities(i - 1, 8, P * (query_block(i - 1) + 1), pT2)
                b = i - 3
                if b >= 0:
                    A.wait_ge(yt_full, 8 + b + 1)
                    n, g = query_block(b), b % 4
                    A.activation(yah[:, 2 * g:2 * g + 2, P * n:P * (n + 1)],
                                 p_yt[:, 0:256].rearrange("p (c t) -> p c t", c=2), ACT.Copy).then_inc(yT_ready, 1)
            turns.skip(2)

            A.wait_ge(dt_step, 1)
            A.activation(dtt[:, 1], dtt[:, 0], ACT.Abs)
            A.activation(dtt[:, 6, 0, :], a_log[:], ACT.Exp)
            A.drain()
            A.activation(dtt[:, 2], dtt[:, 1], ACT.Exp, scale=-1.0).then_inc(dt_act, 1)
            A.wait_ge(dt_step, 2)
            A.activation(dtt[:, 5], dtt[:, 3], ACT.Ln).then_inc(dt_act, 1)

            def into_conv(n):
                s = turns.see()
                if n > 1:
                    A.wait_ge(conv_out, n - 1)
                A.activation(cpad[:, :, 3:3 + S], ps[s][:], ACT.Copy).then_inc(conv_in, 1)
                A.drain().then_inc(turn_free[s], 1)

            def out_of_conv(n, dst):
                A.wait_ge(conv_out, n)
                A.activation(dst[:], dst[:], ACT.Silu).then_inc(xs_ready, 1)

            def rows_back(dst):
                s = turns.see()
                A.activation(dst, ps[s][:], ACT.Copy).then_inc(xtok_ready, 1)
                A.drain().then_inc(turn_free[s], 1)

            A.wait_ge(conv_in, 1)
            into_conv(1)
            out_of_conv(1, bT)
            into_conv(2)
            out_of_conv(2, cT)
            rows_back(btok[:])
            into_conv(3)
            out_of_conv(3, xsT)

            def z_half(i):
                s = turns.see()
                place = gate_out[(i + 2) % 4]
                if i >= 2:
                    A.wait_ge(gate_saved[1], 16)
                A.activation(place[:], ps[s][:, :, 0:256], ACT.Silu)
                A.drain().then_inc(turn_free[s], 1)
                A.dma_start(gates_dram[2 + i // 2][:, :, 256 * (i % 2):256 * (i % 2 + 1)], place[:]).then_inc(gate_saved[2 + i], 16)

            for j in range(4):
                if j < 3:
                    into_conv(4 + j)
                else:
                    s = turns.see()
                    A.wait_ge(mT_saved, 16)
                    A.activation(gate_late[:], ps[s][:], ACT.Tanh, scale=0.5)
                    A.drain().then_inc(turn_free[s], 1)
                    A.dma_start(gates_dram[1], gate_late[:]).then_inc(gate_saved[1], 16)
                rows_back(xtok[:, :, 512 * j:512 * (j + 1)])
                if j < 3:
                    out_of_conv(4 + j, xsT)

            turns.skip()
            for c in range(TT):
                k = slice(32 * (c % 2), 32 * (c % 2) + 32)
                A.wait_ge(acs_ready, c + 1)
                A.activation(st[:, 5, k], st[:, 2, k], ACT.Exp)
                A.activation(st[:, 4, k], st[:, 1, k], ACT.Exp)
                A.activation(st[:, 6, k], st[:, 3, k], ACT.Exp).then_inc(e_ready, 1)
                for half in range(2):
                    s = turns.see()
                    for h in range(16):
                        hh = 16 * half + h
                        A.activation(decay[:, hh, :], ps[s][:, h // 4, P * (h % 4):P * (h % 4 + 1)], ACT.Relu,
                                     bias=st[:, 1, k.start + hh:k.start + hh + 1], scale=-1.0)
                    A.drain().then_inc(turn_free[s], 1)
                    for g in (2 * half, 2 * half + 1):
                        e = decay[:, 8 * g:8 * g + 8, :]
                        A.activation(e, e, ACT.Exp, scale=-1.0).then_inc(e_ready, 1)
                z_half(c)
                turns.skip(1 + (c > 0) + 2 * (c < TT - 1))

            def squares(g):
                A.wait_ge(gated, g + 1)
                for t in range(TT):
                    A.activation(junk3[:], xtok[:, t, 512 * g:512 * (g + 1)], ACT.Square,
                                 accum_out=st[:, 0, 32 + 4 * g + t:33 + 4 * g + t])
                    A.drain()

            def roots(r):
                k = 32 + 8 * r
                A.activation(st[:, 1, k:k + 8], st[:, 0, k:k + 8], ACT.Sqrt, scale=1.0 / 512, bias=st[:, 9, 0:1]).then_inc(rms_ready, 1)

            squares(0)
            squares(1)
            roots(0)
            for g in (2, 3):
                s = turns.see()
                A.activation(sz[g][:], ps[s][:], ACT.Silu).then_inc(sz_ready, 1)
                A.drain().then_inc(turn_free[s], 1)
            high_parts("ssd")
            squares(2)
            squares(3)
            roots(1)
            turns.skip(2)
            high_parts("ssd", first=KC)
            turns.skip(2)
            for c0 in (0, 4):
                A.wait_ge(mT_ready, 1 + c0 // 4)
                if c0 == 0:
                    A.wait_ge(w_used, 2 * JOBS - 5)
                A.activation(hi[:, c0:c0 + 4, :], mT[:, c0:c0 + 4, :], ACT.Copy, scale=0.5).then_inc(hi_ready, 4)
            turns.skip(2)

            norm_tiles(lambda t: xres[:, t, :], lambda t: xn[:, t, :], junk4[:], 16, TT)
            s = turns.see()
            for c in range(4):
                A.activation(hT[:, c, :], ps[s][:, c, :], ACT.Copy, scale=gain("ffn", c)).then_inc(hi_ready, 1)
            A.drain().then_inc(turn_free[s], 1)
            turns.skip(4)
            A.wait_ge(rt_step, 2)
            A.activation(rt[:, 1, :, 0:4], rt[:, 1, :, 0:4], ACT.Exp)
            A.activation(rt[:, 8, :, 0:1], rt[:, 8, :, 0:1], ACT.Exp).then_inc(rt_act, 1)

            def evacuate(s, b, stored):
                A.wait_ge(dn_done, s + 1)
                if stored is not None:
                    A.wait_ge(y_out[b], 16 * stored)
                A.activation(yg[b][:].rearrange("p (c n) -> p c n", c=2), ps[1][:, 0:2, :], ACT.Copy).then_inc(y_ready, 1)

            def step(s, b, stored, first=False):
                A.wait_ge(gu_done, s + 1)
                if not first:
                    A.wait_ge(act_ready, s)
                A.activation(sa[:], ps[0][:, 0, 0:HID], ACT.Silu).then_inc(sa_ready, 1)
                if not first:
                    evacuate(s - 1, (b - 1) % 3, stored)
                A.wait_ge(act_turned, s + 1)
                A.activation(actT[:].rearrange("p f n -> p (f n)"), ps[0][:, 1, 0:2 * P], ACT.Copy).then_inc(actT_ready, 1)

            step(0, 0, None, first=True)
            for s in (1, 2, 3):
                step(s, s % 3, None)
            with A.Fori(0, (SLOTS - 6) // 3) as i:
                for j in (4, 5, 6):
                    step(3 * i + j, j % 3, i + 1)
            for s in range(SLOTS - 2, SLOTS):
                step(s, s % 3, (s - 1) // 3)
            evacuate(SLOTS - 1, (SLOTS - 1) % 3, (SLOTS - 1) // 3)

        @block.vector
        def _(V):
            turns = Turns(V, turn_full, turn_free)
            his = [0]

            def unit_rows(dst, rows, n, count, k):
                V.wait_ge(rms_ready, count)
                V.reciprocal(st[:, 2, k:k + n], st[:, 1, k:k + n])
                V.drain()
                for t in range(n):
                    last = V.tensor_scalar(dst(t), rows(t), st[:, 2, k + t:k + t + 1], None, ALU.mult)
                return last

            def low_parts(name, first=0, n=S, chunks=KC):
                for c0 in range(0, chunks, 4):
                    s = turns.see()
                    for c in range(4):
                        his[0] += 1
                        V.wait_ge(hi_ready, his[0])
                        last = V.scalar_tensor_tensor(lo[:, c0 + c, 0:n], ps[s][:, c, 0:n], gain(name, first + c0 + c),
                                                      hi[:, c0 + c, 0:n].bitcast(F32), ALU.mult, ALU.subtract)
                    last.then_inc(lo_ready, 1)
                    V.drain().then_inc(turn_free[s], 1)

            def rope(x, heads):
                a, b = x[:, :, :, 0:8], x[:, :, :, 8:16]
                c, s = bc(cos[:], 2, heads), bc(sin[:], 2, heads)
                a_s, b_s_ = (rot[:, i, :, 0:8 * heads].rearrange("p t (h f) -> p t h f", h=heads) for i in range(2))
                V.tensor_tensor(a_s, a, s, ALU.mult)
                V.tensor_tensor(b_s_, b, s, ALU.mult)
                V.drain()
                V.tensor_tensor(a, a, c, ALU.mult)
                V.tensor_tensor(b, b, c, ALU.mult)
                V.drain()
                V.tensor_tensor(a, a, b_s_, ALU.subtract)
                return V.tensor_tensor(b, b, a_s, ALU.add)

            V.memset(st[:, 9, :], EPS).then_inc(setup_done, 1)
            V.memset(ones[:], 1.0)
            V.memset(kT1[0][HD:P], 0.0)
            V.memset(mkT[0][HD:P], 0.0)
            V.memset(mkT[1][0:HD], 0.0)
            V.wait_ge(par_in, PARAMS)
            s = turns.see()
            V.tensor_copy(cols[:], ps[s][:, 0, 0:N_ROWS_A + N_ROWS_B]).then_inc(cols_ready, 1)
            V.drain().then_inc(turn_free[s], 1)

            unit_rows(lambda t: xn[:, t, :], lambda t: memb[:, t, :], 2, 1, 0).then_inc(rows_ready, 1)
            V.drain()
            low_parts("mem", n=MEM)
            unit_rows(lambda t: xn[:, t, :], lambda t: xres[:, t, :], TT, 2, 4).then_inc(rows_ready, 1)
            turns.skip()
            low_parts("pre")
            V.memset(kT1[1][0:HD], 0.0)
            turns.skip()
            V.wait_ge(more_in, MORE_PARAMS)
            s = turns.see()
            V.tensor_tensor(brow[:], ps[s][0:4, 1, 0:384], outside[:], ALU.add).then_inc(brow_ready, 1)
            V.tensor_tensor(wspT[:], ps[s][:, 2, :].rearrange("p (g t) -> p g t", g=4), bc(tri[:], 1, 4), ALU.mult)\
                .then_inc(wspT_ready, 1)
            V.drain().then_inc(turn_free[s], 1)

            turns.skip()
            V.wait_ge(v_ready, 1)
            v4 = vt[:].rearrange("p t (g c) -> p (t g) c", g=4)
            t4 = vtmp[:].rearrange("p t (g c) -> p (t g) c", g=4)
            V.tensor_reduce(st[:, 3, 0:16], v4, AX.X, ALU.add)
            V.drain()
            V.tensor_scalar(st[:, 5, 0:16], st[:, 3, 0:16], 1.0 / P, None, ALU.mult)
            V.drain()
            V.tensor_tensor(v4, v4, bc(st[:, 5, 0:16], 2, P), ALU.subtract)
            V.drain()
            V.tensor_tensor(t4, v4, v4, ALU.mult)
            V.drain()
            V.tensor_reduce(st[:, 3, 0:16], t4, AX.X, ALU.add).then_inc(v_ready, 1)
            V.wait_ge(rms_ready, 3)
            V.reciprocal(st[:, 5, 0:16], st[:, 4, 0:16])
            V.drain()
            V.tensor_tensor(v4, v4, bc(st[:, 5, 0:16], 2, P), ALU.mult)
            V.drain()
            V.tensor_tensor(vt[:], vt[:], bc(v_g[:], 1, TT), ALU.mult)
            V.drain()
            V.tensor_tensor(vt[:], vt[:], bc(v_b[:], 1, TT), ALU.add).then_inc(v_normed, 1)
            turns.skip(3)
            V.wait_ge(bias_in, 64)
            s = turns.see()
            for g in range(4):
                last = V.tensor_tensor(yT[:, g, :].rearrange("p (n t) -> p n t", n=TT),
                                       ps[s][:, g, :].rearrange("p (n t) -> p n t", n=TT), bc(b_s[:, g, :], 1, TT), ALU.add)
            V.drain().then_inc(turn_free[s], 1)
            V.wait_ge(u_ready, 1)
            V.tensor_tensor(yT[:, 0:4], yT[:, 0:4], uT[:], ALU.mult)
            V.drain()
            V.wait_ge(z1_ready, 1)
            V.tensor_tensor(yT[:, 0:4], yT[:, 0:4], zT[:, 0:4], ALU.mult).then_inc(ya_ready, 1)

            s = turns.see()
            V.tensor_copy(bias[:], ps[s][:, :, 0:256])
            V.drain().then_inc(turn_free[s], 1)
            turns.skip()

            def probabilities_used(b, base, yt, sinks_too):
                k = b % 4
                V.wait_ge(exp_ready, base + b + 1)
                V.wait_ge(v_full, base + b + 1)
                den = sm[:, 1, k, :]
                if sinks_too:
                    V.tensor_tensor(den, den, sm[:, 4, k, :], ALU.add)
                    V.drain()
                V.reciprocal(sm[:, 5, k, :], den)
                V.drain()
                V.tensor_tensor(yt[:, b % 2, :].rearrange("p (h d) -> p h d", h=4),
                                p_v[:, 0:256].rearrange("p (h d) -> p h d", h=4), bc(sm[:, 5, k, :], 2, HD), ALU.mult)\
                    .then_inc(yt_ready, 1)

            def turned_probabilities(b, base, width, dst):
                V.wait_ge(t_full, 2 * (base + b) + 1)
                V.tensor_copy(dst[:, 0:2, 0:width], p_t[:, :, 0:width]).then_inc(pT_ready[0], 1)

            for i in range(8 + 3):
                if i < 8:
                    k, n = i % 4, i
                    V.wait_ge(s_full, i + 1)
                    if i < 4:
                        width = P if n == 0 else 256
                        for h in range(4):
                            V.tensor_tensor_reduce(pr1[:, i % 2, h, 0:width], p_s[:, h, 0:width], bias[:, h, 256 - width:256],
                                                   1.0, -3e38, ALU.add, ALU.max, sm[:, 0, k, h:h + 1])
                        V.drain().then_inc(s_free, 1)
                        V.tensor_tensor(sm[:, 0, k, :], sm[:, 0, k, :], sinks[:], ALU.max)
                        V.drain()
                        V.tensor_tensor(sm[:, 3, k, :], sinks[:], sm[:, 0, k, :], ALU.subtract)
                    else:
                        V.tensor_reduce(sm[:, 0, k, :], p_s[:, :, 0:MEM], AX.X, ALU.max)
                        V.drain()
                    V.tensor_scalar(sm[:, 2, k, :], sm[:, 0, k, :], -1.0, None, ALU.mult).then_inc(max_ready, 1)
                if i == 2:
                    his[0] += 4
                    V.wait_ge(hi_ready, his[0])
                    V.tensor_tensor(lo[:, 0:4], yT[:, 0:4], hi[:, 0:4].bitcast(F32), ALU.subtract).then_inc(lo_ready, 1)
                if 0 <= i - 1 < 8:
                    turned_probabilities(i - 1, 0, P if i == 1 else 256, pT1)
                if 0 <= i - 2 < 8:
                    probabilities_used(i - 2, 0, yt1, i - 2 < 4)
            V.wait_ge(yT_ready, 8)
            V.wait_ge(z1_ready, 2)
            V.tensor_tensor(yT[:, 4:8], yT[:, 4:8], zT[:, 4:8], ALU.mult).then_inc(z1_ready, 1)
            his[0] += 4
            V.wait_ge(hi_ready, his[0])
            V.tensor_tensor(lo[:, 4:8], yT[:, 4:8], hi[:, 4:8].bitcast(F32), ALU.subtract).then_inc(lo_ready, 1)
            turns.skip()
            V.wait_ge(wo_ready, 2)
            s = turns.see()
            V.tensor_tensor(st[:, 0, 8:8 + TT], st[:, 0, 8:8 + TT], st[:, 0, 20:20 + TT], ALU.add).then_inc(ss_ready, 1)
            V.wait_ge(rms_ready, 4)
            V.reciprocal(st[:, 2, 8:8 + TT], st[:, 1, 8:8 + TT])
            V.drain()

            def recip(t, k, base):
                V.wait_ge(root_ready, base + t + 1)
                V.reciprocal(st[:, 2, k + t:k + t + 1], st[:, 1, k + t:k + t + 1]).then_inc(recip_ready, 1)

            for t in range(TT):
                r = st[:, 2, 8 + t:9 + t]
                V.scalar_tensor_tensor(xn[:, t, 0:512], xn[:, t, 0:512], r, post_g[:, 0:512], ALU.mult, ALU.mult)
                V.scalar_tensor_tensor(xn[:, t, 512:D], ps[s][:, t, :], r, post_g[:, 512:D], ALU.mult, ALU.mult)
                V.drain()
                V.tensor_tensor(xres[:, t, :], xres[:, t, :], xn[:, t, :], ALU.add).then_inc(tile_ready, 1)
                if t > 0:
                    recip(t - 1, 12, 0)
            V.drain().then_inc(turn_free[s], 1)
            recip(TT - 1, 12, 0)

            low_parts("attn")

            turns.skip()
            V.wait_ge(iq_ready, 1)
            rope(iqt[:].rearrange("p t (h d) -> p t h d", h=8), 8).then_inc(iq_rows, 1)
            turns.skip()
            V.wait_ge(small_ready, 1)
            ik = smt[:, :, 0:HD]
            V.tensor_tensor(ikt[:, :, 0:HD], ik, ik, ALU.mult)
            V.tensor_scalar(smt[:, :, HD:HD + 8], smt[:, :, HD:HD + 8], 8 ** -0.5, None, ALU.mult)
            V.drain()
            V.tensor_reduce(st[:, 3, 16:20], ikt[:, :, 0:HD], AX.X, ALU.add).then_inc(sq_ready, 1)
            V.wait_ge(rms_ready, 5)
            V.reciprocal(st[:, 5, 16:20], st[:, 4, 16:20])
            V.drain()
            V.tensor_tensor(ik, ik, bc(st[:, 5, 16:20], 2, HD), ALU.mult)
            V.drain()
            V.tensor_tensor(ikt[:, :, 0:HD], ik, bc(ik_g[:], 1, TT), ALU.mult)
            V.drain()
            rope(ikt[:, :, 0:HD].unsqueeze(2), 1)
            V.drain()
            V.tensor_copy(ikt[:, :, HD:P], ikt[:, :, 0:HD]).then_inc(iq_rows, 1)

            def norm_heads(x, heads, gains, root):
                t = x.shape[1]
                x3 = x.rearrange("p t (h d) -> p t h d", h=heads)
                V.tensor_tensor(x3, x3, bc(root, 3, HD), ALU.mult)
                V.drain()
                return V.tensor_tensor(x3, x3, gains[:].unsqueeze(1).unsqueeze(1).broadcast_to([P, t, heads, HD]), ALU.mult)

            turns.skip()
            V.wait_ge(kv_ready, 1)
            k4 = kvt[:, :, 0:256]
            sq_k = sqr[:, :, 0:256]
            V.tensor_tensor(sq_k, k4, k4, ALU.mult)
            V.drain()
            V.tensor_reduce(st[:, 3, 20:36], sq_k.rearrange("p t (h d) -> p t h d", h=4), AX.X, ALU.add).then_inc(sq_ready, 1)
            V.wait_ge(rms_ready, 6)
            V.reciprocal(st[:, 5, 20:36], st[:, 4, 20:36])
            V.drain()
            norm_heads(k4, 4, k_g, st[:, 5, 20:36].rearrange("p (t h) -> p t h", t=TT))
            V.drain()
            rope(k4.rearrange("p t (h d) -> p t h d", h=4), 4).then_inc(k_rows, 1)
            turns.skip(2)
            V.memset(sel[:, 0, 0:P], 0.0)
            V.drain()
            V.memset(sel[0:64, 0, 64:P], NEG)

            for n in range(1, TT):
                w = P * (n + 1)
                row = score[:, n - 1, 0:w]
                for h4 in range(2):
                    turns.skip()
                    V.wait_ge(rel_ready, 2 * n - 1 + h4)
                    for h in range(4):
                        k = 4 * h4 + h
                        iw = smt[:, n, HD + k:HD + k + 1]
                        if k == 0:
                            last = V.tensor_scalar(row, rel[:, h, 0:w], iw, None, ALU.mult)
                        else:
                            last = V.scalar_tensor_tensor(row, rel[:, h, 0:w], iw, row, ALU.mult, ALU.add)
                        if h == 3:
                            last.then_inc(rel_used, 1)
                        V.drain()
                if n < TT - 1:
                    turns.skip()
                V.memset(score[0:64, n - 1, P * n + 64:w], -1e38)
                V.drain()
                for r in range(TOPK // 8):
                    V.max(top[:, r % 2, :], row)
                    V.drain()
                    V.match_replace(row, top[:, r % 2, :], row, -3e38)
                    V.drain()
                V.tensor_scalar(sel[:, n, 0:w], row, -2e38, NEG, ALU.is_gt, ALU.mult)
                if n > 1:
                    c = n - 2
                    V.wait_ge(sq_q_ready, c + 1)
                    V.tensor_reduce(st[:, 6, 0:64].rearrange("p (t h) -> p t h", t=TT)[:, :, 8 * c:8 * c + 8],
                                    sqr[:].rearrange("p t (h d) -> p t h d", h=8), AX.X, ALU.add).then_inc(sq_q_used, 1)
            V.drain().then_inc(sq_ready, 1)
            turns.see()
            for j, k in ((0, kT2[0][0]), (0, kT2[0][1]), (1, kT2[1][0]), (1, kT2[1][1])):
                V.memset(k[HD * (1 - j):HD * (2 - j)], 0.0)
            turns.skip(2)
            V.wait_ge(q_ready, 2)
            V.wait_ge(rms_ready, 7)
            V.reciprocal(st[:, 8, 0:64], st[:, 7, 0:64])
            V.drain()
            norm_heads(qt[:], 16, q_g, st[:, 8, 0:64].rearrange("p (t h) -> p t h", t=TT))
            V.drain()
            rope(qt[:].rearrange("p t (h d) -> p t h d", h=16), 16).then_inc(q_rows, 1)
            turns.skip(3)

            for i in range(16 + 3):
                if i < 16:
                    k, n = i % 4, query_block(i)
                    width = P * (n + 1)
                    V.wait_ge(s_full, 8 + i + 1)
                    for h in range(4):
                        V.tensor_tensor_reduce(pr2[:, i % 2, h, 0:width], p_s[:, h, 0:width], sel[:, n, 0:width],
                                               1.0, -3e38, ALU.add, ALU.max, sm[:, 0, k, h:h + 1])
                    V.drain().then_inc(s_free, 1)
                    V.tensor_scalar(sm[:, 2, k, :], sm[:, 0, k, :], -1.0, None, ALU.mult).then_inc(max_ready, 1)
                if 0 <= i - 1 < 16:
                    turned_probabilities(i - 1, 8, P * (query_block(i - 1) + 1), pT2)
                if 0 <= i - 2 < 16:
                    probabilities_used(i - 2, 8, yt2, False)
                b = i - 3
                if b >= 0:
                    V.wait_ge(yt_full, 8 + b + 1)
                    nn, g = query_block(b), b % 4
                    V.wait_ge(yT_ready, 8 + b + 1)
                    o = (slice(None), slice(2 * g, 2 * g + 2), slice(P * nn, P * (nn + 1)))
                    V.tensor_tensor(yal[o], p_yt[:, 0:256].rearrange("p (c t) -> p c t", c=2), yah[o].bitcast(F32), ALU.subtract)\
                        .then_inc(yal_ready, 1)
            for c in range(2):
                s = turns.see()
                V.wait_ge(sga_ready, c + 1)
                V.scalar_tensor_tensor(mT[:, 4 * c:4 * c + 4], sg[:, 4 * c:4 * c + 4], 1.0, ps[s][:], ALU.add, ALU.mult)\
                    .then_inc(mT_half, 1)
                V.drain().then_inc(turn_free[s], 1)

            V.tensor_tensor(dtt[:, 0], smt[:, :, 72:SMALL], bc(dt_b[:], 1, TT), ALU.add).then_inc(dt_step, 1)
            V.wait_ge(dt_act, 1)
            V.tensor_scalar(dtt[:, 3], dtt[:, 2], 1.0, None, ALU.add)
            V.drain().then_inc(dt_step, 1)
            V.tensor_scalar(dtt[:, 4], dtt[:, 3], 1.0, None, ALU.is_equal)
            V.drain()
            V.scalar_tensor_tensor(dtt[:, 7], dtt[:, 3], -1.0, dtt[:, 4], ALU.add, ALU.add)
            V.drain()
            V.reciprocal(dtt[:, 7], dtt[:, 7])
            V.drain()
            V.tensor_tensor(dtt[:, 7], dtt[:, 7], dtt[:, 2], ALU.mult)
            V.wait_ge(dt_act, 2)
            V.tensor_tensor(dtt[:, 4], dtt[:, 4], dtt[:, 2], ALU.mult)
            V.drain()
            V.tensor_tensor(dtt[:, 7], dtt[:, 7], dtt[:, 5], ALU.mult)
            V.drain()
            V.tensor_tensor(dtt[:, 7], dtt[:, 7], dtt[:, 4], ALU.add)
            V.drain()
            V.scalar_tensor_tensor(dts[:, 0], dtt[:, 0], 0.0, dtt[:, 7], ALU.max, ALU.add)
            V.tensor_scalar(dtt[:, 6, 1, :], dtt[:, 6, 0, :], -1.0, None, ALU.mult)
            V.drain()
            V.tensor_tensor(dts[:, 1], dts[:, 0], bc(dtt[:, 6, 1, :], 1, TT), ALU.mult).then_inc(dt_step, 1)

            V.memset(cpad[:, :, 0:3], 0.0).then_inc(conv_in, 1)

            def convolve(n, c0, dst):
                V.wait_ge(conv_in, n + 1)
                if dst is xsT and n > 3:
                    V.wait_ge(xtok_ready, n - 2)
                def tap(k, c):
                    j = N_ROWS_A + 24 * k + c0 + c
                    return cols[:, j:j + 1]
                for c in range(4):
                    V.tensor_scalar(dst[:, c, :], cpad[:, c, 0:S], tap(0, c), gain("conv_b", c0 + c), ALU.mult, ALU.add)
                V.drain()
                for k in range(1, 4):
                    for c in range(4):
                        V.scalar_tensor_tensor(dst[:, c, :], cpad[:, c, k:k + S], tap(k, c), dst[:, c, :], ALU.mult, ALU.add)
                    if k < 3:
                        V.drain()
                V.drain().then_inc(conv_out, 1)

            convolve(1, 16, bT)
            convolve(2, 20, cT)
            for j in range(4):
                convolve(3 + j, 4 * j, xsT)
            turns.skip(12)

            V.wait_ge(xtok_ready, 5)
            def cumulative(c):
                k = slice(32 * (c % 2), 32 * (c % 2) + 32)
                s = turns.see()
                V.tensor_copy(st[:, 1, k], ps[s][:, 0, 0:32])
                V.tensor_copy(st[:, 3, k], ps[s][:, 0, 32:64])
                V.tensor_tensor(cb[:], ps[s][:, 1, :].rearrange("p (g l) -> p g l", g=4), bc(tri[:], 1, 4), ALU.mult)
                V.drain().then_inc(turn_free[s], 1)
                V.tensor_tensor(st[:, 2, k], st[:, 3, k], st[:, 1, k], ALU.subtract).then_inc(acs_ready, 1)

            cumulative(0)
            for c in range(TT):
                k = slice(32 * (c % 2), 32 * (c % 2) + 32)
                V.tensor_tensor(xd[:], xtok[:, c, :].rearrange("p (h d) -> p h d", h=32), bc(dts[:, 0, c, :], 2, HD), ALU.mult)\
                    .then_inc(xd_ready, 1)
                V.drain()
                V.wait_ge(e_ready, 5 * c + 1)
                V.tensor_tensor(xe[:], xd[:], bc(st[:, 5, k], 2, HD), ALU.mult).then_inc(xe_ready, 1)
                turns.skip(3)
                for g in range(4):
                    V.wait_ge(e_ready, 5 * c + 2 + g)
                    m = decay[:, 8 * g:8 * g + 8, :]
                    V.tensor_tensor(m, m, bc(cb[:, g, :], 1, 8), ALU.mult).then_inc(m_ready, 1)
                y = xtok[:, c, :].rearrange("p (h d) -> p h d", h=32)
                V.tensor_tensor(y, y, bc(d_skip[:], 2, HD), ALU.mult)
                V.drain()
                s = turns.see()
                V.tensor_tensor(xtok[:, c, :], xtok[:, c, :], ps[s][:].rearrange("p g n -> p (g n)"), ALU.add)
                V.drain().then_inc(turn_free[s], 1)
                if c > 0:
                    s = turns.see()
                    V.tensor_tensor(yoff[:], ps[s][:].rearrange("p g (h d) -> p (g h) d", d=HD), bc(st[:, 4, k], 2, HD), ALU.mult)
                    V.drain().then_inc(turn_free[s], 1)
                if c < TT - 1:
                    cumulative(c + 1)
                    s = turns.see()
                    if c > 0:
                        sh = state[:].rearrange("p (h d) -> p h d", h=32)
                        V.tensor_tensor(sh, sh, bc(st[:, 6, k], 2, HD), ALU.mult)
                        V.drain()
                        V.tensor_tensor(state[:], state[:], ps[s][:].rearrange("p g n -> p (g n)"), ALU.add).then_inc(st_ready, 1)
                    else:
                        V.tensor_copy(state[:], ps[s][:].rearrange("p g n -> p (g n)")).then_inc(st_ready, 1)
                    V.drain().then_inc(turn_free[s], 1)
                if c > 0:
                    V.tensor_tensor(y, y, yoff[:], ALU.add)
                    V.drain()
            V.drain().then_inc(ssd_done, 1)
            turns.skip(2)

            def gate_group(g):
                yg = xtok[:, :, 512 * g:512 * (g + 1)]
                V.tensor_tensor(yg, yg, sz[g][:], ALU.mult).then_inc(gated, 1)

            def unit_groups(r):
                k = 32 + 8 * r
                V.wait_ge(rms_ready, 8 + r)
                V.reciprocal(st[:, 2, k:k + 8], st[:, 1, k:k + 8])
                V.drain()
                for g in (2 * r, 2 * r + 1):
                    for t in range(TT):
                        yg = xtok[:, t, 512 * g:512 * (g + 1)]
                        last = V.tensor_scalar(yg, yg, st[:, 2, 32 + 4 * g + t:33 + 4 * g + t], None, ALU.mult)
                last.then_inc(y_rows, 1)

            for g in range(2):
                V.wait_ge(sz_back[g], 16)
                gate_group(g)
            unit_groups(0)
            V.wait_ge(sz_ready, 1)
            gate_group(2)
            low_parts("ssd")
            V.wait_ge(sz_ready, 2)
            gate_group(3)
            unit_groups(1)
            V.wait_ge(sgb_back, 32)
            V.wait_ge(mT_back, 16)
            for r in range(2):
                if r == 1:
                    low_parts("ssd", first=KC)
                for c in range(2):
                    s = turns.see()
                    V.scalar_tensor_tensor(both[:], sgb[:, 4 * c:4 * c + 4], 1.0, ps[s][:], ALU.add, ALU.mult)
                    V.drain().then_inc(turn_free[s], 1)
                    V.tensor_tensor(mT[:, 4 * c:4 * c + 4], mT[:, 4 * c:4 * c + 4], both[:], ALU.add)
                    last = V.drain()
                    if r == 1:
                        last.then_inc(mT_ready, 1)
                        his[0] += 4
                        V.wait_ge(hi_ready, his[0])
                        V.scalar_tensor_tensor(lo[:, 4 * c:4 * c + 4], mT[:, 4 * c:4 * c + 4], 0.5, hi[:, 4 * c:4 * c + 4].bitcast(F32),
                                               ALU.mult, ALU.subtract).then_inc(lo_ready, 1)
            V.wait_ge(x1_back, 16)
            s = turns.see()
            V.tensor_tensor(xres[:, :, 0:512], xres[:, :, 0:512], ps[s][:], ALU.add)
            V.drain().then_inc(turn_free[s], 1)
            s = turns.see()
            for t in range(TT):
                V.tensor_tensor(xres[:, t, 512:D], xres[:, t, 512:D], ps[s][:, t, :], ALU.add).then_inc(tile_ready, 1)
                if t > 0:
                    recip(t - 1, 16, TT)
            V.drain().then_inc(turn_free[s], 1)
            recip(TT - 1, 16, TT)

            turns.skip()
            s = turns.see()
            for c in range(4):
                last = V.tensor_scalar(hT[:, 4 + c, :], ps[s][:, c, :], gain("ffn", 4 + c), None, ALU.mult)
            last.then_inc(lo_ready, 1)
            V.drain().then_inc(turn_free[s], 1)
            s = turns.see()
            logits = rt[:, 0]
            V.tensor_tensor(logits, ps[s][:, :, 0:36], bc(b_rt[:], 1, TT), ALU.add)
            V.drain().then_inc(turn_free[s], 1)

            def first_max(hot, x, m, key, n):
                V.tensor_tensor(hot, x, bc(m, 2, n), ALU.is_equal)
                V.drain()
                V.tensor_tensor(hot, hot, bc(order[:, 0:n], 1, TT), ALU.mult)
                V.drain()
                V.tensor_reduce(key, hot, AX.X, ALU.max)
                V.drain()
                V.tensor_tensor(hot, hot, bc(key, 2, n), ALU.is_equal)
                V.drain()

            gl, ge, ghot = rt[:, 0, :, 0:4], rt[:, 1, :, 0:4], rt[:, 2, :, 0:4]
            gm, gs, m1, m2, key, p1, p2 = (rt[:, 3, :, i] for i in range(7))
            e_in, hot1, hot2 = rt[:, 4, :, 0:8], rt[:, 5, :, 0:8], rt[:, 6, :, 0:8]
            V.tensor_reduce(gm, gl, AX.X, ALU.max)
            V.drain()
            first_max(ghot, gl, gm, key, 4)
            per_group = rt[:, 7, :, 0:32].rearrange("p t (g e) -> p t g e", g=4)
            V.tensor_tensor(per_group, rt[:, 0, :, 4:36].rearrange("p t (g e) -> p t g e", g=4), bc(ghot, 3, 8), ALU.mult)
            V.drain()
            V.tensor_reduce(e_in, per_group.rearrange("p t g e -> p t e g"), AX.X, ALU.add)
            V.drain()
            V.tensor_reduce(m1, e_in, AX.X, ALU.max)
            V.drain()
            first_max(hot1, e_in, m1, key, 8)
            rest = rt[:, 9, :, 0:8]
            V.tensor_scalar(rest, hot1, NEG, None, ALU.mult)
            V.drain()
            V.tensor_tensor(rest, rest, e_in, ALU.add)
            V.drain()
            V.tensor_reduce(m2, rest, AX.X, ALU.max)
            V.drain()
            first_max(hot2, rest, m2, key, 8)
            for k, h in enumerate((hot1, hot2)):
                V.tensor_tensor(hot[:, k].rearrange("p t (g e) -> p t g e", g=4), bc(ghot, 3, 8), bc(h, 2, 4), ALU.mult)
            V.drain()
            V.tensor_tensor(rt[:, 10, :, 0:32], hot[:, 0], hot[:, 1], ALU.add).then_inc(rt_step, 1)
            V.tensor_tensor(ge, gl, bc(gm, 2, 4), ALU.subtract)
            V.tensor_tensor(rt[:, 8, :, 0], m2, m1, ALU.subtract)
            V.drain().then_inc(rt_step, 1)
            s = turns.see()
            pairs, slots = ps[s][:, 1, 0:32], cnt[:, 0, :]
            V.tensor_scalar(slots, pairs, 0.0, None, ALU.is_gt)
            V.drain()
            for full in range(P, S, P):
                V.scalar_tensor_tensor(slots, pairs, float(full), slots, ALU.is_gt, ALU.add)
                V.drain()
            end = slots
            for i, shift in enumerate((1, 2, 4, 8, 16)):
                V.tensor_copy(cnt[:, 1 + i, 0:shift], end[:, 0:shift])
                V.tensor_tensor(cnt[:, 1 + i, shift:32], end[:, shift:32], end[:, 0:32 - shift], ALU.add)
                V.drain()
                end = cnt[:, 1 + i, :]
            V.tensor_tensor(ends[:], bc(end[0:1, :], 1, SLOTS), bc(iota[0:1, 0:SLOTS], 2, N_EXP), ALU.is_le)
            V.drain()
            V.tensor_reduce(slot_f[:], ends[:], AX.X, ALU.add)
            V.drain()
            V.tensor_scalar(slot_e[:], slot_f[:], float(N_EXP - 1), None, ALU.min).then_inc(slots_ready, 1)
            row0 = cnt[:, 6, :]
            V.tensor_tensor(row0, end, slots, ALU.subtract)
            V.drain()
            V.tensor_scalar(row0, row0, float(P), -1.0, ALU.mult, ALU.add)
            V.drain()
            where = rt[:, 11, :, 0:32]
            V.tensor_tensor(where, ps[s][:, 0, 0:32 * TT].rearrange("p (t e) -> p t e", t=TT), bc(row0, 1, TT), ALU.add)
            V.drain().then_inc(turn_free[s], 1)
            V.tensor_tensor(hot[:], hot[:], bc(where, 1, 2), ALU.mult)
            V.drain()
            V.tensor_reduce(pos[:, 0, :], hot[:].rearrange("p k t e -> p (k t) e"), AX.X, ALU.add)
            V.drain()
            V.tensor_copy(pos_u[:], pos[:, 0, :])
            starts = rt[:, 12, 0:2, :].rearrange("p a b -> p (a b)")[:, 0:SLOTS]
            V.tensor_scalar(starts, iota[:, 0:SLOTS], float(P), None, ALU.mult)
            V.drain()
            V.tensor_tensor(hot_b[:], bc(starts, 1, 2 * TT), bc(pos[:, 0, :], 2, SLOTS), ALU.is_le)
            V.drain()
            V.tensor_reduce(pos[:, 1, :], hot_b[:], AX.X, ALU.add)
            V.drain()
            V.tensor_scalar(pos[:, 1, :], pos[:, 1, :], -1.0, None, ALU.add)
            V.drain()
            V.scalar_tensor_tensor(pos[:, 2, :], pos[:, 1, :], -float(P), pos[:, 0, :], ALU.mult, ALU.add)
            V.tensor_tensor(hot_b[:], bc(iota[:, 0:SLOTS], 1, 2 * TT), bc(pos[:, 1, :], 2, SLOTS), ALU.is_equal)
            V.drain()
            V.tensor_tensor(hot_r[:], bc(iota[:], 1, 2 * TT), bc(pos[:, 2, :], 2, P), ALU.is_equal)
            for k in range(2):
                V.tensor_tensor(hot_b[:, TT * k:TT * (k + 1), :], hot_b[:, TT * k:TT * (k + 1), :], bc(token[:], 2, SLOTS), ALU.mult)
            V.drain().then_inc(rt_step, 1)
            s = turns.see()
            V.tensor_copy(tab_u[:], ps[s][:, 0, 0:SLOTS])
            V.drain().then_inc(table_ready, 1)
            V.wait_ge(rt_act, 1)
            V.tensor_reduce(gs, ge, AX.X, ALU.add)
            V.tensor_scalar(p1, rt[:, 8, :, 0], 1.0, None, ALU.add)
            V.drain()
            V.tensor_tensor(p1, p1, gs, ALU.mult)
            V.drain()
            V.reciprocal(p1, p1)
            V.drain()
            V.tensor_tensor(p2, p1, rt[:, 8, :, 0], ALU.mult)

            def rows_slot(s):
                V.wait_ge(turned, s + 1)
                V.tensor_tensor(xT[:], ps[0][:, 2:4, :].rearrange("p c (k t) -> p (c k) t", t=P), bc(ffn_kp[:], 2, P), ALU.mult)\
                    .then_inc(xT_ready, 1)

            def step(s, b, last=False):
                if not last:
                    rows_slot(s + 1)
                V.wait_ge(sa_ready, s + 1)
                if not (isinstance(s, int) and s == 0):
                    V.wait_ge(act_turned, s)
                V.tensor_tensor(act[:], sa[:], ps[0][:, 0, HID:2 * HID], ALU.mult).then_inc(act_ready, 1)

            rows_slot(0)
            step(0, 0)
            with V.Fori(0, (SLOTS - 3) // 3) as i:
                for j in (1, 2, 3):
                    step(3 * i + j, j % 3)
            step(SLOTS - 2, 1)
            step(SLOTS - 1, 2, last=True)
            for t in range(TT):
                V.wait_ge(back_in[t], 32)
                for k, share in enumerate((p1, p2)):
                    last = V.scalar_tensor_tensor(xres[:, t, :], back[:, TT * k + t, :], share[:, t:t + 1], xres[:, t, :], ALU.mult, ALU.add)
                    if k == 0:
                        V.drain()
                last.then_inc(out_ready, 1)



def kernel(**inputs):
    import concourse.bacc as bacc
    from concourse.bass_utils import run_bass_kernel_spmd

    nc = bacc.Bacc("TRN2", target_bir_lowering=False, num_devices=1)
    arrays = {n: np.ascontiguousarray(a) for n, a in inputs.items()}
    arrays.update(consts())
    d = {n: nc.dram_tensor(n, a.shape, mybir.dt.from_np(a.dtype), kind="ExternalInput").ap() for n, a in arrays.items()}
    out = nc.dram_tensor("out", [1, S, D], F32, kind="ExternalOutput").ap()
    program(nc, d, out)
    return run_bass_kernel_spmd(nc, [arrays], core_ids=[0]).results[0]["out"]
```
